# Optimizing a Trainium2 kernel written in Bass

```python
import math
import jax, jax.numpy as jnp
from jax import lax
import numpy as np

D_MODEL = 1024
BATCH = 1
SEQ = 256
DEPTH = 1

MEM_LEN = 256
EPS = 1e-6
LRU_WIDTH = 512
LRU_BLOCKS = 8
LRU_BLOCK = LRU_WIDTH // LRU_BLOCKS
CONV_WIDTH = 4
LRU_C = 8.0
MLA_HEADS = 8
QK_NOPE = 64
QK_ROPE = 32
QK_HEAD = QK_NOPE + QK_ROPE
V_DIM = 64
Q_LORA = 256
KV_LORA = 128
MLA_WIDTH = MLA_HEADS * V_DIM
ROPE_THETA = 10000.0
Q_BLOCK = 128
MIX_WIDTH = LRU_WIDTH + MLA_WIDTH
OFF_Y = LRU_WIDTH
OFF_CQ = 2 * LRU_WIDTH
OFF_CKV = OFF_CQ + Q_LORA
OFF_KR = OFF_CKV + KV_LORA
IN_COLS = OFF_KR + QK_ROPE
MEM_HEADS = 4
MEM_HEAD_DIM = 128
MEM_WIDTH = MEM_HEADS * MEM_HEAD_DIM
D_FF = 2816
FFN_CONV = 3


def rms_norm(x, g):
    xf = x.astype(jnp.float32)
    y = xf * lax.rsqrt(jnp.mean(xf * xf, axis=-1, keepdims=True) + EPS)
    return (y * g.astype(jnp.float32)).astype(x.dtype)

def depthwise_conv(x, w, b, left, right):
    S = x.shape[1]
    xp = jnp.pad(x, ((0, 0), (left, right), (0, 0)))
    out = xp[:, 0:S] * w[0] + b
    for k in range(1, w.shape[0]):
        out = out + xp[:, k:k + S] * w[k]
    return out

def rope_tables(positions):
    inv = ROPE_THETA ** (-jnp.arange(0, QK_ROPE, 2, dtype=jnp.float32) / QK_ROPE)
    ang = positions.astype(jnp.float32)[..., None] * inv
    return jnp.cos(ang), jnp.sin(ang)

def apply_rope(t, cos, sin):
    half = QK_ROPE // 2
    c = cos[:, :, None, :].astype(t.dtype)
    s = sin[:, :, None, :].astype(t.dtype)
    t1, t2 = t[..., :half], t[..., half:]
    return jnp.concatenate([t1 * c - t2 * s, t1 * s + t2 * c], axis=-1)

def block_diag(x, w):
    B_, S_, _ = x.shape
    xb = x.reshape(B_, S_, LRU_BLOCKS, LRU_BLOCK)
    return jnp.einsum('bsnc,ncd->bsnd', xb, w).reshape(B_, S_, LRU_WIDTH)

def rg_lru(x, w_a, b_a, w_i, b_i, lam, reverse):
    r = jax.nn.sigmoid((block_diag(x, w_a) + b_a).astype(jnp.float32))
    i = jax.nn.sigmoid((block_diag(x, w_i) + b_i).astype(jnp.float32))
    log_a = -LRU_C * r * jax.nn.softplus(-lam.astype(jnp.float32))
    a = jnp.exp(log_a)
    mult = jnp.sqrt(-jnp.expm1(2.0 * log_a))
    b = mult * (i * x.astype(jnp.float32))

    def combine(lhs, rhs):
        a_l, b_l = lhs
        a_r, b_r = rhs
        return a_l * a_r, a_r * b_l + b_r

    _, h = lax.associative_scan(combine, (a, b), reverse=reverse, axis=1)
    return h

def mla_attention(proj, cos, sin, q_a_norm, w_uq, kv_a_norm, w_ukv, q_norm, k_norm):
    B_, S_, _ = proj.shape
    c_q = rms_norm(proj[..., OFF_CQ:OFF_CKV], q_a_norm)
    c_kv = rms_norm(proj[..., OFF_CKV:OFF_KR], kv_a_norm)
    k_rope = proj[..., OFF_KR:IN_COLS]
    q = (c_q @ w_uq).reshape(B_, S_, MLA_HEADS, QK_HEAD)
    kv = (c_kv @ w_ukv).reshape(B_, S_, MLA_HEADS, QK_NOPE + V_DIM)
    k_nope, v = kv[..., :QK_NOPE], kv[..., QK_NOPE:]
    k_rope_h = jnp.broadcast_to(k_rope[:, :, None, :], (B_, S_, MLA_HEADS, QK_ROPE))
    k = jnp.concatenate([k_nope, k_rope_h], axis=-1)
    q = rms_norm(q, q_norm)
    k = rms_norm(k, k_norm)
    q = jnp.concatenate([q[..., :QK_NOPE], apply_rope(q[..., QK_NOPE:], cos, sin)], axis=-1)
    k = jnp.concatenate([k[..., :QK_NOPE], apply_rope(k[..., QK_NOPE:], cos, sin)], axis=-1)
    scale = QK_HEAD ** -0.5
    kh = k.transpose(0, 2, 1, 3)
    vh = v.transpose(0, 2, 1, 3)
    nb = S_ // Q_BLOCK
    qb = q.transpose(0, 2, 1, 3).reshape(B_, MLA_HEADS, nb, Q_BLOCK, QK_HEAD).transpose(2, 0, 1, 3, 4)

    def attend(q_blk):
        s = jnp.einsum('bhqd,bhkd->bhqk', q_blk, kh).astype(jnp.float32) * scale
        p = jax.nn.softmax(s, axis=-1)
        return jnp.einsum('bhqk,bhkd->bhqd', p.astype(vh.dtype), vh)

    o = lax.map(attend, qb)
    return o.transpose(1, 0, 3, 2, 4).reshape(B_, S_, MLA_WIDTH)

def memory_cross_attention(h, mem_n, w_q, w_kv, q_norm, k_norm, w_o):
    B_, S_, _ = h.shape
    M = mem_n.shape[1]
    q = (h @ w_q).reshape(B_, S_, MEM_HEADS, MEM_HEAD_DIM)
    kv = mem_n @ w_kv
    k = kv[..., :MEM_WIDTH].reshape(B_, M, MEM_HEADS, MEM_HEAD_DIM)
    v = kv[..., MEM_WIDTH:].reshape(B_, M, MEM_HEADS, MEM_HEAD_DIM)
    q = rms_norm(q, q_norm)
    k = rms_norm(k, k_norm)
    s = jnp.einsum('bqhd,bkhd->bhqk', q, k).astype(jnp.float32) * (MEM_HEAD_DIM ** -0.5)
    p = jax.nn.softmax(s, axis=-1)
    o = jnp.einsum('bhqk,bkhd->bqhd', p.astype(v.dtype), v).reshape(B_, S_, MEM_WIDTH)
    return o @ w_o

def hybrid_layer(x, mem, cos, sin, attn_norm, w_in, lru_conv_w, lru_conv_b, lru_w_a, lru_b_a,
                 lru_w_i, lru_b_i, lru_lambda, q_a_norm, w_uq, kv_a_norm, w_ukv, mla_q_norm,
                 mla_k_norm, lru_out_norm, mla_out_norm, w_out, mem_attn_norm, mem_norm, w_mem_q,
                 w_mem_kv, mem_q_norm, mem_k_norm, w_mem_o, ffn_norm, w_up, ffn_conv_w, ffn_conv_b,
                 w_down):
    h = rms_norm(x, attn_norm)
    proj = h @ w_in
    xr = proj[..., :OFF_Y]
    yg = proj[..., OFF_Y:OFF_CQ]
    xf = depthwise_conv(xr, lru_conv_w[0], lru_conv_b[0], CONV_WIDTH - 1, 0)
    xb = depthwise_conv(xr, lru_conv_w[1], lru_conv_b[1], 0, CONV_WIDTH - 1)
    hf = rg_lru(xf, lru_w_a[0], lru_b_a[0], lru_w_i[0], lru_b_i[0], lru_lambda[0], False)
    hb = rg_lru(xb, lru_w_a[1], lru_b_a[1], lru_w_i[1], lru_b_i[1], lru_lambda[1], True)
    lru_out = (hf + hb).astype(x.dtype) * jax.nn.gelu(yg)
    mla_out = mla_attention(proj, cos, sin, q_a_norm, w_uq, kv_a_norm, w_ukv, mla_q_norm, mla_k_norm)
    mixed = jnp.concatenate([rms_norm(lru_out, lru_out_norm), rms_norm(mla_out, mla_out_norm)], axis=-1)
    x = x + mixed @ w_out
    x = x + memory_cross_attention(rms_norm(x, mem_attn_norm), rms_norm(mem, mem_norm),
                                   w_mem_q, w_mem_kv, mem_q_norm, mem_k_norm, w_mem_o)
    gu = rms_norm(x, ffn_norm) @ w_up
    gu = depthwise_conv(gu, ffn_conv_w, ffn_conv_b, FFN_CONV // 2, FFN_CONV // 2)
    g, u = gu[..., :D_FF], gu[..., D_FF:]
    x = x + (jax.nn.silu(g) * u) @ w_down
    return x

def first_inputs(seed: int = 0) -> dict:
    key = jax.random.key(seed)
    ks = iter(jax.random.split(key, 40))
    f32 = jnp.float32

    def w(shape, fan_in):
        return jax.random.normal(next(ks), (DEPTH,) + shape, f32) * (fan_in ** -0.5)

    def gain(shape):
        return 1.0 + 0.05 * jax.random.normal(next(ks), (DEPTH,) + shape, f32)

    def bias(shape):
        return 0.01 * jax.random.normal(next(ks), (DEPTH,) + shape, f32)

    x = jax.random.normal(next(ks), (BATCH, SEQ, D_MODEL), f32)
    mem = jax.random.normal(next(ks), (BATCH, MEM_LEN, D_MODEL), f32)
    positions = jnp.broadcast_to(jnp.arange(SEQ, dtype=jnp.int32)[None, :], (BATCH, SEQ))
    u = jax.random.uniform(next(ks), (DEPTH, 2, LRU_WIDTH), f32, 0.9, 0.999)
    s = u ** (1.0 / LRU_C)
    lru_lambda = jnp.log(s) - jnp.log1p(-s)
    return {
        "x": x,
        "mem": mem,
        "positions": positions,
        "attn_norm": gain((D_MODEL,)),
        "w_in": w((D_MODEL, IN_COLS), D_MODEL),
        "lru_conv_w": w((2, CONV_WIDTH, LRU_WIDTH), CONV_WIDTH),
        "lru_conv_b": bias((2, LRU_WIDTH)),
        "lru_w_a": w((2, LRU_BLOCKS, LRU_BLOCK, LRU_BLOCK), LRU_BLOCK),
        "lru_b_a": bias((2, LRU_WIDTH)),
        "lru_w_i": w((2, LRU_BLOCKS, LRU_BLOCK, LRU_BLOCK), LRU_BLOCK),
        "lru_b_i": bias((2, LRU_WIDTH)),
        "lru_lambda": lru_lambda,
        "q_a_norm": gain((Q_LORA,)),
        "w_uq": w((Q_LORA, MLA_HEADS * QK_HEAD), Q_LORA),
        "kv_a_norm": gain((KV_LORA,)),
        "w_ukv": w((KV_LORA, MLA_HEADS * (QK_NOPE + V_DIM)), KV_LORA),
        "mla_q_norm": gain((QK_HEAD,)),
        "mla_k_norm": gain((QK_HEAD,)),
        "lru_out_norm": gain((LRU_WIDTH,)),
        "mla_out_norm": gain((MLA_WIDTH,)),
        "w_out": w((MIX_WIDTH, D_MODEL), MIX_WIDTH),
        "mem_attn_norm": gain((D_MODEL,)),
        "mem_norm": gain((D_MODEL,)),
        "w_mem_q": w((D_MODEL, MEM_WIDTH), D_MODEL),
        "w_mem_kv": w((D_MODEL, 2 * MEM_WIDTH), D_MODEL),
        "mem_q_norm": gain((MEM_HEAD_DIM,)),
        "mem_k_norm": gain((MEM_HEAD_DIM,)),
        "w_mem_o": w((MEM_WIDTH, D_MODEL), MEM_WIDTH),
        "ffn_norm": gain((D_MODEL,)),
        "w_up": w((D_MODEL, 2 * D_FF), D_MODEL),
        "ffn_conv_w": w((FFN_CONV, 2 * D_FF), FFN_CONV),
        "ffn_conv_b": bias((2 * D_FF,)),
        "w_down": w((D_FF, D_MODEL), D_FF),
    }

def first_block(x, mem, positions, attn_norm, w_in, lru_conv_w, lru_conv_b, lru_w_a, lru_b_a,
              lru_w_i, lru_b_i, lru_lambda, q_a_norm, w_uq, kv_a_norm, w_ukv, mla_q_norm,
              mla_k_norm, lru_out_norm, mla_out_norm, w_out, mem_attn_norm, mem_norm, w_mem_q,
              w_mem_kv, mem_q_norm, mem_k_norm, w_mem_o, ffn_norm, w_up, ffn_conv_w, ffn_conv_b,
              w_down):
    cos, sin = rope_tables(positions)
    for l in range(DEPTH):
        x = hybrid_layer(x, mem, cos, sin, attn_norm[l], w_in[l], lru_conv_w[l], lru_conv_b[l],
                         lru_w_a[l], lru_b_a[l], lru_w_i[l], lru_b_i[l], lru_lambda[l],
                         q_a_norm[l], w_uq[l], kv_a_norm[l], w_ukv[l], mla_q_norm[l],
                         mla_k_norm[l], lru_out_norm[l], mla_out_norm[l], w_out[l],
                         mem_attn_norm[l], mem_norm[l], w_mem_q[l], w_mem_kv[l], mem_q_norm[l],
                         mem_k_norm[l], w_mem_o[l], ffn_norm[l], w_up[l], ffn_conv_w[l],
                         ffn_conv_b[l], w_down[l])
    return x


DEPTH_2 = 2

HEAD_DIM = 64
N_ATTN_HEADS = D_MODEL // HEAD_DIM
N_DIFF_HEADS = N_ATTN_HEADS // 4
DIL_GROUPS = ((128, 1), (512, 4), (2048, 16))
HEADS_PER_DIL = (N_ATTN_HEADS - N_DIFF_HEADS) // len(DIL_GROUPS)
N_DIL_HEADS = HEADS_PER_DIL * len(DIL_GROUPS)
DIL_WIDTH = N_DIL_HEADS * HEAD_DIM
DIFF_QK_DIM = HEAD_DIM // 2
DIFF_QK_WIDTH = N_DIFF_HEADS * 2 * DIFF_QK_DIM
DIFF_V_WIDTH = N_DIFF_HEADS * HEAD_DIM
ATTN_IN_WIDTH = 3 * DIL_WIDTH + 2 * DIFF_QK_WIDTH + DIFF_V_WIDTH
ATTN_SPLITS = [DIL_WIDTH, 2 * DIL_WIDTH, 3 * DIL_WIDTH,
               3 * DIL_WIDTH + DIFF_QK_WIDTH, 3 * DIL_WIDTH + 2 * DIFF_QK_WIDTH]
BLOCK = 128
HGRN_HEADS = 8
HGRN_EXPAND = 128
HGRN_FORGET_DIM = HGRN_HEADS * HGRN_EXPAND
HGRN_VDIM = D_MODEL // HGRN_HEADS
HGRN_CHUNK = 64
HGRN_IN_WIDTH = 2 * HGRN_FORGET_DIM + 2 * D_MODEL
N_EXPERTS = 8
TOP_K = 2
D_FF_EXPERT = 3584
N_EVEN = (DEPTH_2 + 1) // 2
N_ODD = DEPTH_2 // 2
NEG_INF = -1e30
F32 = jnp.float32


def rms_norm_2(x, gain):
    xf = x.astype(F32)
    y = xf * lax.rsqrt(jnp.mean(xf * xf, axis=-1, keepdims=True) + EPS)
    return (y * gain.astype(F32)).astype(x.dtype)

def alibi_slopes(n):
    return 2.0 ** (-8.0 * (jnp.arange(n, dtype=F32) + 1.0) / n)

def dilated_window_attention(q, k, v, slopes, window, dilation):
    B, S, H, Dh = q.shape
    span = window // dilation
    assert span <= BLOCK
    n_blk = -(-S // (dilation * BLOCK))
    Lp = n_blk * dilation * BLOCK

    def to_classes(t):
        t = jnp.pad(t, ((0, 0), (0, Lp - S), (0, 0), (0, 0)))
        t = t.reshape(B, Lp // dilation, dilation, H, Dh).transpose(0, 2, 1, 3, 4)
        return t.reshape(B, dilation, n_blk, BLOCK, H, Dh)

    def with_prev(t):
        prev = jnp.pad(t[:, :, :-1], ((0, 0), (0, 0), (1, 0), (0, 0), (0, 0), (0, 0)))
        return jnp.concatenate([prev, t], axis=3)

    qc = to_classes(q)
    kb = with_prev(to_classes(k))
    vb = with_prev(to_classes(v))
    step = jnp.arange(BLOCK)[:, None] + BLOCK - jnp.arange(2 * BLOCK)[None, :]
    not_before_start = (jnp.arange(n_blk)[:, None, None] > 0) | (jnp.arange(2 * BLOCK)[None, None, :] >= BLOCK)
    valid = (step >= 0) & (step <= span) & not_before_start
    bias = -slopes[:, None, None] * (step * dilation).astype(F32)
    s = jnp.einsum('brnqhd,brnkhd->brnhqk', qc, kb).astype(F32) * (Dh ** -0.5) + bias
    s = jnp.where(valid[None, None, :, None], s, NEG_INF)
    lse = jax.nn.logsumexp(s, axis=-1)
    p = jnp.exp(s - lse[..., None])
    o = jnp.einsum('brnhqk,brnkhd->brnqhd', p, vb.astype(F32))

    def from_classes(t):
        X = t.shape[-1]
        t = t.reshape(B, dilation, Lp // dilation, H, X).transpose(0, 2, 1, 3, 4)
        return t.reshape(B, Lp, H, X)[:, :S]

    lse_pos = from_classes(jnp.swapaxes(lse, -1, -2)[..., None])[..., 0]
    return from_classes(o), lse_pos

def differential_attention(q1, q2, k1, k2, v, slopes, lam):
    B, S, H, dk = q1.shape
    n_blk = S // BLOCK
    scale = dk ** -0.5
    kpos = jnp.arange(S)
    vf = v.astype(F32)

    def one_block(args):
        qb1, qb2, blk = args
        dist = (blk * BLOCK + jnp.arange(BLOCK))[:, None] - kpos[None, :]
        causal = dist >= 0
        bias = -slopes[:, None, None] * dist.astype(F32)

        def probs(qb, kk):
            s = jnp.einsum('bqhd,bkhd->bhqk', qb, kk).astype(F32) * scale + bias
            return jax.nn.softmax(jnp.where(causal, s, NEG_INF), axis=-1)

        a = probs(qb1, k1) - lam * probs(qb2, k2)
        return jnp.einsum('bhqk,bkhd->bqhd', a, vf)

    to_blocks = lambda t: t.reshape(B, n_blk, BLOCK, H, dk).transpose(1, 0, 2, 3, 4)
    out = lax.map(one_block, (to_blocks(q1), to_blocks(q2), jnp.arange(n_blk)))
    return out.transpose(1, 0, 2, 3, 4).reshape(B, S, H, 2 * dk)

def dilated_diff_mixer(u, w_in, dil_q_gain, dil_k_gain, diff_q_gain, diff_k_gain,
                       lam_q1, lam_k1, lam_q2, lam_k2, diff_out_gain, w_out, layer):
    B, S, _ = u.shape
    dq, dk, dv, fq, fk, fv = jnp.split(u @ w_in, ATTN_SPLITS, axis=-1)
    slopes = alibi_slopes(N_ATTN_HEADS)
    dq = rms_norm_2(dq.reshape(B, S, N_DIL_HEADS, HEAD_DIM), dil_q_gain)
    dk = rms_norm_2(dk.reshape(B, S, N_DIL_HEADS, HEAD_DIM), dil_k_gain)
    dv = dv.reshape(B, S, N_DIL_HEADS, HEAD_DIM)
    outs, lses = [], []
    for g, (window, dilation) in enumerate(DIL_GROUPS):
        hs = slice(g * HEADS_PER_DIL, (g + 1) * HEADS_PER_DIL)
        o, lse = dilated_window_attention(dq[:, :, hs], dk[:, :, hs], dv[:, :, hs], slopes[hs], window, dilation)
        outs.append(o)
        lses.append(lse)
    alpha = jax.nn.softmax(jnp.stack(lses), axis=0)
    dil_out = jnp.concatenate([alpha[g][..., None] * outs[g] for g in range(len(DIL_GROUPS))], axis=2)
    fq = rms_norm_2(fq.reshape(B, S, N_DIFF_HEADS, 2, DIFF_QK_DIM), diff_q_gain)
    fk = rms_norm_2(fk.reshape(B, S, N_DIFF_HEADS, 2, DIFF_QK_DIM), diff_k_gain)
    fv = fv.reshape(B, S, N_DIFF_HEADS, HEAD_DIM)
    lam_init = 0.8 - 0.6 * math.exp(-0.3 * layer)
    lam = (jnp.exp(jnp.sum(lam_q1.astype(F32) * lam_k1.astype(F32)))
           - jnp.exp(jnp.sum(lam_q2.astype(F32) * lam_k2.astype(F32))) + lam_init)
    diff = differential_attention(fq[..., 0, :], fq[..., 1, :], fk[..., 0, :], fk[..., 1, :],
                                  fv, slopes[N_DIL_HEADS:], lam)
    diff = rms_norm_2(diff, diff_out_gain) * (1.0 - lam_init)
    mixed = jnp.concatenate([dil_out, diff], axis=2).reshape(B, S, D_MODEL).astype(u.dtype)
    return mixed @ w_out

def chunk_gated_recurrence(q, k, v, log_f):
    B, S, H, K = q.shape
    V = v.shape[-1]
    C = HGRN_CHUNK
    n = S // C
    rs = lambda t: t.reshape(B, n, C, H, t.shape[-1]).transpose(1, 0, 3, 2, 4)
    q, k, v, lf = rs(q), rs(k), rs(v), rs(log_f)
    b = jnp.cumsum(lf, axis=-2)
    b_last = b[..., -1:, :]
    b_mid = b[..., C // 2:C // 2 + 1, :]
    scores = jnp.einsum('nbhtk,nbhsk->nbhts', q * jnp.exp(b - b_mid), k * jnp.exp(b_mid - b))
    causal = jnp.tril(jnp.ones((C, C), dtype=bool))
    o_intra = jnp.einsum('nbhts,nbhsv->nbhtv', jnp.where(causal, scores, 0.0), v)
    q_inter = q * jnp.exp(b)
    k_state = k * jnp.exp(b_last - b)
    chunk_decay = jnp.exp(b_last[..., 0, :])

    def step(state, xs):
        qi, ks, vc, dec = xs
        o = jnp.einsum('bhtk,bhkv->bhtv', qi, state)
        state = dec[..., None] * state + jnp.einsum('bhsk,bhsv->bhkv', ks, vc)
        return state, o

    _, o_inter = lax.scan(step, jnp.zeros((B, H, K, V), F32), (q_inter, k_state, v, chunk_decay))
    o = o_intra + o_inter
    return o.transpose(1, 0, 3, 2, 4).reshape(B, S, H, V)

def hgrn2_mixer(u, w_in, lb_logits, out_gain, w_out, layer):
    B, S, _ = u.shape
    q, f_logit, i, g = jnp.split(u @ w_in, [HGRN_FORGET_DIM, 2 * HGRN_FORGET_DIM,
                                            2 * HGRN_FORGET_DIM + D_MODEL], axis=-1)
    sm = jax.nn.softmax(lb_logits.astype(F32), axis=0)
    lb = (jnp.cumsum(sm, axis=0) - sm[0])[layer]
    fl = f_logit.astype(F32)
    log_f = jnp.logaddexp(jnp.log(lb), jnp.log1p(-lb) + jax.nn.log_sigmoid(fl))
    k = (1.0 - lb) * jax.nn.sigmoid(-fl)
    q = jax.nn.silu(q.astype(F32))
    heads = lambda t, d: t.reshape(B, S, HGRN_HEADS, d)
    o = chunk_gated_recurrence(heads(q, HGRN_EXPAND), heads(k, HGRN_EXPAND),
                               heads(i.astype(F32), HGRN_VDIM), heads(log_f, HGRN_EXPAND))
    o = rms_norm_2(o, out_gain) * jax.nn.sigmoid(heads(g.astype(F32), HGRN_VDIM))
    return o.reshape(B, S, D_MODEL).astype(u.dtype) @ w_out

def swiglu(u, w_gate, w_up, w_down):
    return (jax.nn.silu(u @ w_gate) * (u @ w_up)) @ w_down

def moe_swiglu(u, w_router, w_gate, w_up, w_down):
    B, S, D = u.shape
    t = u.reshape(B * S, D)
    logits = (t @ w_router).astype(F32)
    top_vals, top_idx = lax.top_k(logits, TOP_K)
    top_w = jax.nn.softmax(top_vals, axis=-1)
    gates = jnp.sum(jax.nn.one_hot(top_idx, N_EXPERTS, dtype=F32) * top_w[..., None], axis=1)
    out = jnp.zeros((B * S, D), F32)
    for e in range(N_EXPERTS):
        y = swiglu(t, w_gate[e], w_up[e], w_down[e]).astype(F32)
        out = out + gates[:, e:e + 1] * y
    return out.reshape(B, S, D).astype(u.dtype)

def second_inputs(seed: int = 0) -> dict:
    key = jax.random.key(seed)
    ks = iter(jax.random.split(key, 40))
    nrm = lambda shape, scale: jax.random.normal(next(ks), shape, F32) * scale
    gain = lambda shape: 1.0 + nrm(shape, 0.02)
    D, E, O = D_MODEL, N_EVEN, N_ODD
    return {
        "x": nrm((BATCH, SEQ, D), 1.0),
        "attn_norm": gain((E, D)),
        "attn_w_in": nrm((E, D, ATTN_IN_WIDTH), D ** -0.5),
        "dil_q_gain": gain((E, HEAD_DIM)),
        "dil_k_gain": gain((E, HEAD_DIM)),
        "diff_q_gain": gain((E, DIFF_QK_DIM)),
        "diff_k_gain": gain((E, DIFF_QK_DIM)),
        "diff_lambda_q1": nrm((E, DIFF_QK_DIM), 0.1),
        "diff_lambda_k1": nrm((E, DIFF_QK_DIM), 0.1),
        "diff_lambda_q2": nrm((E, DIFF_QK_DIM), 0.1),
        "diff_lambda_k2": nrm((E, DIFF_QK_DIM), 0.1),
        "diff_out_gain": gain((E, HEAD_DIM)),
        "attn_w_out": nrm((E, D, D), D ** -0.5),
        "ffn_norm": gain((E, D)),
        "ffn_w_gate": nrm((E, D, D_FF), D ** -0.5),
        "ffn_w_up": nrm((E, D, D_FF), D ** -0.5),
        "ffn_w_down": nrm((E, D_FF, D), D_FF ** -0.5),
        "hgrn_norm": gain((O, D)),
        "hgrn_w_in": nrm((O, D, HGRN_IN_WIDTH), D ** -0.5),
        "hgrn_lb_logits": nrm((DEPTH_2, HGRN_FORGET_DIM), 0.5),
        "hgrn_out_gain": gain((O, HGRN_VDIM)),
        "hgrn_w_out": nrm((O, D, D), D ** -0.5),
        "moe_norm": gain((O, D)),
        "moe_w_router": nrm((O, D, N_EXPERTS), D ** -0.5),
        "moe_w_gate": nrm((O, N_EXPERTS, D, D_FF_EXPERT), D ** -0.5),
        "moe_w_up": nrm((O, N_EXPERTS, D, D_FF_EXPERT), D ** -0.5),
        "moe_w_down": nrm((O, N_EXPERTS, D_FF_EXPERT, D), D_FF_EXPERT ** -0.5),
    }

def second_block(x, attn_norm, attn_w_in, dil_q_gain, dil_k_gain, diff_q_gain, diff_k_gain,
              diff_lambda_q1, diff_lambda_k1, diff_lambda_q2, diff_lambda_k2, diff_out_gain,
              attn_w_out, ffn_norm, ffn_w_gate, ffn_w_up, ffn_w_down,
              hgrn_norm, hgrn_w_in, hgrn_lb_logits, hgrn_out_gain, hgrn_w_out,
              moe_norm, moe_w_router, moe_w_gate, moe_w_up, moe_w_down):
    h = x
    for layer in range(DEPTH_2):
        j = layer // 2
        if layer % 2 == 0:
            h = h + dilated_diff_mixer(rms_norm_2(h, attn_norm[j]), attn_w_in[j], dil_q_gain[j], dil_k_gain[j],
                                       diff_q_gain[j], diff_k_gain[j], diff_lambda_q1[j], diff_lambda_k1[j],
                                       diff_lambda_q2[j], diff_lambda_k2[j], diff_out_gain[j],
                                       attn_w_out[j], layer).astype(h.dtype)
            h = h + swiglu(rms_norm_2(h, ffn_norm[j]), ffn_w_gate[j], ffn_w_up[j], ffn_w_down[j]).astype(h.dtype)
        else:
            h = h + hgrn2_mixer(rms_norm_2(h, hgrn_norm[j]), hgrn_w_in[j], hgrn_lb_logits,
                                hgrn_out_gain[j], hgrn_w_out[j], layer).astype(h.dtype)
            h = h + moe_swiglu(rms_norm_2(h, moe_norm[j]), moe_w_router[j], moe_w_gate[j],
                               moe_w_up[j], moe_w_down[j]).astype(h.dtype)
    return h


def setup_inputs(seed=0):
    out = dict(first_inputs(seed))
    for name, value in second_inputs(seed + 1).items():
        if name != "x":
            out[name + "_2"] = value
    return out


def reference(
    x, mem, positions, attn_norm, w_in, lru_conv_w, lru_conv_b, lru_w_a, lru_b_a, lru_w_i,
    lru_b_i, lru_lambda, q_a_norm, w_uq, kv_a_norm, w_ukv, mla_q_norm, mla_k_norm, lru_out_norm,
    mla_out_norm, w_out, mem_attn_norm, mem_norm, w_mem_q, w_mem_kv, mem_q_norm, mem_k_norm,
    w_mem_o, ffn_norm, w_up, ffn_conv_w, ffn_conv_b, w_down, attn_norm_2, attn_w_in_2,
    dil_q_gain_2, dil_k_gain_2, diff_q_gain_2, diff_k_gain_2, diff_lambda_q1_2,
    diff_lambda_k1_2, diff_lambda_q2_2, diff_lambda_k2_2, diff_out_gain_2, attn_w_out_2,
    ffn_norm_2, ffn_w_gate_2, ffn_w_up_2, ffn_w_down_2, hgrn_norm_2, hgrn_w_in_2,
    hgrn_lb_logits_2, hgrn_out_gain_2, hgrn_w_out_2, moe_norm_2, moe_w_router_2, moe_w_gate_2,
    moe_w_up_2, moe_w_down_2,
):
    x = first_block(
        x, mem, positions, attn_norm, w_in, lru_conv_w, lru_conv_b, lru_w_a, lru_b_a, lru_w_i,
        lru_b_i, lru_lambda, q_a_norm, w_uq, kv_a_norm, w_ukv, mla_q_norm, mla_k_norm,
        lru_out_norm, mla_out_norm, w_out, mem_attn_norm, mem_norm, w_mem_q, w_mem_kv,
        mem_q_norm, mem_k_norm, w_mem_o, ffn_norm, w_up, ffn_conv_w, ffn_conv_b, w_down,
    )
    return second_block(
        x, attn_norm_2, attn_w_in_2, dil_q_gain_2, dil_k_gain_2, diff_q_gain_2, diff_k_gain_2,
        diff_lambda_q1_2, diff_lambda_k1_2, diff_lambda_q2_2, diff_lambda_k2_2, diff_out_gain_2,
        attn_w_out_2, ffn_norm_2, ffn_w_gate_2, ffn_w_up_2, ffn_w_down_2, hgrn_norm_2,
        hgrn_w_in_2, hgrn_lb_logits_2, hgrn_out_gain_2, hgrn_w_out_2, moe_norm_2,
        moe_w_router_2, moe_w_gate_2, moe_w_up_2, moe_w_down_2,
    )


_drawn_inputs = setup_inputs


def setup_inputs(seed=0):
    import zlib

    import numpy as np

    out = dict(_drawn_inputs(seed))
    spreads = {}
    factors = {'lru_b_a': 8.0,
     'lru_b_i': 8.0,
     'mem_attn_norm': 6.776,
     'mem_norm': 3.802,
     'mem_q_norm': 3.429,
     'mem_k_norm': 3.421,
     'ffn_conv_b': 3.707,
     'attn_norm_2': 2.848,
     'dil_q_gain_2': 8.0,
     'dil_k_gain_2': 8.0,
     'diff_q_gain_2': 8.0,
     'diff_k_gain_2': 5.434,
     'diff_lambda_q2_2': 6.539,
     'diff_lambda_k2_2': 2.824,
     'diff_out_gain_2': 24.886,
     'hgrn_norm_2': 33.785,
     'hgrn_out_gain_2': 109.476,
     'ffn_norm_2': 8.0,
     'moe_norm_2': 7.232}
    for name, (base, spread) in spreads.items():
        noise = np.random.default_rng([zlib.crc32(name.encode()), seed]).standard_normal(out[name].shape)
        drawn = base * np.exp(spread * noise) if base else spread * noise
        out[name] = __import__('jax').numpy.asarray(drawn.astype(out[name].dtype))
    for name, factor in factors.items():
        out[name] = (out[name] * factor).astype(out[name].dtype)
    return out
```

```python
import math

import numpy as np

import concourse.bass as bass
from concourse import mybir

F32 = mybir.dt.float32
I32 = mybir.dt.int32
U32 = mybir.dt.uint32
ALU = mybir.AluOpType
ACT = mybir.ActivationFunctionType
AX = mybir.AxisListType.X

P = 128
S = 256
TT = S // P
D = 1024
KD = D // P
EPS = 1e-6
HALF = 512
SLAB = 4096
RING = 7

LRU_W = 512
LC = LRU_W // P
Q_LORA, KV_LORA, ROPE = 256, 128, 32
HEADS, NOPE, QK, VD = 8, 64, 96, 64
TAIL = Q_LORA + KV_LORA + ROPE
D_FF = 2816
FT = D_FF // P
MEM_HEADS = 4
DIL_HEADS = 12
DIFF_HEADS = 4
HG_HEADS, CHUNK = 8, 64
NE, FE = 8, 3584
ECH = FE // HALF
E_SLABS = 3 * ECH
LAM_INIT = 0.8 - 0.6 * math.exp(-0.3 * 0)
FAR = 1.0e32


def offsets(sizes):
    at, out = 0, {}
    for name, n in sizes:
        out[name] = at
        at += n
    return out, at


CONST, N_CONST = offsets([("ident", P), ("ones", P), ("inv_freq", ROPE // 2), ("reset", S),
                          ("chunk_causal", P), ("tie", NE * NE), ("dist", 4 * (P + S))])
COLS, N_COLS = offsets([("attn_norm", KD), ("mem_attn_norm", KD), ("mem_norm", KD), ("ffn_norm", KD),
                        ("attn_norm_2", KD), ("ffn_norm_2", KD), ("hgrn_norm_2", KD), ("moe_norm_2", KD),
                        ("q_a_norm", 2), ("kv_a_norm", 1), ("lru_out_norm", LC), ("mla_out_norm", LC),
                        ("mem_q_norm", 1), ("mem_k_norm", 1), ("lru_conv_w", 8 * LC), ("lru_conv_b", 2 * LC),
                        ("lru_b_a", 2 * LC), ("lru_b_i", 2 * LC), ("lru_lambda", 2 * LC),
                        ("ffn_conv_w", 3 * 2 * FT), ("ffn_conv_b", 2 * FT), ("hgrn_lb_logits_2", 2 * HG_HEADS),
                        ("moe_w_router_2", KD * NE)])
ROWS, N_ROWS = offsets([("mla_q_norm", QK), ("mla_k_norm", QK), ("dil_q_gain_2", 64), ("dil_k_gain_2", 64),
                        ("diff_q_gain_2", 32), ("diff_k_gain_2", 32), ("diff_lambda_q1_2", 32),
                        ("diff_lambda_k1_2", 32), ("diff_lambda_q2_2", 32), ("diff_lambda_k2_2", 32),
                        ("diff_out_gain_2", 64), ("hgrn_out_gain_2", 128)])

SLABS, N_FIXED = offsets([("w_in", 3), ("lru_gates_uq", 1), ("w_ukv", 1), ("w_out", 2), ("w_mem_kv", 2), ("w_mem_q", 1),
                          ("w_mem_o", 1), ("w_up", 11), ("w_down", 6), ("attn_w_in", 6), ("attn_w_out", 2),
                          ("ffn_gate_up", 11), ("ffn_w_down", 6), ("hgrn_w_in", 8), ("hgrn_w_out", 2)])
N_SLABS = N_FIXED + NE * E_SLABS
assert N_FIXED % RING == 0 and E_SLABS % RING == 0
DIL_SLOPES = [2.0 ** (-8.0 * (h + 1) / 16) for h in range(16)]
NORMS = ["attn_norm", "mem_attn_norm", "mem_norm", "ffn_norm", "attn_norm_2", "ffn_norm_2", "hgrn_norm_2", "moe_norm_2"]


def build(nc, slabs, consts_d, cols_d, rows_d, x_d, mem_d, pos_d, out_d):
    def sb(name, shape, dt=F32):
        return nc.alloc_sbuf_tensor(name, [P] + shape, dt)

    ring = sb("ring", [RING, SLAB])
    x = sb("x", [TT, D])
    hT = sb("hT", [KD, S])
    xn = sb("xn", [TT, D])
    junk = sb("junk", [HALF])
    consts = sb("consts", [N_CONST])
    cols = sb("cols", [N_COLS])
    rows = sb("rows", [N_ROWS])
    pos = sb("pos", [TT], I32)
    small = sb("small", [416])
    work = sb("work", [13312])
    ps = nc.alloc_psum_tensor("ps", [P, 8, HALF], F32)

    taken = [0]

    def tiny(n):
        taken[0] += n
        assert taken[0] <= 416
        return small[:, taken[0] - n:taken[0]]

    def area(at, *shape):
        n = int(np.prod(shape))
        v = work[:, at:at + n]
        if len(shape) == 2:
            v = v.rearrange("p (a b) -> p a b", a=shape[0])
        if len(shape) == 3:
            v = v.rearrange("p (a b c) -> p a b c", a=shape[0], b=shape[1])
        return v

    def const(name, n, at=0):
        return consts[:, CONST[name] + at:CONST[name] + at + n]

    def col(name, c, n=1):
        return cols[:, COLS[name] + c:COLS[name] + c + n]

    def row(name, n):
        return rows[:, ROWS[name]:ROWS[name] + n]

    ident = const("ident", P)
    ones = const("ones", P)

    sems = {}

    SHARED = {
        "att_scores": (16, 8, 40), "att_max": (16, 8, 40), "att_probs": (16, 8, 40),
        "att_transposed": (16, 8, 40), "att_probsT": (16, 8, 40), "att_weighted": (16, 8, 40), "att_out": (16, 8, 40),
        "qkT_ps": dict(mla=8, mem=4, attn=8), "qkT": dict(mla=8, mem=8, attn=8),
        "oT_ps": dict(mla=2, mem=2, attn=4, hgrn=4), "oT": dict(mla=4, mem=2, attn=4, hgrn=4),
        "x_change": dict(mixer=5, memory=4, ffn=9, attn=5, ffn2=9, hgrn=5),
        "ms": dict(lru=1, latent=1, mla_head=2, mla=1, mem_head=2, attn_head=4, diff=1, hgrn=1),
        "std": dict(lru=1, latent=1, mla_head=2, mla=1, mem_head=2, attn_head=1, diff=1, hgrn=1),
        "gu": dict(ffn=FT, ffn2=FT), "gated_sigmoid": dict(ffn=FT, ffn2=FT), "gated_read": dict(ffn=FT, ffn2=FT),
    }
    place = {}
    for shared, parts in SHARED.items():
        start = 0
        for stage, n in (parts.items() if isinstance(parts, dict) else zip(("mla", "mem", "dil"), parts)):
            place[stage + "_" + shared] = (shared, start)
            start += n

    def sem(name):
        shared = place.get(name, (name, 0))[0]
        if shared not in sems:
            sems[shared] = nc.alloc_semaphore(shared)
        return sems[shared]

    def reached(name, value):
        return sem(name), value + place.get(name, (name, 0))[1]

    slab_loaded = [sem(f"slab_loaded{i}") for i in range(RING)]
    released = {}

    tail = area(0, TT, TAIL)
    xrp = area(832, LC, S + 6)
    yg = area(1880, LC, S)
    xc = [area(2904 + 1024 * d, LC, S) for d in range(2)]
    ra = [area(4952 + 1024 * d, LC, S) for d in range(2)]
    ri = [area(7000 + 1024 * d, LC, S) for d in range(2)]
    th = [area(9048 + 1024 * d, LC, S) for d in range(2)]
    mq = area(832, 2 * HEADS, QK)
    mk = area(2368, 2 * HEADS, QK)
    mv = area(3904, TT, HEADS * VD)
    mqT = area(4928, HEADS, S)
    mkT = area(6976, HEADS, S)
    msq = area(4928, 2 * HEADS, QK)
    mo = area(9024, TT, HEADS * VD)
    cn = area(11584, TT, 384)
    cT = area(12352, 3, S)
    mem = area(0, TT, D)
    memT = area(2048, KD, S)
    eq, ek, ev = area(4096, TT, HALF), area(5120, TT, HALF), area(6144, TT, HALF)
    eqT, ekT = area(7168, MEM_HEADS, S), area(8192, MEM_HEADS, S)
    eo = area(9216, TT, HALF)
    esq = area(11776, TT, HALF)
    hid = area(0, FT, S)
    cv = [[area(5632 + 512 * b + 256 * i, S) for i in range(2)] for b in range(2)]
    sg = [area(6656 + 256 * b, S) for b in range(2)]
    dq, dk, dv = area(0, TT, 768), area(1536, TT, 768), area(3072, TT, 768)
    fq, fk, fv = area(4608, TT, 256), area(5120, TT, 256), area(5632, TT, 256)
    dqT, dkT, fqT, fkT = area(6144, 6, S), area(7680, 6, S), area(9216, 2, S), area(9728, 2, S)
    dsq = area(11776, 1536)
    gq, gk, gB = area(0, HG_HEADS, S), area(2048, HG_HEADS, S), area(4096, HG_HEADS, S)
    gv, gg = area(6144, TT, D), area(8192, TT, D)
    gD, gQ, gK = area(10240, 4, S), area(11264, 4, S), area(12288, 4, S)
    kstT = hT[:, 0:4, :]
    AT = hT[:, 4:8, :].rearrange("p a b -> p (a b)").rearrange("p (h c) -> p h c", h=8)
    state = junk[:, 0:512].rearrange("p (h v) -> p h v", h=4)
    ehid = [area(1024 * b, 4, S) for b in range(2)]
    esg = [area(2048 + 256 * b, S) for b in range(4)]

    block_cm = nc.Block()
    block = block_cm.__enter__()

    ssq, msum, std, rstd = tiny(16), tiny(16), tiny(16), tiny(16)
    n_ssq = {}

    NORM_OF = {n: i for i, n in enumerate(NORMS)}
    X_AFTER = {"mixer": 4, "memory": 8, "ffn": 12, "attn2": 16, "ffn2": 20, "hgrn": 24}
    NORM_NEEDS = {"mem_attn_norm": 4, "ffn_norm": 8, "attn_norm_2": 12, "ffn_norm_2": 16, "hgrn_norm_2": 20,
                  "moe_norm_2": 24}

    def attention_units(stage):
        out = []
        if stage == "mla":
            for h in range(HEADS):
                for t in range(TT):
                    out.append(dict(q=mqT[0:QK, h, t * P:(t + 1) * P], k=mkT[0:QK, h, :], nk=S, dv=VD,
                                    v=[mv[:, j, h * VD:(h + 1) * VD] for j in range(2)], dist=None,
                                    out=mo[:, t, h * VD:(h + 1) * VD], kind="plain"))
        if stage == "mem":
            for h in range(MEM_HEADS):
                for t in range(TT):
                    out.append(dict(q=eqT[:, h, t * P:(t + 1) * P], k=ekT[:, h, :], nk=S, dv=P,
                                    v=[ev[:, j, h * P:(h + 1) * P] for j in range(2)], dist=None,
                                    out=eo[:, t, h * P:(h + 1) * P], kind="plain"))
        if stage == "dil":
            for h in range(DIL_HEADS):
                for t in range(TT):
                    b = 64 * (h % 2)
                    nk = P * (t + 1)
                    g = h // 4
                    out.append(dict(q=dqT[b:b + 64, h // 2, t * P:(t + 1) * P], k=dkT[b:b + 64, h // 2, 0:nk], nk=nk,
                                    dv=64, v=[dv[:, j, h * 64:(h + 1) * 64] for j in range(t + 1)],
                                    dist=const("dist", nk, g * (P + S) + t * P), slope=DIL_SLOPES[h],
                                    out=xn[:, t, h * 64:(h + 1) * 64], kind="raw"))
            for h in range(DIFF_HEADS):
                for t in range(TT):
                    for c in range(2):
                        b = 32 * ((2 * h + c) % 4)
                        a = (2 * h + c) // 4
                        nk = P * (t + 1)
                        out.append(dict(q=fqT[b:b + 32, a, t * P:(t + 1) * P], k=fkT[b:b + 32, a, 0:nk], nk=nk,
                                        dv=64, v=[fv[:, j, h * 64:(h + 1) * 64] for j in range(t + 1)],
                                        dist=const("dist", nk, 3 * (P + S) + t * P), slope=DIL_SLOPES[DIL_HEADS + h],
                                        out=xn[:, t, 768 + h * 64:768 + (h + 1) * 64],
                                        kind="plain" if c == 0 else "minus"))
        return out

    UNITS = {s: attention_units(s) for s in ("mla", "mem", "dil")}
    ATT_AT = {"mla": 10048, "mem": 10240, "dil": 10240}
    att = {}
    for s, at in ATT_AT.items():
        n = len(UNITS[s])
        att[s] = dict(s=[area(at + 256 * b, S) for b in range(2)], p=[area(at + 512 + 256 * b, S) for b in range(2)],
                      pT=[area(at + 1024 + 256 * b, S) for b in range(2)],
                      nmax=tiny(n), sum=tiny(n), inv=tiny(n))

    lam4 = tiny(8)
    sp = {k: tiny(8) for k in ("a", "b", "c", "s", "s2", "p", "out")}
    lat = {k: tiny(4) for k in ("ssq", "ms", "std", "r")}
    osq = {k: tiny(2) for k in ("ssq", "ms", "std", "r")}
    heads_st = [sb(f"heads_st{i}", [64]) for i in range(3)]
    rope = {k: area(13120 + 32 * i, TT, ROPE // 2) for i, k in enumerate(("ang", "k", "r", "sin", "cos", "tmp"))}
    lbs = {k: tiny(8) for k in ("d", "lb", "one_minus")}
    dec = tiny(32)
    attn_ms, attn_std = sb("attn_ms", [80]), sb("attn_std", [80])
    alpha = sb("alpha", [2, 24])
    rt = sb("rt", [5, TT, NE])
    rcmp = [area(12288 + 128 * i, TT * NE * NE) for i in range(2)]
    gates = sb("gates", [NE, TT])
    rtv = {k: tiny(2) for k in ("v1", "v2", "ex", "w1", "w2")}
    posf = tiny(2)

    counts = {}

    def counted(ins, name, by=1):
        counts[name] = counts.get(name, 0) + by
        ins.then_inc(sem(name), by)

    @block.tensor
    def _(pe):
        def slab(n):
            pe.wait_ge(slab_loaded[n % RING], 16 * (n // RING + 1))
            return ring[:, n % RING, :]

        def release(n, name):
            released[n] = reached(name, counts[name])

        def accumulate(out, pairs, first=True, last=True):
            for j, (l, r) in enumerate(pairs):
                ins = nc.tensor.matmul(out, l, r, start=(first and j == 0), stop=(last and j == len(pairs) - 1))
            return ins

        def norm(name):
            i = NORM_OF[name]
            pe.wait_ge(*reached("norm_xn", TT * (i + 1)))
            if i == 0:
                pe.wait_ge(*reached("params", 16 * 4))
            for g in range(4):
                for c2 in range(2):
                    for t in range(TT):
                        c = 2 * g + c2
                        ins = nc.tensor.transpose(ps[:, g, c2 * S + t * P:c2 * S + (t + 1) * P],
                                                  xn[:, t, c * P:(c + 1) * P], ident)
                counted(ins, "norm_transposed")
            pe.wait_ge(*reached("norm_out", KD * (i + 1)))

        def attention(stage):
            units = UNITS[stage]
            a = att[stage]
            n = len(units)
            for i in range(n + 2):
                if i < n:
                    u = units[i]
                    if i >= 2:
                        pe.wait_ge(*reached(stage + "_att_probs", i - 1))
                    counted(accumulate(ps[:, i % 2, 0:u["nk"]], [(u["q"], u["k"])]), stage + "_att_scores")
                j = i - 1
                if 0 <= j < n:
                    u = units[j]
                    pe.wait_ge(*reached(stage + "_att_probs", j + 1))
                    if j >= 2:
                        pe.wait_ge(*reached(stage + "_att_probsT", j - 1))
                    for b in range(u["nk"] // P):
                        ins = nc.tensor.transpose(ps[:, 2 + j % 2, b * P:(b + 1) * P], a["p"][j % 2][:, b * P:(b + 1) * P],
                                                  ident)
                    counted(ins, stage + "_att_transposed")
                j = i - 2
                if 0 <= j < n:
                    u = units[j]
                    pe.wait_ge(*reached(stage + "_att_probsT", j + 1))
                    if j >= 2:
                        pe.wait_ge(*reached(stage + "_att_out", j - 1))
                    counted(accumulate(ps[:, 4 + j % 2, 0:u["dv"]],
                                       [(a["pT"][j % 2][:, b * P:(b + 1) * P], u["v"][b]) for b in range(u["nk"] // P)]),
                            stage + "_att_weighted")

        def project_out(stage, slab0, nk, inT, ready):
            for s in range((nk + 3) // 4):
                w = slab(slab0 + s)
                ks = range(4 * s, min(4 * s + 4, nk))
                ready(ks[-1])
                for t in range(TT):
                    for h in range(2):
                        ins = accumulate(ps[:, 4 + 2 * t + h, :],
                                         [(inT[:, k, t * P:(t + 1) * P],
                                           w[:, (k - 4 * s) * D + h * HALF:(k - 4 * s) * D + (h + 1) * HALF]) for k in ks],
                                         first=(s == 0), last=(ks[-1] == nk - 1))
                        if h == 1 and t == 1 or ks[-1] == nk - 1:
                            counted(ins, stage)
                release(slab0 + s, stage)

        def transposes(stage, blocks, banks, evacuated):
            for g in range(0, len(blocks), 4):
                b = banks[(g // 4) % len(banks)]
                if g // 4 >= len(banks):
                    pe.wait_ge(*reached(evacuated, g // 4 - len(banks) + 1))
                for j, src in enumerate(blocks[g:g + 4]):
                    w = src.shape[-1]
                    ins = nc.tensor.transpose(ps[0:w, b, j * P:(j + 1) * P], src, ident)
                counted(ins, stage)

        norm("attn_norm")
        for s in range(2):
            w = slab(SLABS["w_in"] + s).rearrange("p (k n) -> p k n", k=KD)
            for c in range(LC):
                counted(accumulate(ps[:, 4 - 4 * s + c, 0:S],
                                   [(w[:, k, c * P:(c + 1) * P], hT[:, k, :]) for k in range(KD)]), "lru_in")
            release(SLABS["w_in"] + s, "lru_in")
        w = slab(SLABS["w_in"] + 2)[:, 0:KD * TAIL].rearrange("p (k n) -> p k n", k=KD)
        pe.wait_ge(*reached("lru_in_copied", TT))
        for t in range(TT):
            counted(accumulate(ps[:, 4 + t, 0:TAIL],
                               [(hT[:, k, t * P:(t + 1) * P], w[:, k, :]) for k in range(KD)]), "tail")
        release(SLABS["w_in"] + 2, "tail")

        w = slab(SLABS["lru_gates_uq"])
        pe.wait_ge(*reached("conv", 8 * 4))
        pe.wait_ge(*reached("lru_in_copied", 2 * LC))
        pe.wait_ge(*reached("tail_copied", TT))
        for d in range(2):
            for c in range(LC):
                for i in range(2):
                    m = ((d * 2 + i) * LC + c) * P
                    ins = accumulate(ps[:, d * 4 + c, i * S:(i + 1) * S], [(w[:, m:m + P], xc[d][:, c, :])])
                counted(ins, "lru_gates")
        pe.wait_ge(*reached("lru_sq", 1))
        pe.wait_ge(*reached("lru_sigmoid", 8))
        counted(accumulate(ps[:, 0, 0:S], [(ones, th[0][:, c, :]) for c in range(LC)]), "lru_ssq")

        pe.wait_ge(*reached("latent_normed", 4))
        for c in range(3):
            for t in range(TT):
                ins = nc.tensor.transpose(ps[:, 1 + c // 2, (c % 2) * S + t * P:(c % 2) * S + (t + 1) * P],
                                          cn[:, t, c * P:(c + 1) * P], ident)
        counted(ins, "latent_transposed")
        pe.wait_ge(*reached("latentT", 3))
        wq = w[:, 2048:2048 + 1536].rearrange("p (k n) -> p k n", k=2)
        for t in range(TT):
            for h in range(2):
                counted(accumulate(ps[:, 4 + 2 * t + h, 0:384],
                                   [(cT[:, k, t * P:(t + 1) * P], wq[:, k, h * 384:(h + 1) * 384]) for k in range(2)]),
                        "mla_q")
        release(SLABS["lru_gates_uq"], "mla_q")
        w = slab(SLABS["w_ukv"])
        pe.wait_ge(*reached("lru_done", 1))
        for t in range(TT):
            for h in range(2):
                counted(accumulate(ps[:, 2 * t + h, :], [(cT[:, 2, t * P:(t + 1) * P], w[:, h * HALF:(h + 1) * HALF])]),
                        "mla_kv")
        release(SLABS["w_ukv"], "mla_kv")
        pe.wait_ge(*reached("mla_rotated", 2))
        transposes("mla_qkT_ps", [m[:, t * HEADS + h, :] for m in (mq, mk) for h in range(HEADS) for t in range(TT)],
                   range(8), "mla_qkT")
        pe.wait_ge(*reached("mla_qkT", 8))
        attention("mla")
        pe.wait_ge(*reached("mla_normed", TT))
        transposes("mla_oT_ps", [xn[:, t, c * P:(c + 1) * P] for c in range(LC) for t in range(TT)], [0, 1], "")
        pe.wait_ge(*reached("mla_oT", LC))
        pe.wait_ge(*reached("lru_done", 1 + LC))
        project_out("mixer_x_change", SLABS["w_out"], KD, hT, lambda k: None)

        norm("mem_attn_norm")
        norm("mem_norm")
        for j, (s, src) in enumerate(((0, memT), (1, memT), (2, hT))):
            w = slab(SLABS["w_mem_kv"] + s).rearrange("p (k n) -> p k n", k=KD)
            for t in range(TT):
                counted(accumulate(ps[:, 2 * j + t, :], [(src[:, k, t * P:(t + 1) * P], w[:, k, :]) for k in range(KD)]),
                        "mem_in")
            release(SLABS["w_mem_kv"] + s, "mem_in")
        pe.wait_ge(*reached("mem_heads_normed", 2))
        transposes("mem_qkT_ps", [m[:, t, h * P:(h + 1) * P] for m in (eq, ek) for h in range(MEM_HEADS)
                                  for t in range(TT)], range(4), "")
        pe.wait_ge(*reached("mem_qkT", 8))
        attention("mem")
        pe.wait_ge(*reached("mem_att_out", 8))
        transposes("mem_oT_ps", [eo[:, t, c * P:(c + 1) * P] for c in range(4) for t in range(TT)], [0, 1], "")
        pe.wait_ge(*reached("mem_oT", 2))
        project_out("memory_x_change", SLABS["w_mem_o"], 4, hT, lambda k: None)

        def gated(stage, slab0):
            for f in range(FT):
                if f % 2 == 0:
                    w = slab(slab0 + f // 2).rearrange("p (k n) -> p k n", k=KD)
                if f >= 4:
                    pe.wait_ge(*reached(stage + "_gated_read", f - 3))
                for i in range(2):
                    ins = accumulate(ps[:, f % 4, i * S:(i + 1) * S],
                                     [(w[:, k, (2 * i + f % 2) * P:(2 * i + f % 2 + 1) * P], hT[:, k, :])
                                      for k in range(KD)])
                counted(ins, stage + "_gu")
                if f % 2 == 1:
                    release(slab0 + f // 2, stage + "_gu")

        norm("ffn_norm")
        gated("ffn", SLABS["w_up"])
        project_out("ffn_x_change", SLABS["w_down"], FT, hid, lambda k: pe.wait_ge(*reached("ffn_hid", k + 1)))

        norm("attn_norm_2")
        for j in range(6):
            w = slab(SLABS["attn_w_in"] + j).rearrange("p (k n) -> p k n", k=KD)
            for t in range(TT):
                g = 2 * j + t
                if g >= 8:
                    pe.wait_ge(*reached("attn_in_read", g - 7))
                counted(accumulate(ps[:, g % 8, :], [(hT[:, k, t * P:(t + 1) * P], w[:, k, :]) for k in range(KD)]),
                        "attn_in")
            release(SLABS["attn_w_in"] + j, "attn_in")
        pe.wait_ge(*reached("attn_heads_normed", 4))
        pe.wait_ge(*reached("attn_in_read", 12))
        transposes("attn_qkT_ps", [m[:, t, c * P:(c + 1) * P] for m, n in ((dq, 6), (dk, 6), (fq, 2), (fk, 2))
                                   for c in range(n) for t in range(TT)], range(8), "")
        pe.wait_ge(*reached("attn_qkT", 8))
        attention("dil")
        pe.wait_ge(*reached("attn_mixed", 2))
        transposes("attn_oT_ps", [xn[:, t, c * P:(c + 1) * P] for c in range(KD) for t in range(TT)], range(4), "")
        pe.wait_ge(*reached("attn_oT", 4))
        project_out("attn_x_change", SLABS["attn_w_out"], KD, hT, lambda k: None)

        norm("ffn_norm_2")
        gated("ffn2", SLABS["ffn_gate_up"])
        project_out("ffn2_x_change", SLABS["ffn_w_down"], FT, hid, lambda k: pe.wait_ge(*reached("ffn2_gated_read", k + 1)))

        norm("hgrn_norm_2")
        for g in range(24):
            if g < 16:
                s, c = g // 4, g % 4
            else:
                s, c = 4 + (g - 16) // 2, g % 2
            if c == 0:
                w = slab(SLABS["hgrn_w_in"] + s).rearrange("p (k n) -> p k n", k=KD)
            if 8 <= g < 16:
                pe.wait_ge(*reached("hgrn_q_read", g - 7))
            if g >= 16:
                pe.wait_ge(*reached("hgrn_in_read", g - 15))
            if g < 16:
                ins = accumulate(ps[:, g % 8, 0:S], [(w[:, k, c * P:(c + 1) * P], hT[:, k, :]) for k in range(KD)])
            else:
                ins = accumulate(ps[:, g % 8, :], [(hT[:, k, c * P:(c + 1) * P], w[:, k, :]) for k in range(KD)])
            counted(ins, "hgrn_in")
            if g < 16 and c == 3 or g >= 16 and c == 1:
                release(SLABS["hgrn_w_in"] + s, "hgrn_in")
        for half in range(2):
            pe.wait_ge(*reached("hgrn_in_read", 16))
            pe.wait_ge(*reached("hgrn_factors", 4 * half + 3))
            if half == 1:
                pe.wait_ge(*reached("hgrn_state", 12))
            for h in range(4):
                for c in range(4):
                    q0 = 64 * (c % 2)
                    for m, lo in ((32, 0), (64, 32)):
                        col0 = h * P + (c // 2) * 64 + lo
                        ins = nc.tensor.matmul(ps[q0:q0 + m, 0, col0:col0 + 32], gK[:, h, c * 64:c * 64 + m],
                                               gQ[:, h, c * 64 + lo:c * 64 + lo + 32], start=True, stop=True)
            counted(ins, "hgrn_scores")
            pe.wait_ge(*reached("hgrn_factors", 4 * half + 4))
            for h in range(4):
                for t in range(TT):
                    ins = nc.tensor.transpose(ps[:, 1 + h // 2, (h % 2) * S + t * P:(h % 2) * S + (t + 1) * P],
                                              gk[:, 4 * half + h, t * P:(t + 1) * P], ident)
            counted(ins, "hgrn_keysT")
            pe.wait_ge(*reached("hgrn_keysT_copied", 2 * (half + 1)))
            pe.wait_ge(*reached("hgrn_masked", half + 1))
            if half == 1:
                pe.wait_ge(*reached("hgrn_o_copied", 2))
            for c in range(4):
                q0, t = 64 * (c % 2), c // 2
                for h in range(4):
                    head = 4 * half + h
                    v = gv[q0:q0 + 64, t, head * P:(head + 1) * P]
                    o = ps[q0:q0 + 64, 4 + h // 2, (h % 2) * S + t * P:(h % 2) * S + (t + 1) * P]
                    ins = nc.tensor.matmul(o, AT[q0:q0 + 64, head, t * 64:(t + 1) * 64], v, start=True, stop=(c == 0))
                    if c > 0:
                        pe.wait_ge(*reached("hgrn_state", 12 * half + 4 * (c - 1) + h + 1))
                        ins = nc.tensor.matmul(o, gq[:, head, c * 64:(c + 1) * 64], state[:, h, :], start=False,
                                               stop=True)
                    counted(ins, "hgrn_o")
                if c < 3:
                    for h in range(4):
                        head = 4 * half + h
                        if c > 0 or half > 0:
                            pe.wait_ge(*reached("hgrn_state", 12 * half + 4 * c + h - 3))
                        counted(nc.tensor.matmul(ps[:, (3, 6, 7, 0)[h], 0:P], kstT[q0:q0 + 64, h, t * P:(t + 1) * P],
                                                 gv[q0:q0 + 64, t, head * P:(head + 1) * P], start=True, stop=True),
                                "hgrn_kv")
        pe.wait_ge(*reached("hgrn_gated", 1))
        pe.wait_ge(*reached("hgrn_o_copied", 4))
        transposes("hgrn_oT_ps", [xn[:, t, c * P:(c + 1) * P] for c in range(KD) for t in range(TT)], range(4), "")
        pe.wait_ge(*reached("hgrn_oT", 4))
        project_out("hgrn_x_change", SLABS["hgrn_w_out"], KD, hT, lambda k: None)

        norm("moe_norm_2")
        for t in range(TT):
            ins = accumulate(ps[:, 7, t * NE:(t + 1) * NE],
                             [(hT[:, k, t * P:(t + 1) * P], col("moe_w_router_2", k * NE, NE)) for k in range(KD)])
        counted(ins, "logits")
        pe.wait_ge(*reached("logits_read", 1))
        with nc.tensor.Fori(0, NE) as e:
            for ch in range(ECH + 1):
                if ch < ECH:
                    at = [(N_FIXED + 3 * ch + i) % RING for i in range(2)]
                    n = [(N_FIXED + 3 * ch + i) // RING for i in range(2)]
                    w = [ring[:, a, :].rearrange("p (k n) -> p k n", k=KD) for a in at]
                    for i in range(2):
                        pe.wait_ge(slab_loaded[at[i]], e * (16 * E_SLABS // RING) + 16 * (n[i] + 1))
                    for f in range(4):
                        pe.wait_ge(*reached("expert_hid", e * (4 * ECH) + 4 * ch + f + 1))
                        for i in range(2):
                            ins = accumulate(ps[:, f, i * S:(i + 1) * S],
                                             [(w[i][:, k, f * P:(f + 1) * P], hT[:, k, :]) for k in range(KD)])
                        ins.then_inc(sem("expert_gu"), 1)
                if ch >= 1:
                    c = ch - 1
                    a, m = (N_FIXED + 3 * c + 2) % RING, (N_FIXED + 3 * c + 2) // RING
                    pe.wait_ge(slab_loaded[a], e * (16 * E_SLABS // RING) + 16 * (m + 1))
                    pe.wait_ge(*reached("expert_hid", e * (4 * ECH) + 4 * (c + 2)))
                    if c == 0:
                        pe.wait_ge(*reached("expert_out_free", (e + 1) * 4))
                    for t in range(TT):
                        for h in range(2):
                            ins = accumulate(ps[:, 4 + 2 * t + h, :],
                                             [(ehid[c % 2][:, k, t * P:(t + 1) * P],
                                               ring[:, a, k * D + h * HALF:k * D + (h + 1) * HALF]) for k in range(4)],
                                             first=(c == 0), last=(c == ECH - 1))
                    ins.then_inc(sem("expert_down"), 1)

    @block.sync
    def _(sp_):
        sp_.dma_start(x[:], x_d).then_inc(sem("x_loaded"), 16)
        for n in range(N_FIXED):
            if n >= RING:
                sp_.wait_ge(*released[n - RING])
            sp_.dma_start(ring[:, n % RING, :], slabs[n]).then_inc(slab_loaded[n % RING], 16)

        def expert_release(j):
            c = j // 3
            return ("expert_down", c + 1) if j % 3 == 2 else ("expert_gu", 4 * (c + 1))

        for j in range(E_SLABS):
            n = N_FIXED + j
            if j < RING:
                sp_.wait_ge(*released[n - RING])
            else:
                name, v = expert_release(j - RING)
                sp_.wait_ge(*reached(name, v))
            sp_.dma_start(ring[:, n % RING, :], slabs[n]).then_inc(slab_loaded[n % RING], 16)
        with nc.sync.Fori(1, NE) as e:
            for j in range(E_SLABS):
                n = N_FIXED + j
                before = j - RING
                name, v = expert_release(before % E_SLABS)
                per = ECH if name == "expert_down" else 4 * ECH
                sp_.wait_ge(*reached(name, e * per + (v - (per if before < 0 else 0))))
                sp_.dma_start(ring[:, n % RING, :], slabs[e * E_SLABS + n]).then_inc(slab_loaded[n % RING], 16)
        for t in range(TT):
            sp_.wait_ge(*reached("x_final", 4))
            sp_.dma_start(out_d[:, t, :], x[:, t, :]).then_inc(sem("stored"), 16)
        sp_.wait_ge(*reached("stored", 16 * TT))

    @block.scalar
    def _(act):
        act.dma_start(consts[:], consts_d).then_inc(sem("params"), 16)
        act.dma_start(cols[:], cols_d).then_inc(sem("params"), 16)
        act.dma_start(rows[:], rows_d.partition_broadcast(P)).then_inc(sem("params"), 16)
        act.dma_start(pos[:], pos_d).then_inc(sem("params"), 16)
        A = nc.scalar.activation

        def norm(name):
            i = NORM_OF[name]
            src = mem if name == "mem_norm" else x
            if name == "attn_norm":
                act.wait_ge(*reached("x_loaded", 16))
            elif name == "mem_norm":
                act.wait_ge(*reached("mem_loaded", 16))
            else:
                act.wait_ge(*reached("x_ready", NORM_NEEDS[name]))
            for t in range(TT):
                if 2 * i + t >= 1:
                    act.wait_ge(*reached("norm_ssq", 2 * i + t))
                A(ps[:, 6:8, :].rearrange("p a b -> p (a b)"), src[:, t, :], ACT.Square, accum_out=ssq[:, 2 * i + t:2 * i + t + 1]).then_inc(sem("norm_ssq"), 1)
            act.wait_ge(*reached("norm_ms", i + 1))
            A(std[:, 2 * i:2 * i + 2], msum[:, 2 * i:2 * i + 2], ACT.Sqrt).then_inc(sem("norm_std"), 1)
            if i == 0:
                act.wait_ge(*reached("params", 16 * 4))
            dst = memT if name == "mem_norm" else hT
            for c in (0, 1, 4, 5):
                act.wait_ge(*reached("norm_transposed", 4 * i + c // 2 + 1))
                A(dst[:, c, :], ps[:, c // 2, (c % 2) * S:(c % 2 + 1) * S], ACT.Identity, scale=col(name, c)).then_inc(sem("norm_out"), 1)

        def sqrt_of(dst, src, ready, done):
            act.wait_ge(*reached(ready, 1))
            A(dst, src, ACT.Sqrt).then_inc(sem(done), 1)

        def attention(stage):
            a = att[stage]
            units = UNITS[stage]
            n = len(units)
            for i in range(n + 1):
                if i < n:
                    u = units[i]
                    act.wait_ge(*reached(stage + "_att_max", i + 1))
                    if i >= 2:
                        act.wait_ge(*reached(stage + "_att_transposed", i - 1))
                    src = ps[:, i % 2, 0:u["nk"]] if u["dist"] is None else a["s"][i % 2][:, 0:u["nk"]]
                    ins = A(a["p"][i % 2][:, 0:u["nk"]], src, ACT.Exp, bias=a["nmax"][:, i:i + 1],
                            accum_out=a["sum"][:, i:i + 1])
                    ins.then_inc(sem(stage + "_att_probs"), 1)
                j = i - 1
                if j >= 0:
                    u = units[j]
                    act.wait_ge(*reached(stage + "_att_transposed", j + 1))
                    if j >= 2:
                        act.wait_ge(*reached(stage + "_att_weighted", j - 1))
                    A(a["pT"][j % 2][:, 0:u["nk"]], ps[:, 2 + j % 2, 0:u["nk"]], ACT.Copy).then_inc(sem(stage + "_att_probsT"), 1)

        norm("attn_norm")
        for j in range(2 * LC):
            act.wait_ge(*reached("lru_in", j + 1))
            c = j % LC
            dst = xrp[:, c, 3:3 + S] if j < LC else yg[:, c, :]
            A(dst, ps[:, 4 - 4 * (j // LC) + c, 0:S], ACT.Copy).then_inc(sem("lru_in_copied"), 1)
        for t in range(TT):
            act.wait_ge(*reached("tail", t + 1))
            A(tail[:, t, :], ps[:, 4 + t, 0:TAIL], ACT.Copy).then_inc(sem("tail_copied"), 1)
        act.wait_ge(*reached("lam_abs", 1))
        A(sp["b"], sp["a"], ACT.Exp, scale=-1.0).then_inc(sem("lam_exp"), 1)
        for d in range(2):
            for c in range(LC):
                act.wait_ge(*reached("lru_gates", d * LC + c + 1))
                A(ra[d][:, c, :], ps[:, d * 4 + c, 0:S], ACT.Sigmoid, bias=col("lru_b_a", d * LC + c))
                A(ri[d][:, c, :], ps[:, d * 4 + c, S:2 * S], ACT.Sigmoid,
                  bias=col("lru_b_i", d * LC + c)).then_inc(sem("lru_sigmoid"), 1)
        act.wait_ge(*reached("softplus", 1))
        act.wait_ge(*reached("lru_sigmoid", 8))
        for d in range(2):
            for c in range(LC):
                s = sp["out"][:, d * LC + c:d * LC + c + 1]
                A(th[d][:, c, :], ra[d][:, c, :], ACT.Tanh, scale=s).then_inc(sem("lru_tanh"), 1)
        act.wait_ge(*reached("lru_tanh", 8))
        for d in range(2):
            for c in range(LC):
                s = sp["out"][:, d * LC + c:d * LC + c + 1]
                A(ra[d][:, c, :], ra[d][:, c, :], ACT.Exp, scale=s).then_inc(sem("lru_a"), 1)
        for d in range(2):
            act.wait_ge(*reached("lru_mult2", d + 1))
            A(th[d][:], th[d][:], ACT.Sqrt).then_inc(sem("lru_mult"), 1)
        act.wait_ge(*reached("gelu_z", 1))
        A(th[1][:], th[1][:], ACT.Sigmoid, scale=2.0 * math.sqrt(2.0 / math.pi)).then_inc(sem("gelu_sig"), 1)
        act.wait_ge(*reached("lru_gated", 1))
        A(th[0][:], ri[0][:], ACT.Square).then_inc(sem("lru_sq"), 1)
        sqrt_of(ri[1][:, 0, :], ri[1][:, 1, :], "lru_ms", "lru_std")
        for j, (t, a, b) in enumerate(((0, 0, 256), (1, 0, 256), (0, 256, 384), (1, 256, 384))):
            if j == 0:
                act.wait_ge(*reached("tail_copied", TT))
                act.wait_ge(*reached("norm_ssq", 2))
            else:
                act.wait_ge(*reached("latent_ssq", j))
            A(junk[:, 0:b - a], tail[:, t, a:b], ACT.Square, accum_out=lat["ssq"][:, j:j + 1]).then_inc(sem("latent_ssq"), 1)
        sqrt_of(lat["std"], lat["ms"], "latent_ms", "latent_std")
        act.wait_ge(*reached("latent_transposed", 1))
        for c in range(3):
            g = col("q_a_norm", c) if c < 2 else col("kv_a_norm", 0)
            A(cT[:, c, :], ps[:, 1 + c // 2, (c % 2) * S:(c % 2) * S + S], ACT.Identity, scale=g).then_inc(sem("latentT"), 1)
        for t in range(TT):
            for h in range(2):
                act.wait_ge(*reached("mla_q", 2 * t + h + 1))
                A(mq[:, t * HEADS + 4 * h:t * HEADS + 4 * h + 4, :],
                  ps[:, 4 + 2 * t + h, 0:384].rearrange("p (a b) -> p a b", a=4), ACT.Copy).then_inc(sem("mla_q_copied"), 1)
        for t in range(TT):
            for h in range(2):
                act.wait_ge(*reached("mla_kv", 2 * t + h + 1))
                kv = ps[:, 2 * t + h, :].rearrange("p (a b) -> p a b", a=4)
                A(mk[:, t * HEADS + 4 * h:t * HEADS + 4 * h + 4, 0:NOPE], kv[:, :, 0:NOPE], ACT.Copy)
                A(mv[:, t, h * 256:(h + 1) * 256].rearrange("p (a b) -> p a b", a=4), kv[:, :, NOPE:NOPE + VD],
                  ACT.Copy).then_inc(sem("mla_kv_copied"), 1)
        act.wait_ge(*reached("rope_angle", 2))
        A(rope["sin"][:], rope["r"][:], ACT.Sin)
        A(rope["cos"][:], rope["ang"][:], ACT.Sin).then_inc(sem("rope_table"), 1)
        for i in range(2):
            act.wait_ge(*reached("mla_head_ms", i + 1))
            A(heads_st[1][:, 16 * i:16 * i + 16], heads_st[0][:, 16 * i:16 * i + 16], ACT.Sqrt).then_inc(sem("mla_head_std"), 1)
        for g in range(8):
            act.wait_ge(*reached("mla_qkT_ps", g + 1))
            dst = (mqT if g < 4 else mkT)[0:QK, 2 * (g % 4):2 * (g % 4) + 2, :]
            A(dst, ps[0:QK, g, :].rearrange("p (a b) -> p a b", a=2), ACT.Copy).then_inc(sem("mla_qkT"), 1)
        attention("mla")
        for t in range(TT):
            act.wait_ge(*reached("mla_att_out", 16))
            if t == 0:
                act.wait_ge(*reached("latent_ssq", 4))
            else:
                act.wait_ge(*reached("mla_ssq", 1))
            A(junk[:, 0:HALF], mo[:, t, :], ACT.Square, accum_out=osq["ssq"][:, t:t + 1]).then_inc(sem("mla_ssq"), 1)
        sqrt_of(osq["std"], osq["ms"], "mla_ms", "mla_std")
        for c in range(LC):
            act.wait_ge(*reached("mla_oT_ps", c // 2 + 1))
            A(hT[:, LC + c, :], ps[:, c // 2, (c % 2) * S:(c % 2) * S + S], ACT.Identity,
              scale=col("mla_out_norm", c)).then_inc(sem("mla_oT"), 1)

        act.wait_ge(*reached("x_ready", X_AFTER["mixer"]))
        act.dma_start(mem[:], mem_d).then_inc(sem("mem_loaded"), 16)
        norm("mem_attn_norm")
        norm("mem_norm")
        for j in range(6):
            act.wait_ge(*reached("mem_in", j + 1))
            dst = (ek, ev, eq)[j // 2]
            A(dst[:, j % 2, :], ps[:, j, :], ACT.Copy).then_inc(sem("mem_in_copied"), 1)
        for i in range(2):
            act.wait_ge(*reached("mem_head_ms", i + 1))
            A(heads_st[1][:, 32 + 8 * i:40 + 8 * i], heads_st[0][:, 32 + 8 * i:40 + 8 * i],
              ACT.Sqrt).then_inc(sem("mem_head_std"), 1)
        for j in range(8):
            act.wait_ge(*reached("mem_qkT_ps", j // 2 + 1))
            h = j % 4
            A((eqT if j < 4 else ekT)[:, h, :], ps[:, j // 2, (j % 2) * S:(j % 2) * S + S], ACT.Identity,
              scale=col("mem_q_norm" if j < 4 else "mem_k_norm", 0)).then_inc(sem("mem_qkT"), 1)
        attention("mem")
        for g in range(2):
            act.wait_ge(*reached("mem_oT_ps", g + 1))
            A(hT[:, 2 * g:2 * g + 2, :], ps[:, g, :].rearrange("p (a b) -> p a b", a=2), ACT.Copy).then_inc(sem("mem_oT"), 1)

        norm("ffn_norm")
        for f in range(FT + 1):
            if f < FT:
                act.wait_ge(*reached("ffn_gu", f + 1))
                if f >= 2:
                    act.wait_ge(*reached("ffn_hid", f - 1))
                for i in range(2):
                    c = f + i * FT
                    ins = A(cv[f % 2][i], ps[:, f % 4, i * S:(i + 1) * S], ACT.Identity,
                            scale=col("ffn_conv_w", 2 * FT + c), bias=col("ffn_conv_b", c))
                ins.then_inc(sem("ffn_centre"), 1)
            if f >= 1:
                j = f - 1
                act.wait_ge(*reached("ffn_gated_read", j + 1))
                A(sg[j % 2], cv[j % 2][0], ACT.Sigmoid).then_inc(sem("ffn_gated_sigmoid"), 1)

        norm("attn_norm_2")
        pieces = [(dq, 0, 768), (dk, 768, 1536), (dv, 1536, 2304), (fq, 2304, 2560), (fk, 2560, 2816), (fv, 2816, 3072)]
        for j in range(6):
            for t in range(TT):
                act.wait_ge(*reached("attn_in", 2 * j + t + 1))
                for dst, a, b in pieces:
                    lo, hi = max(a, j * HALF), min(b, (j + 1) * HALF)
                    if lo < hi:
                        ins = A(dst[:, t, lo - a:hi - a], ps[:, (2 * j + t) % 8, lo - j * HALF:hi - j * HALF], ACT.Copy)
                ins.then_inc(sem("attn_in_read"), 1)
        act.wait_ge(*reached("attn_head_ms", 4))
        A(attn_std[:], attn_ms[:], ACT.Sqrt).then_inc(sem("attn_head_std"), 1)
        act.wait_ge(*reached("lam_dots", 2))
        A(lam4[:, 2:4], lam4[:, 0:2], ACT.Exp).then_inc(sem("lam_exps"), 1)
        for g in range(8):
            act.wait_ge(*reached("attn_qkT_ps", g + 1))
            dst = [dqT, dqT, dqT, dkT, dkT, dkT, fqT, fkT][g]
            c = 2 * (g % 3) if g < 6 else 0
            A(dst[:, c:c + 2, :], ps[:, g, :].rearrange("p (a b) -> p a b", a=2), ACT.Copy).then_inc(sem("attn_qkT"), 1)
        attention("dil")
        act.wait_ge(*reached("alpha_diff", 1))
        A(alpha[:, 0], alpha[:, 0], ACT.Exp).then_inc(sem("alpha_exp"), 1)
        act.wait_ge(*reached("diff_ms", 1))
        A(heads_st[1][:, 48:56], heads_st[0][:, 48:56], ACT.Sqrt).then_inc(sem("diff_std"), 1)
        for g in range(4):
            act.wait_ge(*reached("attn_oT_ps", g + 1))
            A(hT[:, 2 * g:2 * g + 2, :], ps[:, g, :].rearrange("p (a b) -> p a b", a=2), ACT.Copy).then_inc(sem("attn_oT"), 1)

        norm("ffn_norm_2")
        for f in range(FT):
            act.wait_ge(*reached("ffn2_gu", f + 1))
            if f >= 2:
                act.wait_ge(*reached("ffn2_gated_read", f - 1))
            A(sg[f % 2], ps[:, f % 4, 0:S], ACT.Sigmoid).then_inc(sem("ffn2_gated_sigmoid"), 1)

        act.wait_ge(*reached("lb_diff", 1))
        A(lbs["lb"], lbs["d"], ACT.Sigmoid)
        A(lbs["one_minus"], lbs["d"], ACT.Sigmoid, scale=-1.0).then_inc(sem("lb"), 1)
        norm("hgrn_norm_2")
        for g in range(24):
            act.wait_ge(*reached("hgrn_in", g + 1))
            if g < 8:
                A(gq[:, g, :], ps[:, g % 8, 0:S], ACT.Sigmoid).then_inc(sem("hgrn_q_sigmoid"), 1)
            elif g < 16:
                A(gB[:, g - 8, :], ps[:, g % 8, 0:S], ACT.Sigmoid)
                A(gk[:, g - 8, :], ps[:, g % 8, 0:S], ACT.Sigmoid, scale=-1.0).then_inc(sem("hgrn_in_read"), 1)
            elif g < 20:
                A(gv[:, g % 2, ((g - 16) // 2) * HALF:((g - 16) // 2 + 1) * HALF], ps[:, g % 8, :],
                  ACT.Copy).then_inc(sem("hgrn_in_read"), 1)
            else:
                A(gg[:, g % 2, ((g - 20) // 2) * HALF:((g - 20) // 2 + 1) * HALF], ps[:, g % 8, :],
                  ACT.Sigmoid).then_inc(sem("hgrn_in_read"), 1)
        act.wait_ge(*reached("hgrn_forget", 1))
        A(gB[:], gB[:], ACT.Ln).then_inc(sem("hgrn_logf"), 1)
        for half in range(2):
            hs = slice(4 * half, 4 * half + 4)
            act.wait_ge(*reached("hgrn_d1", half + 1))
            if half == 1:
                act.wait_ge(*reached("hgrn_scores", 1))
            A(gQ[:], gD[:], ACT.Exp).then_inc(sem("hgrn_eq"), 1)
            A(gK[:], gD[:], ACT.Exp, scale=-1.0).then_inc(sem("hgrn_eq"), 1)
            act.wait_ge(*reached("hgrn_eq", 4 * half + 2))
            A(gD[:], gB[:, hs, :], ACT.Exp).then_inc(sem("hgrn_eq"), 1)
            A(dec[:, 16 * half:16 * half + 16], gB[:, hs, :].rearrange("p h (c j) -> p (h c) j", j=CHUNK)[:, :, CHUNK - 1], ACT.Exp).then_inc(sem("hgrn_dec"), 1)
            act.wait_ge(*reached("hgrn_d2", half + 1))
            A(gD[:], gD[:], ACT.Exp).then_inc(sem("hgrn_eq"), 1)
            for b in range(2):
                act.wait_ge(*reached("hgrn_keysT", half + 1))
                if half == 1:
                    act.wait_ge(*reached("hgrn_kv", 12))
                A(kstT[:, 2 * b:2 * b + 2, :], ps[:, 1 + b, :].rearrange("p (a c) -> p a c", a=2),
                  ACT.Copy).then_inc(sem("hgrn_keysT_copied"), 1)
            for b in range(2):
                act.wait_ge(*reached("hgrn_o", 16 * (half + 1)))
                for t in range(TT):
                    dst = xn[:, t, (4 * half + 2 * b) * P:(4 * half + 2 * b + 2) * P].rearrange("p (a v) -> p a v", a=2)
                    src = ps[:, 4 + b, :].rearrange("p (a t v) -> p t a v", a=2, t=TT)[:, t]
                    ins = A(dst, src, ACT.Copy)
                ins.then_inc(sem("hgrn_o_copied"), 1)
        act.wait_ge(*reached("hgrn_ms", 1))
        A(heads_st[1][:, 0:16], heads_st[0][:, 0:16], ACT.Sqrt).then_inc(sem("hgrn_std"), 1)
        for g in range(4):
            act.wait_ge(*reached("hgrn_oT_ps", g + 1))
            A(hT[:, 2 * g:2 * g + 2, :], ps[:, g, :].rearrange("p (a b) -> p a b", a=2), ACT.Copy).then_inc(sem("hgrn_oT"), 1)

        norm("moe_norm_2")
        act.wait_ge(*reached("route_diff", 1))
        A(rtv["ex"], rtv["v2"], ACT.Exp).then_inc(sem("route_exp"), 1)
        with nc.scalar.Fori(0, NE) as e:
            for i in range(4 * ECH):
                act.wait_ge(*reached("expert_gu", e * (4 * ECH) + i + 1))
                A(esg[i % 4], ps[:, i % 4, 0:S], ACT.Sigmoid).then_inc(sem("expert_sigmoid"), 1)

    @block.vector
    def _(dve):
        V = nc.vector
        steps = [0]

        def step(ins):
            ins.then_inc(sem("vector_step"), 1)
            steps[0] += 1
            dve.wait_ge(*reached("vector_step", steps[0]))

        def settle():
            step(V.tensor_copy(lam4[:, 7:8], ones[:, 0:1]))

        def norm(name):
            i = NORM_OF[name]
            src = mem if name == "mem_norm" else x
            dve.wait_ge(*reached("norm_ssq", 2 * (i + 1)))
            V.tensor_scalar(msum[:, 2 * i:2 * i + 2], ssq[:, 2 * i:2 * i + 2], 1.0 / D, EPS, ALU.mult,
                            ALU.add).then_inc(sem("norm_ms"), 1)
            dve.wait_ge(*reached("norm_std", i + 1))
            step(V.reciprocal(rstd[:, 2 * i:2 * i + 2], std[:, 2 * i:2 * i + 2]))
            if i > 0:
                dve.wait_ge(*reached("norm_transposed", 4 * i))
            for t in range(TT):
                V.tensor_scalar(xn[:, t, :], src[:, t, :], rstd[:, 2 * i + t:2 * i + t + 1], None,
                                ALU.mult).then_inc(sem("norm_xn"), 1)
            dst = memT if name == "mem_norm" else hT
            for c in (2, 3, 6, 7):
                dve.wait_ge(*reached("norm_transposed", 4 * i + c // 2 + 1))
                V.tensor_scalar(dst[:, c, :], ps[:, c // 2, (c % 2) * S:(c % 2 + 1) * S], col(name, c), None,
                                ALU.mult).then_inc(sem("norm_out"), 1)

        def residual(stage, n):
            for t in range(TT):
                for h in range(2):
                    dve.wait_ge(*reached(stage, n - 3 + 2 * t + h))
                    xs = x[:, t, h * HALF:(h + 1) * HALF]
                    V.tensor_tensor(xs, ps[:, 4 + 2 * t + h, :], xs, ALU.add).then_inc(sem("x_ready"), 1)

        def attention(stage):
            a = att[stage]
            units = UNITS[stage]
            n = len(units)
            for i in range(n + 2):
                if i < n:
                    u = units[i]
                    dve.wait_ge(*reached(stage + "_att_scores", i + 1))
                    src = ps[:, i % 2, 0:u["nk"]]
                    nm = a["nmax"][:, i:i + 1]
                    if u["dist"] is None:
                        V.reduce_max(nm, src, AX, negate=True).then_inc(sem(stage + "_att_max"), 1)
                    else:
                        if i >= 2:
                            dve.wait_ge(*reached(stage + "_att_probs", i - 1))
                        s = a["s"][i % 2][:, 0:u["nk"]]
                        step(V.scalar_tensor_tensor(out=s, in0=u["dist"], scalar=-u["slope"], in1=src, op0=ALU.mult,
                                                    op1=ALU.add))
                        V.reduce_max(nm, s, AX, negate=True).then_inc(sem(stage + "_att_max"), 1)
                j = i - 2
                if j >= 0:
                    u = units[j]
                    dve.wait_ge(*reached(stage + "_att_probs", j + 1))
                    inv = a["inv"][:, j:j + 1]
                    if u["kind"] == "raw":
                        dve.wait_ge(*reached(stage + "_att_weighted", j + 1))
                        V.tensor_copy(u["out"], ps[:, 4 + j % 2, 0:u["dv"]]).then_inc(sem(stage + "_att_out"), 1)
                        continue
                    step(V.reciprocal(inv, a["sum"][:, j:j + 1]))
                    if u["kind"] == "minus":
                        step(V.tensor_scalar(inv, inv, lam4[:, 4:5], None, ALU.mult))
                    dve.wait_ge(*reached(stage + "_att_weighted", j + 1))
                    if u["kind"] == "plain":
                        V.tensor_scalar(u["out"], ps[:, 4 + j % 2, 0:u["dv"]], inv, None,
                                        ALU.mult).then_inc(sem(stage + "_att_out"), 1)
                    else:
                        dve.wait_ge(*reached(stage + "_att_out", j))
                        V.scalar_tensor_tensor(out=u["out"], in0=ps[:, 4 + j % 2, 0:u["dv"]], scalar=inv, in1=u["out"],
                                               op0=ALU.mult, op1=ALU.add).then_inc(sem(stage + "_att_out"), 1)
            settle()

        def head_norm(buf, n, w, scratch, ms, stdv, inv, ready, std_sem, std_n, gain, scale):
            sq = scratch[:, 0:n * w].rearrange("p (a b) -> p a b", a=n)
            step(V.tensor_tensor(sq, buf, buf, ALU.mult))
            step(V.tensor_reduce(ms, sq, AX, ALU.add))
            V.tensor_scalar(ms, ms, 1.0 / (w * scale * scale), EPS / (scale * scale), ALU.mult,
                            ALU.add).then_inc(sem(ready), 1)
            dve.wait_ge(*reached(std_sem, std_n))
            step(V.reciprocal(inv, stdv))
            step(V.tensor_tensor(buf, buf, inv.unsqueeze(2).to_broadcast([P, n, w]), ALU.mult))
            if gain is not None:
                step(V.tensor_tensor(buf, buf, gain.unsqueeze(1).to_broadcast([P, n, w]), ALU.mult))

        V.memset(xrp[:, :, 0:3], 0.0)
        step(V.memset(xrp[:, :, S + 3:S + 6], 0.0))
        norm("attn_norm")
        lam = col("lru_lambda", 0, 8)
        step(V.tensor_scalar(sp["c"], lam, -1.0, None, ALU.mult))
        V.tensor_tensor(sp["a"], sp["c"], lam, ALU.max).then_inc(sem("lam_abs"), 1)
        dve.wait_ge(*reached("lam_exp", 1))
        step(V.tensor_scalar(sp["s"], sp["b"], 2.0, None, ALU.add))
        step(V.reciprocal(sp["s"], sp["s"]))
        step(V.tensor_tensor(sp["s"], sp["s"], sp["b"], ALU.mult))
        step(V.tensor_tensor(sp["s2"], sp["s"], sp["s"], ALU.mult))
        step(V.tensor_scalar(sp["p"], sp["s2"], 1.0 / 17, None, ALU.mult))
        for n in (15, 13, 11, 9, 7, 5, 3):
            step(V.scalar_tensor_tensor(out=sp["p"], in0=sp["p"], scalar=1.0 / n, in1=sp["s2"], op0=ALU.add, op1=ALU.mult))
        step(V.scalar_tensor_tensor(out=sp["p"], in0=sp["p"], scalar=1.0, in1=sp["s"], op0=ALU.add, op1=ALU.mult))
        step(V.tensor_scalar(sp["c"], sp["c"], 0.0, -8.0, ALU.max, ALU.mult))
        V.scalar_tensor_tensor(out=sp["out"], in0=sp["p"], scalar=-16.0, in1=sp["c"], op0=ALU.mult,
                               op1=ALU.add).then_inc(sem("softplus"), 1)
        for k in range(4):
            for d in range(2):
                for c in range(LC):
                    j = d * LC + c
                    if k == 0:
                        dve.wait_ge(*reached("lru_in_copied", c + 1))
                    elif j == 0:
                        dve.wait_ge(*reached("conv", 8 * k))
                    src = xrp[:, c, k + 3 * d:k + 3 * d + S]
                    w = col("lru_conv_w", (d * 4 + k) * LC + c)
                    if k == 0:
                        ins = V.tensor_scalar(xc[d][:, c, :], src, w, col("lru_conv_b", d * LC + c), ALU.mult, ALU.add)
                    else:
                        ins = V.scalar_tensor_tensor(out=xc[d][:, c, :], in0=src, scalar=w, in1=xc[d][:, c, :],
                                                     op0=ALU.mult, op1=ALU.add)
                    ins.then_inc(sem("conv"), 1)
        dve.wait_ge(*reached("lru_in_copied", 8))
        dve.wait_ge(*reached("conv", 32))
        for d in range(2):
            dve.wait_ge(*reached("lru_tanh", 4 * (d + 1)))
            dve.wait_ge(*reached("lru_sigmoid", 8))
            u = xrp[:].rearrange("p a b -> p (a b)")[:, 0:1024].rearrange("p (a b) -> p a b", a=4)
            step(V.tensor_scalar(u, th[d][:], -1.0, 1.0, ALU.mult, ALU.add))
            step(V.reciprocal(u, u))
            V.scalar_tensor_tensor(out=th[d][:], in0=th[d][:], scalar=-2.0, in1=u, op0=ALU.mult,
                                   op1=ALU.mult).then_inc(sem("lru_mult2"), 1)
            step(V.tensor_tensor(ri[d][:], ri[d][:], xc[d][:], ALU.mult))
        for d in range(2):
            dve.wait_ge(*reached("lru_mult", d + 1))
            dve.wait_ge(*reached("lru_a", 4 * (d + 1)))
            step(V.tensor_tensor(ri[d][:], ri[d][:], th[d][:], ALU.mult))
            for c in range(LC):
                r = slice(None, None, -1) if d else slice(None)
                ins = V.tensor_tensor_scan(xc[d][:, c, r], ra[d][:, c, r], ri[d][:, c, r], 0.0, ALU.mult, ALU.add)
            step(ins)
        z = th[1]
        step(V.tensor_tensor(z[:], yg[:], yg[:], ALU.mult))
        step(V.tensor_scalar(z[:], z[:], 0.044715, 1.0, ALU.mult, ALU.add))
        V.tensor_tensor(z[:], z[:], yg[:], ALU.mult).then_inc(sem("gelu_z"), 1)
        step(V.tensor_tensor(xc[0][:], xc[0][:], xc[1][:], ALU.add))
        step(V.tensor_tensor(xc[0][:], xc[0][:], yg[:], ALU.mult))
        dve.wait_ge(*reached("gelu_sig", 1))
        V.tensor_tensor(ri[0][:], xc[0][:], z[:], ALU.mult).then_inc(sem("lru_gated"), 1)
        dve.wait_ge(*reached("lru_ssq", 1))
        V.tensor_scalar(ri[1][:, 1, :], ps[:, 0, 0:S], 1.0 / LRU_W, EPS, ALU.mult, ALU.add).then_inc(sem("lru_ms"), 1)
        dve.wait_ge(*reached("lru_std", 1))
        ins = V.reciprocal(ri[1][:, 2, :], ri[1][:, 0, :])
        ins.then_inc(sem("lru_done"), 1)
        dve.wait_ge(*reached("lru_done", 1))
        for c in range(LC):
            V.scalar_tensor_tensor(out=hT[:, c, :], in0=ri[0][:, c, :], scalar=col("lru_out_norm", c), in1=ri[1][:, 2, :],
                                   op0=ALU.mult, op1=ALU.mult).then_inc(sem("lru_done"), 1)
        dve.wait_ge(*reached("latent_ssq", 4))
        V.tensor_scalar(lat["ms"][:, 0:2], lat["ssq"][:, 0:2], 1.0 / Q_LORA, EPS, ALU.mult, ALU.add)
        step(V.tensor_scalar(lat["ms"][:, 2:4], lat["ssq"][:, 2:4], 1.0 / KV_LORA, EPS, ALU.mult, ALU.add))
        V.sem_inc(sem("latent_ms"), 1)
        dve.wait_ge(*reached("latent_std", 1))
        step(V.reciprocal(lat["r"], lat["std"]))
        for j, (t, a, b) in enumerate(((0, 0, 256), (1, 0, 256), (0, 256, 384), (1, 256, 384))):
            V.tensor_scalar(cn[:, t, a:b], tail[:, t, a:b], lat["r"][:, j:j + 1], None, ALU.mult).then_inc(sem("latent_normed"), 1)
        dve.wait_ge(*reached("params", 64))
        step(V.tensor_copy(posf, pos[:]))
        for t in range(TT):
            ins = V.tensor_scalar(rope["ang"][:, t, :], const("inv_freq", ROPE // 2), posf[:, t:t + 1], None, ALU.mult)
        step(ins)
        turn = 2.0 * math.pi
        c1 = float(np.float32(np.round(turn * 256) / 256))
        c2 = float(np.float32(np.round((turn - c1) * 2 ** 20) / 2 ** 20))
        c3 = float(np.float32(turn - c1 - c2))
        near = 1.5 * 2.0 ** 23

        def reduced(dst, src):
            step(V.tensor_scalar(rope["k"][:], src, 1.0 / turn, near, ALU.mult, ALU.add))
            step(V.tensor_scalar(rope["k"][:], rope["k"][:], near, None, ALU.subtract))
            for n, cc in enumerate((c1, c2, c3)):
                step(V.scalar_tensor_tensor(out=dst, in0=rope["k"][:], scalar=-cc, in1=(src if n == 0 else dst),
                                            op0=ALU.mult, op1=ALU.add))
            step(V.tensor_scalar(dst, dst, math.pi * (1 - 1e-7), -math.pi * (1 - 1e-7), ALU.min, ALU.max))

        reduced(rope["r"][:], rope["ang"][:])
        V.sem_inc(sem("rope_angle"), 1)
        step(V.tensor_scalar(rope["tmp"][:], rope["r"][:], math.pi / 2, None, ALU.add))
        reduced(rope["ang"][:], rope["tmp"][:])
        V.sem_inc(sem("rope_angle"), 1)
        dve.wait_ge(*reached("mla_q_copied", 4))
        dve.wait_ge(*reached("mla_kv_copied", 4))
        for t in range(TT):
            ins = V.tensor_copy(mk[:, t * HEADS:(t + 1) * HEADS, NOPE:QK],
                                tail[:, t, 384:416].unsqueeze(1).to_broadcast([P, HEADS, ROPE]))
        step(ins)
        msq_flat = msq[:].rearrange("p a b -> p (a b)")
        for i, (m, gain, scale) in enumerate(((mq, "mla_q_norm", QK ** -0.5), (mk, "mla_k_norm", 1.0))):
            st = [h[:, 16 * i:16 * i + 16] for h in heads_st]
            head_norm(m, 16, QK, msq_flat, st[0], st[1], st[2], "mla_head_ms", "mla_head_std", i + 1, row(gain, QK), scale)
            dve.wait_ge(*reached("rope_table", 1))
            H2 = ROPE // 2
            m4 = m.rearrange("p (t h) c -> p t h c", t=TT)
            t1, t2 = m4[:, :, :, NOPE:NOPE + H2], m4[:, :, :, NOPE + H2:QK]
            cosb = rope["cos"][:].unsqueeze(2).to_broadcast([P, TT, HEADS, H2])
            sinb = rope["sin"][:].unsqueeze(2).to_broadcast([P, TT, HEADS, H2])
            tmp = [msq_flat[:, 256 * j:256 * j + 256].rearrange("p (t h c) -> p t h c", t=TT, h=HEADS) for j in range(4)]
            V.tensor_tensor(tmp[0], t1, cosb, ALU.mult)
            V.tensor_tensor(tmp[1], t2, sinb, ALU.mult)
            V.tensor_tensor(tmp[2], t1, sinb, ALU.mult)
            step(V.tensor_tensor(tmp[3], t2, cosb, ALU.mult))
            V.tensor_tensor(t1, tmp[0], tmp[1], ALU.subtract)
            step(V.tensor_tensor(t2, tmp[2], tmp[3], ALU.add))
            V.sem_inc(sem("mla_rotated"), 1)
        attention("mla")
        dve.wait_ge(*reached("mla_ssq", TT))
        V.tensor_scalar(osq["ms"], osq["ssq"], 1.0 / HALF, EPS, ALU.mult, ALU.add).then_inc(sem("mla_ms"), 1)
        dve.wait_ge(*reached("mla_std", 1))
        step(V.reciprocal(osq["r"], osq["std"]))
        for t in range(TT):
            V.tensor_scalar(xn[:, t, 0:HALF], mo[:, t, :], osq["r"][:, t:t + 1], None, ALU.mult).then_inc(sem("mla_normed"), 1)
        residual("mixer_x_change", 5)

        norm("mem_attn_norm")
        norm("mem_norm")
        dve.wait_ge(*reached("mem_in_copied", 6))
        for i, (m, scale) in enumerate(((eq, P ** -0.5), (ek, 1.0))):
            st = [h[:, 32 + 8 * i:40 + 8 * i] for h in heads_st]
            head_norm(m[:].rearrange("p t (h c) -> p (t h) c", h=MEM_HEADS), 8, P, esq[:].rearrange("p a b -> p (a b)"),
                      st[0], st[1], st[2], "mem_head_ms", "mem_head_std", i + 1, None, scale)
            V.sem_inc(sem("mem_heads_normed"), 1)
        attention("mem")
        residual("memory_x_change", 4)

        norm("ffn_norm")
        for f in range(FT + 1):
            if f < FT:
                dve.wait_ge(*reached("ffn_centre", f + 1))
                for tap in range(2):
                    for i in range(2):
                        w = col("ffn_conv_w", tap * 2 * 2 * FT + f + i * FT)
                        y, src = cv[f % 2][i], ps[:, f % 4, i * S:(i + 1) * S]
                        a, b = (slice(1, S), slice(0, S - 1)) if tap == 0 else (slice(0, S - 1), slice(1, S))
                        ins = V.scalar_tensor_tensor(out=y[:, a], in0=src[:, b], scalar=w, in1=y[:, a], op0=ALU.mult,
                                                     op1=ALU.add)
                    if tap == 0:
                        step(ins)
                ins.then_inc(sem("ffn_gated_read"), 1)
            if f >= 1:
                j = f - 1
                dve.wait_ge(*reached("ffn_gated_sigmoid", j + 1))
                dve.wait_ge(*reached("ffn_gated_read", j + 1))
                step(V.tensor_tensor(sg[j % 2], sg[j % 2], cv[j % 2][0], ALU.mult))
                V.tensor_tensor(hid[:, j, :], sg[j % 2], cv[j % 2][1], ALU.mult).then_inc(sem("ffn_hid"), 1)
        residual("ffn_x_change", 9)

        norm("attn_norm_2")
        for i in range(2):
            step(V.tensor_tensor(junk[:, 0:32], row(f"diff_lambda_q{i + 1}_2", 32), row(f"diff_lambda_k{i + 1}_2", 32), ALU.mult))
            V.tensor_reduce(lam4[:, i:i + 1], junk[:, 0:32], AX, ALU.add).then_inc(sem("lam_dots"), 1)
            dve.wait_ge(*reached("lam_dots", i + 1))
        dve.wait_ge(*reached("attn_in_read", 12))
        lists = ((dq, 12, 64, 0, "dil_q_gain_2", 64 ** -0.5), (dk, 12, 64, 24, "dil_k_gain_2", 1.0),
                 (fq, 8, 32, 48, "diff_q_gain_2", 32 ** -0.5), (fk, 8, 32, 64, "diff_k_gain_2", 1.0))
        flat = dsq
        for m, h, w, o, gain, scale in lists:
            n = TT * h
            buf = m[:].rearrange("p t (h c) -> p (t h) c", h=h)
            step(V.tensor_tensor(flat[:, 0:n * w].rearrange("p (a b) -> p a b", a=n), buf, buf, ALU.mult))
            step(V.tensor_reduce(attn_ms[:, o:o + n], flat[:, 0:n * w].rearrange("p (a b) -> p a b", a=n), AX, ALU.add))
            V.tensor_scalar(attn_ms[:, o:o + n], attn_ms[:, o:o + n], 1.0 / (w * scale * scale), EPS / (scale * scale),
                            ALU.mult, ALU.add).then_inc(sem("attn_head_ms"), 1)
        dve.wait_ge(*reached("attn_head_std", 1))
        step(V.reciprocal(attn_ms[:], attn_std[:]))
        for m, h, w, o, gain, scale in lists:
            n = TT * h
            buf = m[:].rearrange("p t (h c) -> p (t h) c", h=h)
            step(V.tensor_tensor(buf, buf, attn_ms[:, o:o + n].unsqueeze(2).to_broadcast([P, n, w]), ALU.mult))
            V.tensor_tensor(buf, buf, row(gain, w).unsqueeze(1).to_broadcast([P, n, w]),
                            ALU.mult).then_inc(sem("attn_heads_normed"), 1)
        dve.wait_ge(*reached("lam_exps", 1))
        step(V.tensor_tensor(lam4[:, 4:5], lam4[:, 3:4], lam4[:, 2:3], ALU.subtract))
        step(V.tensor_scalar(lam4[:, 4:5], lam4[:, 4:5], LAM_INIT, None, ALU.subtract))
        attention("dil")
        nm = att["dil"]["nmax"][:, 0:24].rearrange("p (g x) -> p g x", g=3)
        sm = att["dil"]["sum"][:, 0:24].rearrange("p (g x) -> p g x", g=3)
        al = alpha[:, 0].rearrange("p (g x) -> p g x", g=3)
        a2 = alpha[:, 1].rearrange("p (g x) -> p g x", g=3)
        step(V.tensor_tensor(a2[:, 0], nm[:, 0], nm[:, 1], ALU.min))
        step(V.tensor_tensor(a2[:, 0], a2[:, 0], nm[:, 2], ALU.min))
        V.tensor_tensor(al, a2[:, 0:1].to_broadcast([P, 3, 8]), nm, ALU.subtract).then_inc(sem("alpha_diff"), 1)
        dve.wait_ge(*reached("alpha_exp", 1))
        step(V.tensor_tensor(a2, al, sm, ALU.mult))
        step(V.tensor_tensor(a2[:, 0], a2[:, 0], a2[:, 1], ALU.add))
        step(V.tensor_tensor(a2[:, 0], a2[:, 0], a2[:, 2], ALU.add))
        step(V.reciprocal(a2[:, 0], a2[:, 0]))
        step(V.tensor_tensor(al, al, a2[:, 0:1].to_broadcast([P, 3, 8]), ALU.mult))
        af = alpha[:, 0].rearrange("p (h t) -> p t h", t=TT)
        for t in range(TT):
            o = xn[:, t, 0:768].rearrange("p (h v) -> p h v", v=64)
            ins = V.tensor_tensor(o, o, af[:, t, :].unsqueeze(2).to_broadcast([P, 12, 64]), ALU.mult)
        ins.then_inc(sem("attn_mixed"), 1)
        fo = xn[:, :, 768:1024]
        sqv = dsq[:, 0:512].rearrange("p (a b) -> p a b", a=TT)
        step(V.tensor_tensor(sqv, fo, fo, ALU.mult))
        st = [h[:, 48:56] for h in heads_st]
        step(V.tensor_reduce(st[0], dsq[:, 0:512].rearrange("p (a b) -> p a b", a=8), AX, ALU.add))
        k2 = (1.0 - LAM_INIT) ** 2
        V.tensor_scalar(st[0], st[0], 1.0 / (64 * k2), EPS / k2, ALU.mult, ALU.add).then_inc(sem("diff_ms"), 1)
        dve.wait_ge(*reached("diff_std", 1))
        step(V.reciprocal(st[2], st[1]))
        for t in range(TT):
            o = fo[:, t, :].rearrange("p (h v) -> p h v", v=64)
            step(V.tensor_tensor(o, o, st[2][:, 4 * t:4 * t + 4].unsqueeze(2).to_broadcast([P, 4, 64]), ALU.mult))
            ins = V.tensor_tensor(o, o, row("diff_out_gain_2", 64).unsqueeze(1).to_broadcast([P, 4, 64]), ALU.mult)
        ins.then_inc(sem("attn_mixed"), 1)
        residual("attn_x_change", 5)

        norm("ffn_norm_2")
        for f in range(FT):
            dve.wait_ge(*reached("ffn2_gated_sigmoid", f + 1))
            step(V.tensor_tensor(sg[f % 2], sg[f % 2], ps[:, f % 4, 0:S], ALU.mult))
            V.tensor_tensor(hid[:, f, :], sg[f % 2], ps[:, f % 4, S:2 * S], ALU.mult).then_inc(sem("ffn2_gated_read"), 1)
        residual("ffn2_x_change", 9)

        V.tensor_tensor(lbs["d"], col("hgrn_lb_logits_2", 8, 8), col("hgrn_lb_logits_2", 0, 8),
                        ALU.subtract).then_inc(sem("lb_diff"), 1)
        norm("hgrn_norm_2")
        for g in range(8):
            dve.wait_ge(*reached("hgrn_q_sigmoid", g + 1))
            V.tensor_tensor(gq[:, g, :], gq[:, g, :], ps[:, g, 0:S], ALU.mult).then_inc(sem("hgrn_q_read"), 1)
        dve.wait_ge(*reached("lb", 1))
        for g in range(8):
            dve.wait_ge(*reached("hgrn_in_read", g + 1))
            V.tensor_scalar(gB[:, g, :], gB[:, g, :], lbs["one_minus"][:, g:g + 1], lbs["lb"][:, g:g + 1], ALU.mult, ALU.add)
            ins = V.tensor_scalar(gk[:, g, :], gk[:, g, :], lbs["one_minus"][:, g:g + 1], None, ALU.mult)
        step(ins)
        V.sem_inc(sem("hgrn_forget"), 1)
        dve.wait_ge(*reached("hgrn_in_read", 16))
        dve.wait_ge(*reached("hgrn_logf", 1))
        V.memset(AT[:], 0.0)
        for h in range(HG_HEADS):
            ins = V.tensor_tensor_scan(gB[:, h, :], const("reset", S), gB[:, h, :], 0.0, ALU.mult, ALU.add)
        step(ins)

        def chunks(v):
            return v.rearrange("p h (c j) -> p (h c) j", j=CHUNK)

        causal = const("chunk_causal", P).bitcast(U32)
        for half in range(2):
            hs = slice(4 * half, 4 * half + 4)
            b16 = chunks(gB[:, hs, :])
            if half == 1:
                dve.wait_ge(*reached("hgrn_factors", 4))
            V.tensor_tensor(chunks(gD[:]), b16, b16[:, :, CHUNK // 2:CHUNK // 2 + 1].to_broadcast([P, 16, CHUNK]),
                            ALU.subtract).then_inc(sem("hgrn_d1"), 1)
            dve.wait_ge(*reached("hgrn_eq", 4 * half + 1))
            V.tensor_tensor(gQ[:], gQ[:], gq[:, hs, :], ALU.mult).then_inc(sem("hgrn_factors"), 1)
            dve.wait_ge(*reached("hgrn_eq", 4 * half + 2))
            V.tensor_tensor(gK[:], gK[:], gk[:, hs, :], ALU.mult).then_inc(sem("hgrn_factors"), 1)
            dve.wait_ge(*reached("hgrn_factors", 4 * half + 2))
            dve.wait_ge(*reached("hgrn_eq", 4 * half + 3))
            V.tensor_tensor(gq[:, hs, :], gq[:, hs, :], gD[:], ALU.mult).then_inc(sem("hgrn_factors"), 1)
            dve.wait_ge(*reached("hgrn_factors", 4 * half + 3))
            V.tensor_tensor(chunks(gD[:]), b16[:, :, CHUNK - 1:CHUNK].to_broadcast([P, 16, CHUNK]), b16,
                            ALU.subtract).then_inc(sem("hgrn_d2"), 1)
            dve.wait_ge(*reached("hgrn_eq", 4 * half + 4))
            V.tensor_tensor(gk[:, hs, :], gk[:, hs, :], gD[:], ALU.mult).then_inc(sem("hgrn_factors"), 1)
            dve.wait_ge(*reached("hgrn_scores", half + 1))
            for h in range(4):
                ins = V.copy_predicated(AT[:, 4 * half + h, :], causal, ps[:, 0, h * P:(h + 1) * P])
            ins.then_inc(sem("hgrn_masked"), 1)
            dve.wait_ge(*reached("hgrn_dec", half + 1))
            for c in range(3):
                for h in range(4):
                    dve.wait_ge(*reached("hgrn_kv", 12 * half + 4 * c + h + 1))
                    kv = ps[:, (3, 6, 7, 0)[h], 0:P]
                    if c == 0:
                        if half == 1:
                            dve.wait_ge(*reached("hgrn_o", 16))
                        V.tensor_copy(state[:, h, :], kv).then_inc(sem("hgrn_state"), 1)
                    else:
                        dve.wait_ge(*reached("hgrn_o", 16 * half + 4 * c + h + 1))
                        dve.wait_ge(*reached("hgrn_state", 12 * half + 4 * (c - 1) + h + 1))
                        V.scalar_tensor_tensor(out=state[:, h, :], in0=state[:, h, :], scalar=dec[:, 16 * half + 4 * h + c:16 * half + 4 * h + c + 1],
                                               in1=kv, op0=ALU.mult, op1=ALU.add).then_inc(sem("hgrn_state"), 1)
        dve.wait_ge(*reached("hgrn_o_copied", 4))
        o16 = xn[:].rearrange("p t (h v) -> p (t h) v", v=P)
        sqg = work[:, 0:2048].rearrange("p (a b) -> p a b", a=16)
        step(V.tensor_tensor(sqg, o16, o16, ALU.mult))
        st = [h[:, 0:16] for h in heads_st]
        step(V.tensor_reduce(st[0], sqg, AX, ALU.add))
        V.tensor_scalar(st[0], st[0], 1.0 / P, EPS, ALU.mult, ALU.add).then_inc(sem("hgrn_ms"), 1)
        dve.wait_ge(*reached("hgrn_std", 1))
        step(V.reciprocal(st[2], st[1]))
        step(V.tensor_tensor(o16, o16, st[2].unsqueeze(2).to_broadcast([P, 16, P]), ALU.mult))
        step(V.tensor_tensor(o16, o16, row("hgrn_out_gain_2", P).unsqueeze(1).to_broadcast([P, 16, P]), ALU.mult))
        V.tensor_tensor(xn[:], xn[:], gg[:], ALU.mult).then_inc(sem("hgrn_gated"), 1)
        residual("hgrn_x_change", 5)

        norm("moe_norm_2")
        L, rank, s1, s2, tmp = (rt[:, i] for i in range(5))
        dve.wait_ge(*reached("logits", 1))
        step(V.tensor_copy(L, ps[:, 7, 0:TT * NE].rearrange("p (t e) -> p t e", t=TT)))
        V.sem_inc(sem("logits_read"), 1)
        g3 = [r[:].rearrange("p (t e j) -> p t e j", t=TT, e=NE) for r in rcmp]
        full = [P, TT, NE, NE]
        step(V.tensor_tensor(g3[0], L.unsqueeze(2).to_broadcast(full), L.unsqueeze(3).to_broadcast(full), ALU.is_gt))
        step(V.tensor_tensor(g3[1], L.unsqueeze(2).to_broadcast(full), L.unsqueeze(3).to_broadcast(full), ALU.is_equal))
        tie = const("tie", NE * NE)
        for t in range(TT):
            step(V.tensor_tensor(rcmp[1][:, t * 64:(t + 1) * 64], rcmp[1][:, t * 64:(t + 1) * 64], tie, ALU.mult))
        step(V.tensor_tensor(g3[0], g3[0], g3[1], ALU.add))
        step(V.tensor_reduce(rank, g3[0], AX, ALU.add))
        for s, r, v in ((s1, 0.0, "v1"), (s2, 1.0, "v2")):
            step(V.tensor_scalar(s, rank, r, None, ALU.is_equal))
            step(V.tensor_tensor(tmp, s, L, ALU.mult))
            step(V.tensor_reduce(rtv[v], tmp, AX, ALU.add))
        V.tensor_tensor(rtv["v2"], rtv["v2"], rtv["v1"], ALU.subtract).then_inc(sem("route_diff"), 1)
        dve.wait_ge(*reached("route_exp", 1))
        step(V.tensor_scalar(rtv["w1"], rtv["ex"], 1.0, None, ALU.add))
        step(V.reciprocal(rtv["w1"], rtv["w1"]))
        step(V.tensor_tensor(rtv["w2"], rtv["w1"], rtv["ex"], ALU.mult))
        for t in range(TT):
            step(V.tensor_scalar(tmp[:, t, :], s1[:, t, :], rtv["w1"][:, t:t + 1], None, ALU.mult))
            step(V.scalar_tensor_tensor(out=gates[:, :, t], in0=s2[:, t, :], scalar=rtv["w2"][:, t:t + 1], in1=tmp[:, t, :],
                                        op0=ALU.mult, op1=ALU.add))
        V.sem_inc(sem("expert_hid"), 4)
        V.sem_inc(sem("expert_out_free"), 4)
        with nc.vector.Fori(0, NE) as e:
            for i in range(4 * ECH):
                dve.wait_ge(*reached("expert_sigmoid", e * (4 * ECH) + i + 1))
                b = i % 4
                if i % 4 == 0 and i >= 8:
                    dve.wait_ge(*reached("expert_down", e * ECH + (i // 4 - 1)))
                V.tensor_tensor(esg[b], esg[b], ps[:, b, 0:S], ALU.mult).then_inc(sem("expert_gated"), 1)
                dve.wait_ge(*reached("expert_gated", e * (4 * ECH) + i + 1))
                V.tensor_tensor(ehid[(i // 4) % 2][:, b, :], esg[b], ps[:, b, S:2 * S], ALU.mult).then_inc(sem("expert_hid"), 1)
            dve.wait_ge(*reached("expert_down", (e + 1) * ECH))
            for t in range(TT):
                for h in range(2):
                    xs = x[:, t, h * HALF:(h + 1) * HALF]
                    V.scalar_tensor_tensor(out=xs, in0=ps[:, 4 + 2 * t + h, :], scalar=gates[:, bass.ds(e, 1), t],
                                           in1=xs, op0=ALU.mult, op1=ALU.add).then_inc(sem("expert_out_free"), 1)
            dve.wait_ge(*reached("expert_out_free", (e + 2) * 4))
        V.sem_inc(sem("x_final"), 4)

    block_cm.__exit__(None, None, None)


def constants():
    c = np.zeros((P, N_CONST), np.float32)

    def put(name, v):
        v = np.asarray(v, np.float32).reshape(P, -1)
        c[:, CONST[name]:CONST[name] + v.shape[1]] = v

    p = np.arange(P)
    put("ident", np.eye(P))
    put("ones", np.ones((P, P)))
    put("inv_freq", np.broadcast_to(10000.0 ** (-np.arange(0, ROPE, 2) / ROPE), (P, ROPE // 2)))
    put("reset", np.broadcast_to(np.arange(S) % CHUNK != 0, (P, S)))
    put("chunk_causal", (p[:, None] % CHUNK) <= (p[None, :] % CHUNK))
    put("tie", np.broadcast_to((np.arange(NE)[None, :] < np.arange(NE)[:, None]).reshape(1, -1), (P, NE * NE)))
    dist = []
    for window, dilation in ((128, 1), (512, 4), (2048, 16), (S, 1)):
        for t in range(TT):
            gap = (t * P + p)[:, None] - np.arange(P * (t + 1))[None, :]
            dist.append(np.where((gap >= 0) & (gap % dilation == 0) & (gap <= window), gap, FAR))
    put("dist", np.concatenate(dist, axis=1))
    return c


def by_feature(v, n):
    return np.moveaxis(np.asarray(v, np.float32).reshape(-1, n, P), 2, 0).reshape(P, -1)


def k_tiles(w):
    k, n = w.shape
    return w.reshape(k // P, P, n).transpose(1, 0, 2).reshape(P, -1)


def lay_out(a):
    f = {k: np.asarray(v) for k, v in a.items()}
    cols = np.zeros((P, N_COLS), np.float32)
    for name in COLS:
        v = f[name]
        n = {"ffn_conv_w": 2 * FT, "ffn_conv_b": 2 * FT}.get(name, v.shape[-1] // P)
        if name == "moe_w_router_2":
            m = k_tiles(v[0])
        else:
            m = by_feature(v, n)
        cols[:, COLS[name]:COLS[name] + m.shape[1]] = m
    rows = np.zeros((1, N_ROWS), np.float32)
    for name in ROWS:
        rows[0, ROWS[name]:ROWS[name] + f[name].size] = f[name].reshape(-1)

    slabs = np.zeros((N_SLABS, P, SLAB), np.float32)

    def put(n, m, at=0):
        slabs[n, :, at:at + m.shape[1]] = m

    def by_columns(name, w, width=HALF):
        for j in range(0, w.shape[1], width):
            put(SLABS[name] + j // width, k_tiles(w[:, j:j + width]))

    def by_rows(name, w):
        for j in range(0, w.shape[0], HALF):
            put(SLABS[name] + j // HALF, k_tiles(w[j:j + HALF]))

    w_in = f["w_in"][0]
    by_columns("w_in", w_in[:, 0:2 * LRU_W])
    put(SLABS["w_in"] + 2, k_tiles(w_in[:, 2 * LRU_W:]))
    gates = np.zeros((P, 2, 2, LC, P), np.float32)
    for i, name in enumerate(("lru_w_a", "lru_w_i")):
        w = f[name][0]
        for d in range(2):
            for c in range(LC):
                for b in range(2):
                    gates[64 * b:64 * b + 64, d, i, c, 64 * b:64 * b + 64] = w[d, 2 * c + b]
    put(SLABS["lru_gates_uq"], gates.reshape(P, -1))
    put(SLABS["lru_gates_uq"], k_tiles(f["w_uq"][0]), 2048)
    put(SLABS["w_ukv"], k_tiles(f["w_ukv"][0]))
    by_rows("w_out", f["w_out"][0])
    by_columns("w_mem_kv", f["w_mem_kv"][0])
    by_columns("w_mem_q", f["w_mem_q"][0])
    by_rows("w_mem_o", f["w_mem_o"][0])
    w_up = f["w_up"][0]
    for name, gate, up in (("w_up", w_up[:, :D_FF], w_up[:, D_FF:]),
                           ("ffn_gate_up", f["ffn_w_gate_2"][0], f["ffn_w_up_2"][0])):
        for j in range(FT // 2):
            cut = slice(2 * P * j, 2 * P * (j + 1))
            put(SLABS[name] + j, k_tiles(np.concatenate([gate[:, cut], up[:, cut]], axis=1)))
    by_rows("w_down", f["w_down"][0])
    by_columns("attn_w_in", f["attn_w_in_2"][0])
    by_rows("attn_w_out", f["attn_w_out_2"][0])
    by_rows("ffn_w_down", f["ffn_w_down_2"][0])
    by_columns("hgrn_w_in", f["hgrn_w_in_2"][0])
    by_rows("hgrn_w_out", f["hgrn_w_out_2"][0])
    for e in range(NE):
        at = N_FIXED + e * E_SLABS
        for c in range(ECH):
            cut = slice(c * HALF, (c + 1) * HALF)
            put(at + 3 * c, k_tiles(f["moe_w_gate_2"][0, e][:, cut]))
            put(at + 3 * c + 1, k_tiles(f["moe_w_up_2"][0, e][:, cut]))
            put(at + 3 * c + 2, k_tiles(f["moe_w_down_2"][0, e][cut]))

    def token_major(v):
        return np.ascontiguousarray(v.reshape(TT, P, -1).transpose(1, 0, 2))

    return {"slabs": slabs, "consts": constants(), "cols": cols, "rows": rows, "x": token_major(f["x"]),
            "mem": token_major(f["mem"]),
            "pos": np.ascontiguousarray(f["positions"].reshape(TT, P).T.astype(np.int32))}


def kernel(**inputs):
    import concourse.bacc as bacc
    from concourse.bass_utils import run_bass_kernel_spmd

    nc = bacc.Bacc("TRN2", target_bir_lowering=False, num_devices=1)
    arrays = lay_out(inputs)
    args = [nc.dram_tensor("in_" + name, a.shape, mybir.dt.from_np(a.dtype), kind="ExternalInput").ap()
            for name, a in arrays.items()]
    out = nc.dram_tensor("out", (P, TT, D), F32, kind="ExternalOutput").ap()
    build(nc, *args, out)
    r = run_bass_kernel_spmd(nc, [{"in_" + name: a for name, a in arrays.items()}], core_ids=[0])
    got = r.results[0]["out"]
    return np.ascontiguousarray(got.transpose(1, 0, 2)).reshape(1, S, D)
```

```python
import math

import numpy as np

import concourse.bass as bass
from concourse import mybir

F32 = mybir.dt.float32
I32 = mybir.dt.int32
U32 = mybir.dt.uint32
ALU = mybir.AluOpType
ACT = mybir.ActivationFunctionType
AX = mybir.AxisListType.X

P = 128
S = 256
WORK = 13312
TT = S // P
D = 1024
KD = D // P
EPS = 1e-6
HALF = 512
UNIT = 2048
RAW = 7
SPLIT = 3

LRU_W = 512
LC = LRU_W // P
Q_LORA, KV_LORA, ROPE = 256, 128, 32
HEADS, NOPE, QK, VD = 8, 64, 96, 64
TAIL = Q_LORA + KV_LORA + ROPE
D_FF = 2816
FT = D_FF // P
MEM_HEADS = 4
DIL_HEADS = 12
DIFF_HEADS = 4
HG_HEADS, CHUNK = 8, 64
NE, FE = 8, 3584
ECH = FE // HALF
E_UNITS = 6 * ECH
LAM_INIT = 0.8 - 0.6 * math.exp(-0.3 * 0)
FAR = 1.0e32


def offsets(sizes):
    at, out = 0, {}
    for name, n in sizes:
        out[name] = at
        at += n
    return out, at


CONST, N_CONST = offsets([("ident", P), ("ones", P), ("inv_freq", ROPE // 2), ("reset", S),
                          ("chunk_causal", P), ("tie", NE * NE), ("slot", P), ("before", P), ("dist", 4 * (P + S))])
COLS, N_COLS = offsets([("attn_norm", KD), ("mem_attn_norm", KD), ("mem_norm", KD), ("ffn_norm", KD),
                        ("attn_norm_2", KD), ("ffn_norm_2", KD), ("hgrn_norm_2", KD), ("moe_norm_2", KD),
                        ("q_a_norm", 2), ("kv_a_norm", 1), ("lru_out_norm", LC), ("mla_out_norm", LC),
                        ("mem_q_norm", 1), ("mem_k_norm", 1), ("lru_conv_w", 8 * LC), ("lru_conv_b", 2 * LC),
                        ("lru_b_a", 2 * LC), ("lru_b_i", 2 * LC), ("lru_lambda", 2 * LC),
                        ("ffn_conv_w", 3 * 2 * FT), ("ffn_conv_b", 2 * FT), ("hgrn_lb_logits_2", 2 * HG_HEADS),
                        ("moe_w_router_2", KD * NE), ("dil_q_gain_2", 1), ("dil_k_gain_2", 1), ("diff_q_gain_2", 1),
                        ("diff_k_gain_2", 1)])
ROWS, N_ROWS = offsets([("mla_q_norm", QK), ("mla_k_norm", QK), ("diff_lambda_q1_2", 32),
                        ("diff_lambda_k1_2", 32), ("diff_lambda_q2_2", 32), ("diff_lambda_k2_2", 32),
                        ("diff_out_gain_2", 64), ("hgrn_out_gain_2", 128)])
F32R = mybir.dt.float32r

UNITS_AT, N_FIXED = offsets([("w_in", 4), ("w_in_tail", 2), ("w_uq", 1), ("w_ukv", 1), ("w_out", 4), ("w_mem_kv", 4),
                             ("w_mem_q", 2), ("w_mem_o", 2), ("w_up", FT), ("w_down", FT // 2), ("attn_w_in", 12),
                             ("attn_w_out", 4), ("ffn_gate_up", FT), ("ffn_w_down", FT // 2), ("hgrn_w_in", 16),
                             ("hgrn_w_out", 4)])
N_UNITS = N_FIXED + NE * E_UNITS
FIRST_RAW = N_FIXED % RAW
assert E_UNITS % RAW == 0 and E_UNITS % SPLIT == 0
EXPERT_ORDER = []
for _c in range(ECH + 1):
    if _c < ECH:
        EXPERT_ORDER += [("gate", _c, 0), ("gate", _c, 1), ("up", _c, 0), ("up", _c, 1)]
    if _c > 0:
        EXPERT_ORDER += [("down", _c - 1, 0), ("down", _c - 1, 1)]
UNIT_OF = {u: j for j, u in enumerate(EXPERT_ORDER)}
DIL_SLOPES = [2.0 ** (-8.0 * (h + 1) / 16) for h in range(16)]
NORMS = ["attn_norm", "mem_attn_norm", "mem_norm", "ffn_norm", "attn_norm_2", "ffn_norm_2", "hgrn_norm_2", "moe_norm_2"]


def build(nc, units_d, consts_d, cols_d, rows_d, moe_gain_d, lru_w_d, x_d, mem_d, pos_d, out_d):
    def sb(name, shape, dt=F32):
        return nc.alloc_sbuf_tensor(name, [P] + shape, dt)

    raw = sb("raw", [RAW, UNIT])
    wh = sb("wh", [SPLIT, UNIT], F32R)
    wl = sb("wl", [SPLIT, UNIT], F32R)
    x = sb("x", [TT, D])
    hT_at = nc.sbuf_base
    hTh = sb("hTh", [KD, S], F32R)
    hTl = sb("hTl", [KD, S], F32R)
    hP = nc.alloc_sbuf_tensor_at("hP", [P, KD, S], F32, offset=hT_at)
    xn = sb("xn", [TT, D])
    junk = sb("junk", [HALF])
    consts = sb("consts", [N_CONST])
    cols = sb("cols", [N_COLS])
    rows = sb("rows", [N_ROWS])
    pos = sb("pos", [TT], I32)
    small = sb("small", [416])
    work_at = nc.sbuf_base
    work = sb("work", [WORK])
    work_r = nc.alloc_sbuf_tensor_at("work_r", [P, WORK], F32R, offset=work_at)
    work_b = nc.alloc_sbuf_tensor_at("work_b", [P, 2 * WORK], mybir.dt.bfloat16, offset=work_at)
    ps = nc.alloc_psum_tensor("ps", [P, 8, HALF], F32)

    taken = [0]

    def tiny(n):
        taken[0] += n
        assert taken[0] <= 416
        return small[:, taken[0] - n:taken[0]]

    def area(at, *shape, of=None):
        n = int(np.prod(shape))
        assert at + n <= WORK
        v = (work if of is None else of)[:, at:at + n]
        if len(shape) == 2:
            v = v.rearrange("p (a b) -> p a b", a=shape[0])
        if len(shape) == 3:
            v = v.rearrange("p (a b c) -> p a b c", a=shape[0], b=shape[1])
        return v

    def const(name, n, at=0):
        return consts[:, CONST[name] + at:CONST[name] + at + n]

    def col(name, c, n=1):
        return cols[:, COLS[name] + c:COLS[name] + c + n]

    def row(name, n):
        return rows[:, ROWS[name]:ROWS[name] + n]

    ident = const("ident", P)
    ones = const("ones", P)

    sems = {}

    SHARED = {
        "oT_hi": dict(mla=4, mem=2, attn=4, hgrn=4), "hid_hi": dict(ffn=FT, ffn2=FT), "hid": dict(ffn=FT, ffn2=FT),
        "att_scores": (16, 8, 40), "att_max": (16, 8, 40), "att_probs": (16, 8, 40),
        "att_transposed": (16, 8, 40), "att_probsT": (16, 8, 40), "att_weighted": (16, 8, 40), "att_out": (16, 8, 40),
        "qkT_ps": dict(mla=8, mem=4, attn=8), "qkT": dict(mla=8, mem=8, attn=8),
        "oT_ps": dict(mla=2, mem=2, attn=4, hgrn=4), "oT": dict(mla=4, mem=2, attn=4, hgrn=4),
        "x_change": dict(mixer=7, memory=5, ffn=14, attn=7, ffn2=14, hgrn=7),
        "ms": dict(lru=1, latent=1, mla_head=2, mla=1, mem_head=2, attn_head=4, diff=1, hgrn=1),
        "std": dict(lru=1, latent=1, mla_head=2, mla=1, mem_head=2, attn_head=4, diff=1, hgrn=1),
        "gu": dict(ffn=FT, ffn2=FT), "gated_sigmoid": dict(ffn=FT, ffn2=FT), "gated_read": dict(ffn=FT, ffn2=FT),
    }
    place = {}
    for shared, parts in SHARED.items():
        start = 0
        for stage, n in (parts.items() if isinstance(parts, dict) else zip(("mla", "mem", "dil"), parts)):
            place[stage + "_" + shared] = (shared, start)
            start += n

    def sem(name):
        shared = place.get(name, (name, 0))[0]
        if shared not in sems:
            sems[shared] = nc.alloc_semaphore(shared)
        return sems[shared]

    def reached(name, value):
        return sem(name), value + place.get(name, (name, 0))[1]

    def tile_of(name, i):
        return reached(name, 3 * (i // TT) + 2 + i % TT)

    raw_loaded = [sem(f"raw_loaded{i}") for i in range(RAW)]
    released = {}

    tail = area(0, TT, TAIL)
    xrp = area(832, LC, S + 6)
    yg = area(1880, LC, S)
    xc = [area(2904 + 1024 * d, LC, S) for d in range(2)]
    ra = [area(4952 + 1024 * d, LC, S) for d in range(2)]
    ri = [area(7000 + 1024 * d, LC, S) for d in range(2)]
    th = [area(9048 + 1024 * d, LC, S) for d in range(2)]
    z = xrp.rearrange("p a b -> p (a b)")[:, 0:1024].rearrange("p (a b) -> p a b", a=4)
    root = [hP[:, 4 * d:4 * d + 4, :] for d in range(2)]
    mq = area(832, 2 * HEADS, QK)
    mk = area(2368, 2 * HEADS, QK)
    mv = area(3904, TT, HEADS * VD)
    mqT = area(4928, HEADS, S)
    mkT = area(6976, HEADS, S)
    msq = area(4928, 2 * HEADS, QK)
    mo = area(9024, TT, HEADS * VD)
    cn = area(11616, TT, 384)
    cTh, cTl = area(10080, 3, S, of=work_r), area(10848, 3, S, of=work_r)
    lru_w = area(11264, 16, P)
    mem = area(0, TT, D)
    memTh, memTl = area(2048, KD, S, of=work_r), area(10240, KD, S, of=work_r)
    eq, ek, ev = area(4096, TT, HALF), area(5120, TT, HALF), area(6144, TT, HALF)
    eqT, ekT = area(7168, MEM_HEADS, S), area(8192, MEM_HEADS, S)
    eo = area(9216, TT, HALF)
    esq = area(11776, TT, HALF)
    hidh, hidl = area(0, FT, S, of=work_r), area(5632, FT, S, of=work_r)
    cv = [[xn[:, b // 2, 512 * (b % 2) + 256 * i:512 * (b % 2) + 256 * (i + 1)] for i in range(2)] for b in range(4)]
    sg = [area(12288 + 256 * b, S) for b in range(4)]
    dq, dk, dv = area(0, TT, 768), area(1536, TT, 768), area(3072, TT, 768)
    fq, fk, fv = area(4608, TT, 256), area(5120, TT, 256), area(5632, TT, 256)
    dqT, dkT, fqT, fkT = area(6144, 6, S), area(7680, 6, S), area(9216, 2, S), area(9728, 2, S)
    dsq = area(11776, 1536)
    gq, gk, gB = area(0, HG_HEADS, S), area(2048, HG_HEADS, S), area(4096, HG_HEADS, S)
    gv, gg = area(6144, TT, D), area(8192, TT, D)
    gD, gQ, gK = area(10240, 4, S), area(11264, 4, S), area(12288, 4, S)
    kstT = hP[:, 0:4, :]
    AT = hP[:, 4:8, :].rearrange("p a b -> p (a b)").rearrange("p (h c) -> p h c", h=8)
    state = junk[:, 0:512].rearrange("p (h v) -> p h v", h=4)
    moe_gain = area(4096, D)
    parts = [work_b[:, 2048 * i:2048 * (i + 1)].rearrange("p (t d) -> p t d", t=TT) for i in range(3)]
    xeh, xel = area(4096, KD, P, of=work_r), area(5120, KD, P, of=work_r)
    ehh = [area(8192 + 512 * b, 4, P, of=work_r) for b in range(2)]
    ehl = [area(9216 + 512 * b, 4, P, of=work_r) for b in range(2)]
    eh = [area(10240 + 512 * b, HALF) for b in range(2)]
    esg = area(11264, HALF)
    y_e = area(11776, D)
    GT = area(12800, TT, P)
    G = work_b[:, 2 * 13056:2 * 13056 + TT * P].rearrange("p (t s) -> p t s", t=TT)
    Gw = junk[:, 0:256].rearrange("p (t s) -> p t s", t=TT)
    slot = const("slot", P)

    block_cm = nc.Block()
    block = block_cm.__enter__()

    ssq, msum, std, rstd = tiny(16), tiny(16), tiny(16), tiny(16)
    n_ssq = {}

    NORM_OF = {n: i for i, n in enumerate(NORMS)}
    X_AFTER = {"mixer": 4, "memory": 8, "ffn": 12, "attn2": 16, "ffn2": 20, "hgrn": 24}
    NORM_NEEDS = {"mem_attn_norm": 4, "ffn_norm": 8, "attn_norm_2": 12, "ffn_norm_2": 16, "hgrn_norm_2": 20,
                  "moe_norm_2": 24}

    def attention_units(stage):
        out = []
        if stage == "mla":
            for h in range(HEADS):
                for t in range(TT):
                    out.append(dict(q=mqT[0:QK, h, t * P:(t + 1) * P], k=mkT[0:QK, h, :], nk=S, dv=VD,
                                    v=[mv[:, j, h * VD:(h + 1) * VD] for j in range(2)], dist=None,
                                    out=mo[:, t, h * VD:(h + 1) * VD], kind="plain"))
        if stage == "mem":
            for h in range(MEM_HEADS):
                for t in range(TT):
                    out.append(dict(q=eqT[:, h, t * P:(t + 1) * P], k=ekT[:, h, :], nk=S, dv=P,
                                    v=[ev[:, j, h * P:(h + 1) * P] for j in range(2)], dist=None,
                                    out=eo[:, t, h * P:(h + 1) * P], kind="plain"))
        if stage == "dil":
            for h in range(DIL_HEADS):
                for t in range(TT):
                    b = 64 * (h % 2)
                    nk = P * (t + 1)
                    g = h // 4
                    out.append(dict(q=dqT[b:b + 64, h // 2, t * P:(t + 1) * P], k=dkT[b:b + 64, h // 2, 0:nk], nk=nk,
                                    dv=64, v=[dv[:, j, h * 64:(h + 1) * 64] for j in range(t + 1)],
                                    dist=const("dist", nk, g * (P + S) + t * P), slope=DIL_SLOPES[h],
                                    out=xn[:, t, h * 64:(h + 1) * 64], kind="raw"))
            for h in range(DIFF_HEADS):
                for t in range(TT):
                    for c in range(2):
                        b = 32 * ((2 * h + c) % 4)
                        a = (2 * h + c) // 4
                        nk = P * (t + 1)
                        out.append(dict(q=fqT[b:b + 32, a, t * P:(t + 1) * P], k=fkT[b:b + 32, a, 0:nk], nk=nk,
                                        dv=64, v=[fv[:, j, h * 64:(h + 1) * 64] for j in range(t + 1)],
                                        dist=const("dist", nk, 3 * (P + S) + t * P), slope=DIL_SLOPES[DIL_HEADS + h],
                                        out=xn[:, t, 768 + h * 64:768 + (h + 1) * 64],
                                        kind="plain" if c == 0 else "minus"))
        return out

    UNITS = {s: attention_units(s) for s in ("mla", "mem", "dil")}
    ATT_AT = {"mla": 10048, "mem": 10240, "dil": 10240}
    att = {}
    for s, at in ATT_AT.items():
        n = len(UNITS[s])
        att[s] = dict(s=[area(at + 256 * b, S) for b in range(2)], p=[area(at + 512 + 256 * b, S) for b in range(2)],
                      pT=[area(at + 1024 + 256 * b, S) for b in range(2)],
                      nmax=tiny(n), sum=tiny(n), inv=tiny(n))

    lam4 = tiny(8)
    warm = tiny(1)
    mla_gain = tiny(2)
    sp = {k: tiny(8) for k in ("a", "b", "c", "s", "s2", "p", "out")}
    lat = {k: tiny(4) for k in ("ssq", "ms", "std", "r")}
    osq = {k: tiny(2) for k in ("ssq", "ms", "std", "r")}
    heads_st = [sb(f"heads_st{i}", [64]) for i in range(3)]
    rope = {k: area(13120 + 32 * i, TT, ROPE // 2) for i, k in enumerate(("ang", "k", "r", "sin", "cos", "tmp"))}
    lbs = {k: tiny(8) for k in ("d", "lb", "one_minus")}
    dec = tiny(32)
    attn_ms, attn_std = junk[:, 128:208], junk[:, 208:288]
    rh, rl = sb("rh", [KD * NE], F32R), sb("rl", [KD * NE], F32R)
    alpha = sb("alpha", [2, 24])
    rt = junk[:, 324:404].rearrange("p (i t e) -> p i t e", i=5, t=TT)
    rcmp = [area(12288 + 128 * i, TT * NE * NE) for i in range(2)]
    gates = junk[:, 256:290].rearrange("p (e t) -> p e t", t=TT)
    slots = junk[:, 290:324].rearrange("p (e t) -> p e t", t=TT)
    over = sb("over", [1], I32)
    logitsT = work[0:NE, 12288 + 2 * TT * NE * NE:12288 + 2 * TT * NE * NE + S]
    xsel = rcmp[1][:, 0:TT * NE].rearrange("p (t e) -> p t e", t=TT)
    rtv = {k: tiny(2) for k in ("v1", "v2", "ex", "w1", "w2")}
    posf = tiny(2)

    counts = {}

    def counted(ins, name, by=1):
        counts[name] = counts.get(name, 0) + by
        ins.then_inc(sem(name), by)

    @block.tensor
    def _(pe):
        def unit(n):
            pe.wait_ge(sem("lo_made"), n + 1)
            return wh[:, n % SPLIT, :], wl[:, n % SPLIT, :]

        def release(n, name):
            released[n] = reached(name, counts[name])

        def split_product(out, terms, first=True, last=True, ready=None):
            for j, (sh, sl, mh, ml) in enumerate(terms):
                if ready is not None:
                    ready(j)
                nc.tensor.matmul(out, sh, mh, start=(first and j == 0), stop=False)
                nc.tensor.matmul(out, sh, ml, start=False, stop=False)
                ins = nc.tensor.matmul(out, sl, mh, start=False, stop=(last and j == len(terms) - 1))
            return ins

        def by_k(w, k, n):
            return [p[:, 0:k * n].rearrange("p (k n) -> p k n", k=k) for p in w]

        def accumulate(out, pairs, first=True, last=True):
            for j, (l, r) in enumerate(pairs):
                ins = nc.tensor.matmul(out, l, r, start=(first and j == 0), stop=(last and j == len(pairs) - 1))
            return ins

        fresh = [0, 0]

        def norm(name):
            i = NORM_OF[name]
            pe.wait_ge(*reached("norm_xn", TT * (i + 1)))
            if i == 0:
                pe.wait_ge(*reached("params", 16 * 3))
            for g in range(4):
                for c2 in range(2):
                    for t in range(TT):
                        c = 2 * g + c2
                        ins = nc.tensor.transpose(ps[:, g, c2 * S + t * P:c2 * S + (t + 1) * P],
                                                  xn[:, t, c * P:(c + 1) * P], ident)
                counted(ins, "norm_transposed")
            fresh[:] = [i, 0]

        def tile_ready(k):
            i, done = fresh
            if k >= done:
                fresh[1] = 2 * (k // 2) + 2
                pe.wait_ge(*reached("norm_out", KD * i + fresh[1]))

        def attention(stage):
            units = UNITS[stage]
            a = att[stage]
            n = len(units)
            for i in range(n + 2):
                if i < n:
                    u = units[i]
                    if i >= 2:
                        pe.wait_ge(*reached(stage + "_att_probs", i - 1))
                    counted(accumulate(ps[:, i % 2, 0:u["nk"]], [(u["q"], u["k"])]), stage + "_att_scores")
                j = i - 1
                if 0 <= j < n:
                    u = units[j]
                    pe.wait_ge(*reached(stage + "_att_probs", j + 1))
                    if j >= 2:
                        pe.wait_ge(*reached(stage + "_att_probsT", j - 1))
                    for b in range(u["nk"] // P):
                        ins = nc.tensor.transpose(ps[:, 2 + j % 2, b * P:(b + 1) * P], a["p"][j % 2][:, b * P:(b + 1) * P],
                                                  ident)
                    counted(ins, stage + "_att_transposed")
                j = i - 2
                if 0 <= j < n:
                    u = units[j]
                    pe.wait_ge(*reached(stage + "_att_probsT", j + 1))
                    if j >= 2:
                        pe.wait_ge(*reached(stage + "_att_out", j - 1))
                    counted(accumulate(ps[:, 4 + j % 2, 0:u["dv"]],
                                       [(a["pT"][j % 2][:, b * P:(b + 1) * P], u["v"][b]) for b in range(u["nk"] // P)]),
                            stage + "_att_weighted")

        def project_out(stage, n0, nk, inh, inl, ready):
            for n in range(nk // 2):
                w = by_k(unit(n0 + n), 2, D)
                last = n == nk // 2 - 1
                ready(2 * n + 1)
                for t in range(TT):
                    for h in range(2):
                        ts, hs = slice(t * P, (t + 1) * P), slice(h * HALF, (h + 1) * HALF)
                        ins = split_product(ps[:, 4 + 2 * t + h, :],
                                            [(inh[:, 2 * n + k, ts], inl[:, 2 * n + k, ts], w[0][:, k, hs], w[1][:, k, hs])
                                             for k in range(2)], first=(n == 0), last=last)
                        if last or h == 1 and t == 1:
                            counted(ins, stage)
                release(n0 + n, stage)

        def feature_major(out, w, c):
            cs = slice(c * P, (c + 1) * P)
            return split_product(out, [(w[0][:, k, cs], w[1][:, k, cs], hTh[:, k, :], hTl[:, k, :]) for k in range(KD)],
                                 ready=tile_ready)

        def token_major(name, n0, srch, srcl, banks, width=HALF):
            for half in range(2):
                w = by_k(unit(n0 + half), KD // 2, width)
                for t in range(TT):
                    ts = slice(t * P, (t + 1) * P)
                    ks = [4 * half + k for k in range(4)]
                    ins = split_product(ps[:, banks[t], 0:width],
                                        [(srch[:, k, ts], srcl[:, k, ts], w[0][:, k - 4 * half, :], w[1][:, k - 4 * half, :])
                                         for k in ks], first=(half == 0), last=(half == 1),
                                        ready=lambda j: tile_ready(4 * half + j))
                    if half == 1 or t == 1:
                        counted(ins, name)
                release(n0 + half, name)

        def transposes(stage, blocks, banks, evacuated):
            for g in range(0, len(blocks), 4):
                b = banks[(g // 4) % len(banks)]
                if g // 4 >= len(banks):
                    pe.wait_ge(*reached(evacuated, g // 4 - len(banks) + 1))
                for j, src in enumerate(blocks[g:g + 4]):
                    w = src.shape[-1]
                    ins = nc.tensor.transpose(ps[0:w, b, j * P:(j + 1) * P], src, ident)
                counted(ins, stage)

        norm("attn_norm")
        for n in range(4):
            w = by_k(unit(UNITS_AT["w_in"] + n), KD, S)
            for c in range(2):
                counted(feature_major(ps[:, (4 + 2 * n + c) % 8, 0:S], w, c), "lru_in")
            release(UNITS_AT["w_in"] + n, "lru_in")
        pe.wait_ge(*reached("lru_in_copied", TT))
        token_major("tail", UNITS_AT["w_in_tail"], hTh, hTl, (4, 5), TAIL)

        pe.wait_ge(*reached("lru_w_loaded", 16))
        pe.wait_ge(*reached("conv", 8 * 4))
        pe.wait_ge(*reached("lru_in_copied", 2 * LC))
        pe.wait_ge(*reached("tail_copied", TT))
        for d in range(2):
            for c in range(LC):
                for i in range(2):
                    ins = accumulate(ps[:, d * 4 + c, i * S:(i + 1) * S],
                                     [(lru_w[:, (d * 2 + i) * LC + c, :], xc[d][:, c, :])])
                counted(ins, "lru_gates")
        pe.wait_ge(*reached("lru_sq", 1))
        pe.wait_ge(*reached("lru_sigmoid", 8))
        counted(accumulate(ps[:, 0, 0:S], [(ones, th[0][:, c, :]) for c in range(LC)]), "lru_ssq")

        pe.wait_ge(*reached("latent_normed", 4))
        for c in range(3):
            for t in range(TT):
                ins = nc.tensor.transpose(ps[:, 1 + c // 2, (c % 2) * S + t * P:(c % 2) * S + (t + 1) * P],
                                          cn[:, t, c * P:(c + 1) * P], ident)
        counted(ins, "latent_transposed")
        pe.wait_ge(*reached("latentT", 3))
        w = by_k(unit(UNITS_AT["w_uq"]), 2, 768)
        for t in range(TT):
            for h in range(2):
                ts, hs = slice(t * P, (t + 1) * P), slice(h * 384, (h + 1) * 384)
                counted(split_product(ps[:, 4 + 2 * t + h, 0:384],
                                      [(cTh[:, k, ts], cTl[:, k, ts], w[0][:, k, hs], w[1][:, k, hs]) for k in range(2)]),
                        "mla_q")
        release(UNITS_AT["w_uq"], "mla_q")
        w = unit(UNITS_AT["w_ukv"])
        pe.wait_ge(*reached("lru_done", 1))
        for t in range(TT):
            for h in range(2):
                ts, hs = slice(t * P, (t + 1) * P), slice(h * HALF, (h + 1) * HALF)
                counted(split_product(ps[:, 2 * t + h, :], [(cTh[:, 2, ts], cTl[:, 2, ts], w[0][:, hs], w[1][:, hs])]),
                        "mla_kv")
        release(UNITS_AT["w_ukv"], "mla_kv")
        pe.wait_ge(*reached("mla_rotated", 2))
        transposes("mla_qkT_ps", [m[:, t * HEADS + h, :] for m in (mq, mk) for h in range(HEADS) for t in range(TT)],
                   range(8), "mla_qkT")
        pe.wait_ge(*reached("mla_qkT", 8))
        attention("mla")
        pe.wait_ge(*reached("mla_normed", TT))
        transposes("mla_oT_ps", [xn[:, t, c * P:(c + 1) * P] for c in range(LC) for t in range(TT)], [0, 1], "")
        pe.wait_ge(*reached("mla_oT", LC))
        pe.wait_ge(*reached("lru_outT", 1))
        project_out("mixer_x_change", UNITS_AT["w_out"], KD, hTh, hTl, lambda k: None)

        norm("mem_attn_norm")
        tile_ready(KD - 1)
        norm("mem_norm")
        token_major("mem_in", UNITS_AT["w_mem_kv"], memTh, memTl, (0, 1))
        token_major("mem_in", UNITS_AT["w_mem_kv"] + 2, memTh, memTl, (2, 3))
        token_major("mem_in", UNITS_AT["w_mem_q"], hTh, hTl, (4, 5))
        pe.wait_ge(*reached("mem_heads_normed", 2))
        transposes("mem_qkT_ps", [m[:, t, h * P:(h + 1) * P] for m in (eq, ek) for h in range(MEM_HEADS)
                                  for t in range(TT)], range(4), "")
        pe.wait_ge(*reached("mem_qkT", 8))
        attention("mem")
        pe.wait_ge(*reached("mem_att_out", 8))
        transposes("mem_oT_ps", [eo[:, t, c * P:(c + 1) * P] for c in range(4) for t in range(TT)], [0, 1], "")
        pe.wait_ge(*reached("mem_oT", 2))
        project_out("memory_x_change", UNITS_AT["w_mem_o"], 4, hTh, hTl, lambda k: None)

        def gated(stage, n0):
            for f in range(FT):
                w = by_k(unit(n0 + f), KD, S)
                if f >= 4:
                    pe.wait_ge(*reached(stage + "_gated_read", f - 3))
                for i in range(2):
                    ins = feature_major(ps[:, f % 4, i * S:(i + 1) * S], w, i)
                counted(ins, stage + "_gu")
                release(n0 + f, stage + "_gu")

        norm("ffn_norm")
        gated("ffn", UNITS_AT["w_up"])
        project_out("ffn_x_change", UNITS_AT["w_down"], FT, hidh, hidl, lambda k: pe.wait_ge(*reached("ffn_hid", k + 1)))

        norm("attn_norm_2")
        for j in range(6):
            if j >= 4:
                pe.wait_ge(*reached("attn_in_read", 2 * j - 6))
            token_major("attn_in", UNITS_AT["attn_w_in"] + 2 * j, hTh, hTl, ((2 * j) % 8, (2 * j + 1) % 8))
        pe.wait_ge(*reached("attn_in_read", 12))
        bank = 0
        for i, (m, n) in enumerate(((dq, 6), (dk, 6), (fq, 2), (fk, 2))):
            pe.wait_ge(*reached("attn_heads_normed", i + 1))
            transposes("attn_qkT_ps", [m[:, t, c * P:(c + 1) * P] for c in range(n) for t in range(TT)],
                       range(bank, bank + n // 2), "")
            bank += n // 2
        pe.wait_ge(*reached("attn_qkT", 8))
        attention("dil")
        pe.wait_ge(*reached("attn_mixed", 2))
        transposes("attn_oT_ps", [xn[:, t, c * P:(c + 1) * P] for c in range(KD) for t in range(TT)], range(4), "")
        pe.wait_ge(*reached("attn_oT", 4))
        project_out("attn_x_change", UNITS_AT["attn_w_out"], KD, hTh, hTl, lambda k: None)

        norm("ffn_norm_2")
        gated("ffn2", UNITS_AT["ffn_gate_up"])
        project_out("ffn2_x_change", UNITS_AT["ffn_w_down"], FT, hidh, hidl,
                    lambda k: pe.wait_ge(*reached("ffn2_hid", k + 1)))

        norm("hgrn_norm_2")
        for g in range(16):
            if g % 2 == 0:
                w = by_k(unit(UNITS_AT["hgrn_w_in"] + g // 2), KD, S)
            if g >= 8:
                pe.wait_ge(*reached("hgrn_q_read", g - 7))
            counted(feature_major(ps[:, g % 8, 0:S], w, g % 2), "hgrn_in")
            if g % 2 == 1:
                release(UNITS_AT["hgrn_w_in"] + g // 2, "hgrn_in")
        for j in range(4):
            pe.wait_ge(*reached("hgrn_in_read", 2 * j + 2))
            token_major("hgrn_in2", UNITS_AT["hgrn_w_in"] + 8 + 2 * j, hTh, hTl, (2 * j, 2 * j + 1))
        for half in range(2):
            pe.wait_ge(*reached("hgrn_in_read", 16))
            pe.wait_ge(*reached("hgrn_factors", 4 * half + 3))
            if half == 1:
                pe.wait_ge(*reached("hgrn_state", 12))
            for h in range(4):
                for c in range(4):
                    q0 = 64 * (c % 2)
                    for m, lo in ((32, 0), (64, 32)):
                        col0 = h * P + (c // 2) * 64 + lo
                        ins = nc.tensor.matmul(ps[q0:q0 + m, 0, col0:col0 + 32], gK[:, h, c * 64:c * 64 + m],
                                               gQ[:, h, c * 64 + lo:c * 64 + lo + 32], start=True, stop=True)
            counted(ins, "hgrn_scores")
            pe.wait_ge(*reached("hgrn_factors", 4 * half + 4))
            for h in range(4):
                for t in range(TT):
                    ins = nc.tensor.transpose(ps[:, 1 + h // 2, (h % 2) * S + t * P:(h % 2) * S + (t + 1) * P],
                                              gk[:, 4 * half + h, t * P:(t + 1) * P], ident)
            counted(ins, "hgrn_keysT")
            pe.wait_ge(*reached("hgrn_keysT_copied", 2 * (half + 1)))
            pe.wait_ge(*reached("hgrn_masked", half + 1))
            if half == 1:
                pe.wait_ge(*reached("hgrn_o_copied", 2))
            for c in range(4):
                q0, t = 64 * (c % 2), c // 2
                for h in range(4):
                    head = 4 * half + h
                    v = gv[q0:q0 + 64, t, head * P:(head + 1) * P]
                    o = ps[q0:q0 + 64, 4 + h // 2, (h % 2) * S + t * P:(h % 2) * S + (t + 1) * P]
                    ins = nc.tensor.matmul(o, AT[q0:q0 + 64, head, t * 64:(t + 1) * 64], v, start=True, stop=(c == 0))
                    if c > 0:
                        pe.wait_ge(*reached("hgrn_state", 12 * half + 4 * (c - 1) + h + 1))
                        ins = nc.tensor.matmul(o, gq[:, head, c * 64:(c + 1) * 64], state[:, h, :], start=False,
                                               stop=True)
                    counted(ins, "hgrn_o")
                if c < 3:
                    for h in range(4):
                        head = 4 * half + h
                        if c > 0 or half > 0:
                            pe.wait_ge(*reached("hgrn_state", 12 * half + 4 * c + h - 3))
                        counted(nc.tensor.matmul(ps[:, (3, 6, 7, 0)[h], 0:P], kstT[q0:q0 + 64, h, t * P:(t + 1) * P],
                                                 gv[q0:q0 + 64, t, head * P:(head + 1) * P], start=True, stop=True),
                                "hgrn_kv")
        pe.wait_ge(*reached("hgrn_gated", 1))
        pe.wait_ge(*reached("hgrn_o_copied", 4))
        transposes("hgrn_oT_ps", [xn[:, t, c * P:(c + 1) * P] for c in range(KD) for t in range(TT)], range(4), "")
        pe.wait_ge(*reached("hgrn_oT", 4))
        project_out("hgrn_x_change", UNITS_AT["hgrn_w_out"], KD, hTh, hTl, lambda k: None)

        norm("moe_norm_2")
        pe.wait_ge(sem("router_lo"), 1)
        split_product(ps[0:NE, 7, 0:S], [(rh[:, k * NE:(k + 1) * NE], rl[:, k * NE:(k + 1) * NE], hTh[:, k, :], hTl[:, k, :])
                                         for k in range(KD)], ready=tile_ready).then_inc(sem("logits"), 1)
        pe.wait_ge(sem("logits_read"), 1)
        for t in range(TT):
            ins = nc.tensor.transpose(ps[:, 6, t * NE:(t + 1) * NE], logitsT[:, t * P:(t + 1) * P], ident[0:NE, 0:NE])
        ins.then_inc(sem("logits"), 1)
        pe.wait_ge(sem("selected"), 1)
        before = const("before", P)
        sel = rt[:, 2]
        accumulate(ps[:, 7, 0:NE], [(before, sel[:, 0, :])])
        accumulate(ps[:, 7, NE:2 * NE], [(ones, sel[:, 0, :]), (before, sel[:, 1, :])])
        accumulate(ps[:, 7, 2 * NE:3 * NE], [(ones, sel[:, 0, :]), (ones, sel[:, 1, :])]).then_inc(sem("slots_ps"), 1)
        pe.wait_ge(sem("routed"), 1)
        pe.sem_inc(sem("unit_used"), 3)

        def gather(q, value):
            pe.wait_ge(sem("chosen"), value + 1)
            if not (isinstance(value, int) and value == 0 and q == 0):
                pe.wait_ge(sem("bank7_free"), value * 3 + q)
            for d in range(4):
                c = 4 * q + d
                for t in range(TT):
                    for i in range(3):
                        ins = nc.tensor.matmul(ps[:, 7, d * P:(d + 1) * P], parts[i][:, t, c * P:(c + 1) * P], G[:, t, :],
                                               start=(t == 0 and i == 0), stop=(t == TT - 1 and i == 2))
            ins.then_inc(sem("bank7_full"), 1)

        def experts(first, last):
            with nc.tensor.Fori(first, last) as e:
                def unit_of(what):
                    j = UNIT_OF[what]
                    pe.wait_ge(sem("lo_made"), e * E_UNITS + (N_FIXED + j + 1))
                    s = (N_FIXED + j) % SPLIT
                    n = HALF if what[0] != "down" else D
                    return by_k((wh[:, s, :], wl[:, s, :]), UNIT // n, n)

                for c in range(ECH + 1):
                    b = 2 * (c % 2)
                    if c < ECH:
                        if c == 0:
                            pe.wait_ge(sem("bank7_free"), e * 3 + 2)
                        pe.wait_ge(sem("hidden"), e * ECH + (c + 1))
                        if c == 1:
                            pe.wait_ge(sem("out_added"), (e + 1) * 4)
                    for i, what in enumerate(("gate", "up")):
                        if c == ECH:
                            break
                        if i == 1 and c > 0:
                            transposed(e, c - 1)
                        for half in range(2):
                            w = unit_of((what, c, half))
                            ks = [4 * half + k for k in range(4)]
                            ins = split_product(ps[:, b + i, :],
                                                [(xeh[:, k, :], xel[:, k, :], w[0][:, k - 4 * half, :], w[1][:, k - 4 * half, :])
                                                 for k in ks], first=(half == 0), last=(half == 1))
                            ins.then_inc(sem("unit_used"), 1)
                    if c == ECH:
                        transposed(e, c - 1)
                        gather(1, e + 1)
                    if c > 0:
                        d = c - 1
                        if c == ECH - 1:
                            pe.wait_ge(sem("weighted"), e + 1)
                            pe.wait_ge(sem("bank7_free"), e * 3 + 2)
                            for t in range(TT):
                                ins = nc.tensor.transpose(ps[:, 7, t * P:(t + 1) * P], Gw[:, t, :], ident)
                            ins.then_inc(sem("bank7_full"), 1)
                        pe.wait_ge(sem("expert_hid"), e * ECH + d + 1)
                        if d == 0:
                            pe.wait_ge(sem("y_copied"), (e + 1) * 2)
                        for half in range(2):
                            w = unit_of(("down", d, half))
                            for h in range(2):
                                hs = slice(h * HALF, (h + 1) * HALF)
                                ins = split_product(ps[:, 4 + h, :],
                                                    [(ehh[d % 2][:, 2 * half + k, :], ehl[d % 2][:, 2 * half + k, :],
                                                      w[0][:, k, hs], w[1][:, k, hs]) for k in range(2)],
                                                    first=(d == 0 and half == 0), last=(d == ECH - 1 and half == 1))
                            ins.then_inc(sem("unit_used"), 1)
                        if c == ECH - 1:
                            gather(0, e + 1)
                pe.wait_ge(sem("y_copied"), (e + 2) * 2)
                pe.wait_ge(sem("bank7_free"), e * 3 + 5)
                for t in range(TT):
                    for h in range(2):
                        nc.tensor.matmul(ps[:, (6, 7, 2, 3)[2 * t + h], :], GT[:, t, :], y_e[:, h * HALF:(h + 1) * HALF],
                                         start=True, stop=True).then_inc(sem("out_change"), 1)

        def transposed(e, c):
            pe.wait_ge(sem("hidden"), e * ECH + (c + 3))
            if c == 0:
                pe.wait_ge(sem("out_added"), (e + 1) * 4)
            else:
                pe.wait_ge(sem("expert_hid"), e * ECH + c)
            for f in range(4):
                ins = nc.tensor.transpose(ps[:, 6, f * P:(f + 1) * P], eh[c % 2][:, f * P:(f + 1) * P], ident)
            ins.then_inc(sem("hidden_transposed"), 1)

        for q in range(2):
            gather(q, 0)
        experts(0, NE)
        with nc.tensor.If(nc.tensor.value_load(over[0:1, 0:1], min_val=0, max_val=1)):
            experts(NE, 2 * NE)

    @block.sync
    def _(sp_):
        sp_.dma_start(x[:], x_d).then_inc(sem("x_loaded"), 16)
        small_consts = CONST["dist"]
        sp_.dma_start(cols[:], cols_d).then_inc(sem("params"), 16)
        sp_.dma_start(consts[:, 0:small_consts], consts_d[:, 0:small_consts]).then_inc(sem("params"), 16)
        sp_.dma_start(pos[:], pos_d).then_inc(sem("params"), 16)

        def load(n, slot_n, source):
            sp_.dma_start(raw[:, slot_n % RAW, :], source).then_inc(raw_loaded[slot_n % RAW], 16)

        head = RAW + FIRST_RAW
        for n in range(head):
            if n >= RAW:
                sp_.wait_ge(sem("lo_made"), n - RAW + 1)
            load(n, n, units_d[n])
            if n == 3:
                sp_.dma_start(lru_w[:], lru_w_d).then_inc(sem("lru_w_loaded"), 16)
            if n == RAW - 1:
                sp_.dma_start(rows[:], rows_d.partition_broadcast(P)).then_inc(sem("late_params"), 16)
                sp_.dma_start(consts[:, small_consts:], consts_d[:, small_consts:]).then_inc(sem("late_params"), 16)
        assert (N_UNITS - head) % RAW == 0
        with nc.sync.Fori(0, (N_UNITS - head) // RAW) as g:
            for j in range(RAW):
                sp_.wait_ge(sem("lo_made"), g * RAW + (head + j - RAW + 1))
                load(None, head + j, units_d[g * RAW + (head + j)])

        def follow(n, source):
            sp_.wait_ge(sem("lo_made"), n - RAW + 1)
            load(None, n, units_d[source])

        for j in range(SPLIT):
            follow(N_UNITS + j, N_FIXED + j)
        sp_.wait_ge(sem("routed"), 1)
        with nc.sync.If(nc.sync.value_load(over[0:1, 0:1], min_val=0, max_val=1)):
            groups = (NE * E_UNITS - SPLIT) // RAW
            with nc.sync.Fori(0, groups) as g:
                for j in range(RAW):
                    n = N_UNITS + SPLIT + j
                    sp_.wait_ge(sem("lo_made"), g * RAW + (n - RAW + 1))
                    load(None, n, units_d[g * RAW + (N_FIXED + SPLIT + j)])
            for j in range(SPLIT + groups * RAW, NE * E_UNITS + SPLIT):
                follow(N_UNITS + j, N_FIXED + j % (NE * E_UNITS))
        for t in range(TT):
            sp_.wait_ge(*reached("x_final", 4))
            sp_.dma_start(out_d[:, t, :], x[:, t, :]).then_inc(sem("stored"), 16)
        sp_.wait_ge(*reached("stored", 16 * TT))

    @block.scalar
    def _(act):
        A = nc.scalar.activation
        made = [0]

        def hi_to(m):
            for n in range(made[0], m):
                act.wait_ge(raw_loaded[n % RAW], 16 * (n // RAW + 1))
                if n >= SPLIT:
                    act.wait_ge(*released[n - SPLIT])
                A(wh[:, n % SPLIT, :], raw[:, n % RAW, :], ACT.Copy).then_inc(sem("hi_made"), 1)
            made[0] = max(made[0], m)

        def norm(name, ahead):
            i = NORM_OF[name]
            src = mem if name == "mem_norm" else x
            if name == "attn_norm":
                act.wait_ge(*reached("x_loaded", 16))
            elif name == "mem_norm":
                act.wait_ge(*reached("mem_loaded", 16))
            else:
                A(warm, ones[:, 0:1], ACT.Sqrt)
            for t in range(TT):
                if name in NORM_NEEDS:
                    act.wait_ge(*reached("x_ready", NORM_NEEDS[name] - (2 if t == 0 else 0)))
                A(xn[:, t, :], src[:, t, :], ACT.Square, accum_out=ssq[:, 2 * i + t:2 * i + t + 1]).then_inc(sem("norm_ssq"), 1)
            act.wait_ge(*reached("norm_ms", i + 1))
            A(std[:, 2 * i:2 * i + 2], msum[:, 2 * i:2 * i + 2], ACT.Sqrt).then_inc(sem("norm_std"), 1)
            if i == 0:
                hi_to(1)
                act.wait_ge(*reached("params", 16 * 3))
            dst = memTh if name == "mem_norm" else hTh
            for c in range(KD):
                act.wait_ge(*reached("norm_transposed", 4 * i + c // 2 + 1))
                A(dst[:, c, :], ps[:, c // 2, (c % 2) * S:(c % 2 + 1) * S], ACT.Identity,
                  scale=col(name, c)).then_inc(sem("norm_hi"), 1)
            hi_to(ahead)

        def sqrt_of(dst, src, ready, done):
            act.wait_ge(*reached(ready, 1))
            A(dst, src, ACT.Sqrt).then_inc(sem(done), 1)

        def attention(stage):
            a = att[stage]
            units = UNITS[stage]
            n = len(units)
            for i in range(n + 1):
                if i < n:
                    u = units[i]
                    act.wait_ge(*reached(stage + "_att_max", i + 1))
                    if i >= 2:
                        act.wait_ge(*reached(stage + "_att_transposed", i - 1))
                    src = ps[:, i % 2, 0:u["nk"]] if u["dist"] is None else a["s"][i % 2][:, 0:u["nk"]]
                    ins = A(a["p"][i % 2][:, 0:u["nk"]], src, ACT.Exp, bias=a["nmax"][:, i:i + 1],
                            accum_out=a["sum"][:, i:i + 1])
                    ins.then_inc(sem(stage + "_att_probs"), 1)
                j = i - 1
                if j >= 0:
                    u = units[j]
                    act.wait_ge(*reached(stage + "_att_transposed", j + 1))
                    if j >= 2:
                        act.wait_ge(*reached(stage + "_att_weighted", j - 1))
                    A(a["pT"][j % 2][:, 0:u["nk"]], ps[:, 2 + j % 2, 0:u["nk"]], ACT.Copy).then_inc(sem(stage + "_att_probsT"), 1)

        def oT_high(stage, groups):
            for g in range(groups):
                act.wait_ge(*reached(stage + "_oT_ps", g + 1))
                A(hTh[:, 2 * g:2 * g + 2, :], ps[:, g, :].rearrange("p (a b) -> p a b", a=2),
                  ACT.Copy).then_inc(sem(stage + "_oT_hi"), 1)

        norm("attn_norm", 3)
        act.wait_ge(*reached("lam_abs", 1))
        A(sp["b"], sp["a"], ACT.Exp, scale=-1.0).then_inc(sem("lam_exp"), 1)
        for j in range(2 * LC):
            act.wait_ge(*reached("lru_in", j + 1))
            c = j % LC
            dst = xrp[:, c, 3:3 + S] if j < LC else yg[:, c, :]
            A(dst, ps[:, (4 + j) % 8, 0:S], ACT.Copy).then_inc(sem("lru_in_copied"), 1)
            if j % 2 == 1:
                hi_to(j // 2 + 4)
        for t in range(TT):
            act.wait_ge(*tile_of("tail", t))
            A(tail[:, t, :], ps[:, 4 + t, 0:TAIL], ACT.Copy).then_inc(sem("tail_copied"), 1)
        hi_to(UNITS_AT["w_ukv"] + 2)
        for d in range(2):
            for c in range(LC):
                act.wait_ge(*reached("lru_gates", d * LC + c + 1))
                A(ra[d][:, c, :], ps[:, d * 4 + c, 0:S], ACT.Sigmoid, bias=col("lru_b_a", d * LC + c))
                A(ri[d][:, c, :], ps[:, d * 4 + c, S:2 * S], ACT.Sigmoid,
                  bias=col("lru_b_i", d * LC + c)).then_inc(sem("lru_sigmoid"), 1)
        act.wait_ge(*reached("gelu_z", 1))
        A(z, z, ACT.Sigmoid, scale=2.0 * math.sqrt(2.0 / math.pi)).then_inc(sem("gelu_sig"), 1)
        act.wait_ge(*reached("softplus", 1))
        act.wait_ge(*reached("lru_sigmoid", 8))
        for d in range(2):
            for c in range(LC):
                s = sp["out"][:, d * LC + c:d * LC + c + 1]
                A(th[d][:, c, :], ra[d][:, c, :], ACT.Tanh, scale=s).then_inc(sem("lru_tanh"), 1)
        act.wait_ge(*reached("lru_tanh", 8))
        for d in range(2):
            A(root[d], th[d][:], ACT.Ln, scale=-1.0, bias=ones[:, 0:1]).then_inc(sem("lru_ln"), 1)
        for d in range(2):
            act.wait_ge(*reached("lru_ln", d + 1))
            A(root[d], root[d], ACT.Exp, scale=-0.5).then_inc(sem("lru_root"), 1)
        for d in range(2):
            for c in range(LC):
                s = sp["out"][:, d * LC + c:d * LC + c + 1]
                A(ra[d][:, c, :], ra[d][:, c, :], ACT.Exp, scale=s).then_inc(sem("lru_a"), 1)
        for d in range(2):
            act.wait_ge(*reached("lru_ln", 2))
            A(th[d][:], th[d][:], ACT.Sqrt, scale=-2.0).then_inc(sem("lru_mult"), 1)
        act.wait_ge(*reached("lru_gated", 1))
        A(th[0][:], ri[0][:], ACT.Square).then_inc(sem("lru_sq"), 1)
        sqrt_of(ri[1][:, 0, :], ri[1][:, 1, :], "lru_ms", "lru_std")
        for j, (t, a, b) in enumerate(((0, 0, 256), (1, 0, 256), (0, 256, 384), (1, 256, 384))):
            if j == 0:
                act.wait_ge(*reached("tail_copied", TT))
                act.wait_ge(*reached("norm_ssq", 2))
            else:
                act.wait_ge(*reached("latent_ssq", j))
            A(junk[:, 0:b - a], tail[:, t, a:b], ACT.Square, accum_out=lat["ssq"][:, j:j + 1]).then_inc(sem("latent_ssq"), 1)
        sqrt_of(lat["std"], lat["ms"], "latent_ms", "latent_std")
        act.wait_ge(*reached("lru_scaled", LC))
        A(hTh[:, 0:LC, :], th[0][:], ACT.Copy).then_inc(sem("lru_hi"), 1)
        act.wait_ge(*reached("latent_transposed", 1))
        for c in range(3):
            g = col("q_a_norm", c) if c < 2 else col("kv_a_norm", 0)
            A(cTh[:, c, :], ps[:, 1 + c // 2, (c % 2) * S:(c % 2) * S + S], ACT.Identity,
              scale=g).then_inc(sem("latent_hi"), 1)
        for t in range(TT):
            for h in range(2):
                act.wait_ge(*reached("mla_q", 2 * t + h + 1))
                A(mq[:, t * HEADS + 4 * h:t * HEADS + 4 * h + 4, :],
                  ps[:, 4 + 2 * t + h, 0:384].rearrange("p (a b) -> p a b", a=4), ACT.Copy).then_inc(sem("mla_q_copied"), 1)
        for t in range(TT):
            for h in range(2):
                act.wait_ge(*reached("mla_kv", 2 * t + h + 1))
                kv = ps[:, 2 * t + h, :].rearrange("p (a b) -> p a b", a=4)
                A(mk[:, t * HEADS + 4 * h:t * HEADS + 4 * h + 4, 0:NOPE], kv[:, :, 0:NOPE], ACT.Copy)
                A(mv[:, t, h * 256:(h + 1) * 256].rearrange("p (a b) -> p a b", a=4), kv[:, :, NOPE:NOPE + VD],
                  ACT.Copy).then_inc(sem("mla_kv_copied"), 1)
        hi_to(UNITS_AT["w_ukv"] + 4)
        act.wait_ge(*reached("rope_angle", 2))
        A(rope["sin"][:], rope["r"][:], ACT.Sin)
        A(rope["cos"][:], rope["ang"][:], ACT.Sin).then_inc(sem("rope_table"), 1)
        for i in range(2):
            act.wait_ge(*reached("mla_head_ms", i + 1))
            A(heads_st[1][:, 16 * i:16 * i + 16], heads_st[0][:, 16 * i:16 * i + 16], ACT.Sqrt).then_inc(sem("mla_head_std"), 1)
        for g in range(8):
            act.wait_ge(*reached("mla_qkT_ps", g + 1))
            dst = (mqT if g < 4 else mkT)[0:QK, 2 * (g % 4):2 * (g % 4) + 2, :]
            A(dst, ps[0:QK, g, :].rearrange("p (a b) -> p a b", a=2), ACT.Copy).then_inc(sem("mla_qkT"), 1)
        attention("mla")
        for t in range(TT):
            act.wait_ge(*reached("mla_att_out", 16))
            if t == 0:
                act.wait_ge(*reached("latent_ssq", 4))
            else:
                act.wait_ge(*reached("mla_ssq", 1))
            A(junk[:, 0:HALF], mo[:, t, :], ACT.Square, accum_out=osq["ssq"][:, t:t + 1]).then_inc(sem("mla_ssq"), 1)
        sqrt_of(osq["std"], osq["ms"], "mla_ms", "mla_std")
        for c in range(LC):
            act.wait_ge(*reached("mla_oT_ps", c // 2 + 1))
            A(hTh[:, LC + c, :], ps[:, c // 2, (c % 2) * S:(c % 2) * S + S], ACT.Identity,
              scale=col("mla_out_norm", c)).then_inc(sem("mla_oT_hi"), 1)
        hi_to(UNITS_AT["w_mem_kv"] + 2)

        act.wait_ge(*reached("x_ready", X_AFTER["mixer"]))
        act.dma_start(mem[:], mem_d).then_inc(sem("mem_loaded"), 16)
        norm("mem_attn_norm", UNITS_AT["w_mem_kv"] + 3)
        norm("mem_norm", 0)
        for j in range(6):
            if j % 2 == 0:
                hi_to(UNITS_AT["w_mem_kv"] + j + 4)
            act.wait_ge(*tile_of("mem_in", j))
            dst = (ek, ev, eq)[j // 2]
            A(dst[:, j % 2, :], ps[:, j, :], ACT.Copy).then_inc(sem("mem_in_copied"), 1)
            if j % 2 == 1:
                hi_to(UNITS_AT["w_mem_kv"] + j + 4)
        for i in range(2):
            act.wait_ge(*reached("mem_head_ms", i + 1))
            A(heads_st[1][:, 32 + 8 * i:40 + 8 * i], heads_st[0][:, 32 + 8 * i:40 + 8 * i],
              ACT.Sqrt).then_inc(sem("mem_head_std"), 1)
        for j in range(8):
            act.wait_ge(*reached("mem_qkT_ps", j // 2 + 1))
            h = j % 4
            A((eqT if j < 4 else ekT)[:, h, :], ps[:, j // 2, (j % 2) * S:(j % 2) * S + S], ACT.Identity,
              scale=col("mem_q_norm" if j < 4 else "mem_k_norm", 0)).then_inc(sem("mem_qkT"), 1)
        attention("mem")
        oT_high("mem", 2)
        hi_to(UNITS_AT["w_up"] + 2)

        norm("ffn_norm", UNITS_AT["w_up"] + 3)
        for f in range(FT + 2):
            if f < FT:
                act.wait_ge(*reached("ffn_gu", f + 1))
                if f >= 4:
                    act.wait_ge(*reached("ffn_product", f - 3))
                for i in range(2):
                    c = f + i * FT
                    ins = A(cv[f % 4][i], ps[:, f % 4, i * S:(i + 1) * S], ACT.Identity,
                            scale=col("ffn_conv_w", 2 * FT + c), bias=col("ffn_conv_b", c))
                ins.then_inc(sem("ffn_centre"), 1)
                hi_to(UNITS_AT["w_up"] + f + 4)
            if 1 <= f <= FT:
                j = f - 1
                act.wait_ge(*reached("ffn_gated_read", j + 1))
                A(sg[j % 4], cv[j % 4][0], ACT.Sigmoid).then_inc(sem("ffn_gated_sigmoid"), 1)
            if f >= 2:
                j = f - 2
                act.wait_ge(*reached("ffn_product", j + 1))
                A(hidh[:, j, :], sg[j % 4], ACT.Copy).then_inc(sem("ffn_hid_hi"), 1)
        hi_to(UNITS_AT["attn_w_in"] + 2)

        norm("attn_norm_2", UNITS_AT["attn_w_in"] + 3)
        pieces = [(dq, 0, 768), (dk, 768, 1536), (dv, 1536, 2304), (fq, 2304, 2560), (fk, 2560, 2816), (fv, 2816, 3072)]
        for j in range(6):
            hi_to(UNITS_AT["attn_w_in"] + 2 * j + 4)
            for t in range(TT):
                act.wait_ge(*tile_of("attn_in", 2 * j + t))
                for dst, a, b in pieces:
                    lo, hi = max(a, j * HALF), min(b, (j + 1) * HALF)
                    if lo < hi:
                        ins = A(dst[:, t, lo - a:hi - a], ps[:, (2 * j + t) % 8, lo - j * HALF:hi - j * HALF], ACT.Copy)
                ins.then_inc(sem("attn_in_read"), 1)
            hi_to(UNITS_AT["attn_w_in"] + 2 * j + 5)
            for i in {2: (0,), 3: (1,), 5: (2, 3)}.get(j, ()):
                o, n = (0, 24, 48, 64)[i], (24, 24, 16, 16)[i]
                act.wait_ge(*reached("attn_head_ms", i + 1))
                A(attn_std[:, o:o + n], attn_ms[:, o:o + n], ACT.Sqrt).then_inc(sem("attn_head_std"), 1)
        act.wait_ge(*reached("lam_dots", 2))
        A(lam4[:, 2:4], lam4[:, 0:2], ACT.Exp).then_inc(sem("lam_exps"), 1)
        for g in range(8):
            act.wait_ge(*reached("attn_qkT_ps", g + 1))
            dst = [dqT, dqT, dqT, dkT, dkT, dkT, fqT, fkT][g]
            c = 2 * (g % 3) if g < 6 else 0
            gain = ("dil_q_gain_2", "dil_k_gain_2")[g // 3] if g < 6 else ("diff_q_gain_2", "diff_k_gain_2")[g - 6]
            A(dst[:, c:c + 2, :], ps[:, g, :].rearrange("p (a b) -> p a b", a=2), ACT.Identity,
              scale=col(gain, 0)).then_inc(sem("attn_qkT"), 1)
        attention("dil")
        act.wait_ge(*reached("alpha_diff", 1))
        A(alpha[:, 0], alpha[:, 0], ACT.Exp).then_inc(sem("alpha_exp"), 1)
        act.wait_ge(*reached("diff_ms", 1))
        A(heads_st[1][:, 48:56], heads_st[0][:, 48:56], ACT.Sqrt).then_inc(sem("diff_std"), 1)
        oT_high("attn", 4)
        hi_to(UNITS_AT["ffn_gate_up"] + 2)

        norm("ffn_norm_2", UNITS_AT["ffn_gate_up"] + 3)
        for f in range(FT + 1):
            if f < FT:
                act.wait_ge(*reached("ffn2_gu", f + 1))
                A(sg[f % 4], ps[:, f % 4, 0:S], ACT.Sigmoid).then_inc(sem("ffn2_gated_sigmoid"), 1)
                hi_to(UNITS_AT["ffn_gate_up"] + f + 4)
            if f >= 1:
                j = f - 1
                act.wait_ge(*reached("ffn2_gated_read", j + 1))
                A(hidh[:, j, :], sg[j % 4], ACT.Copy).then_inc(sem("ffn2_hid_hi"), 1)
        hi_to(UNITS_AT["hgrn_w_in"] + 2)

        A(rh[:], col("moe_w_router_2", 0, KD * NE), ACT.Copy).then_inc(sem("router_hi"), 1)
        act.wait_ge(*reached("lb_diff", 1))
        A(lbs["lb"], lbs["d"], ACT.Sigmoid)
        A(lbs["one_minus"], lbs["d"], ACT.Sigmoid, scale=-1.0).then_inc(sem("lb"), 1)
        norm("hgrn_norm_2", UNITS_AT["hgrn_w_in"] + 3)
        for g in range(24):
            if g >= 16 and g % 2 == 0:
                hi_to(UNITS_AT["hgrn_w_in"] + g - 8 + 4)
            act.wait_ge(*(reached("hgrn_in", g + 1) if g < 16 else tile_of("hgrn_in2", g - 16)))
            if g < 8:
                A(gq[:, g, :], ps[:, g % 8, 0:S], ACT.Sigmoid).then_inc(sem("hgrn_q_sigmoid"), 1)
            elif g < 16:
                A(gB[:, g - 8, :], ps[:, g % 8, 0:S], ACT.Sigmoid)
                A(gk[:, g - 8, :], ps[:, g % 8, 0:S], ACT.Sigmoid, scale=-1.0).then_inc(sem("hgrn_in_read"), 1)
            elif g < 20:
                A(gv[:, g % 2, ((g - 16) // 2) * HALF:((g - 16) // 2 + 1) * HALF], ps[:, g % 8, :],
                  ACT.Copy).then_inc(sem("hgrn_in_read"), 1)
            else:
                A(gg[:, g % 2, ((g - 20) // 2) * HALF:((g - 20) // 2 + 1) * HALF], ps[:, g % 8, :],
                  ACT.Sigmoid).then_inc(sem("hgrn_in_read"), 1)
            if g % 2 == 1:
                hi_to(UNITS_AT["hgrn_w_in"] + (g // 2 if g < 16 else g - 8) + 4)
        act.wait_ge(*reached("hgrn_forget", 1))
        A(gB[:], gB[:], ACT.Ln).then_inc(sem("hgrn_logf"), 1)
        for half in range(2):
            hs = slice(4 * half, 4 * half + 4)
            act.wait_ge(*reached("hgrn_d1", half + 1))
            if half == 1:
                act.wait_ge(*reached("hgrn_scores", 1))
            A(gQ[:], gD[:], ACT.Exp).then_inc(sem("hgrn_eq"), 1)
            A(gK[:], gD[:], ACT.Exp, scale=-1.0).then_inc(sem("hgrn_eq"), 1)
            act.wait_ge(*reached("hgrn_eq", 4 * half + 2))
            A(gD[:], gB[:, hs, :], ACT.Exp).then_inc(sem("hgrn_eq"), 1)
            A(dec[:, 16 * half:16 * half + 16], gB[:, hs, :].rearrange("p h (c j) -> p (h c) j", j=CHUNK)[:, :, CHUNK - 1], ACT.Exp).then_inc(sem("hgrn_dec"), 1)
            act.wait_ge(*reached("hgrn_d2", half + 1))
            A(gD[:], gD[:], ACT.Exp).then_inc(sem("hgrn_eq"), 1)
            for b in range(2):
                act.wait_ge(*reached("hgrn_keysT", half + 1))
                if half == 1:
                    act.wait_ge(*reached("hgrn_kv", 12))
                A(kstT[:, 2 * b:2 * b + 2, :], ps[:, 1 + b, :].rearrange("p (a c) -> p a c", a=2),
                  ACT.Copy).then_inc(sem("hgrn_keysT_copied"), 1)
            for b in range(2):
                act.wait_ge(*reached("hgrn_o", 16 * (half + 1)))
                for t in range(TT):
                    dst = xn[:, t, (4 * half + 2 * b) * P:(4 * half + 2 * b + 2) * P].rearrange("p (a v) -> p a v", a=2)
                    src = ps[:, 4 + b, :].rearrange("p (a t v) -> p t a v", a=2, t=TT)[:, t]
                    ins = A(dst, src, ACT.Copy)
                ins.then_inc(sem("hgrn_o_copied"), 1)
        act.wait_ge(*reached("hgrn_ms", 1))
        A(heads_st[1][:, 0:16], heads_st[0][:, 0:16], ACT.Sqrt).then_inc(sem("hgrn_std"), 1)
        oT_high("hgrn", 4)
        hi_to(N_FIXED + 2)

        act.wait_ge(*reached("x_ready", X_AFTER["hgrn"]))
        act.dma_start(moe_gain, moe_gain_d.partition_broadcast(P)).then_inc(sem("moe_gain"), 16)
        norm("moe_norm_2", N_FIXED + SPLIT)
        for i in range(2):
            act.wait_ge(sem("tokens_left"), i + 1)
            A(parts[i][:], xn[:], ACT.Copy).then_inc(sem("tokens_part"), 1)
        act.wait_ge(*reached("route_diff", 1))
        A(rtv["ex"], rtv["v2"], ACT.Exp).then_inc(sem("route_exp"), 1)
        act.wait_ge(sem("routed"), 1)
        def tokens_high(q, e):
            act.wait_ge(sem("bank7_full"), e * 3 + q + 1)
            A(xeh[:, 4 * q:4 * q + 4, :], ps[:, 7, :].rearrange("p (a b) -> p a b", a=4), ACT.Copy).then_inc(sem("tokens_hi"), 1)

        def experts(first, last):
            with nc.scalar.Fori(first, last) as e:
                def hi(j):
                    n = N_FIXED + j
                    act.wait_ge(raw_loaded[n % RAW], e * (16 * E_UNITS // RAW) + 16 * (n // RAW + 1))
                    act.wait_ge(sem("unit_used"), e * E_UNITS + (j + 1))
                    A(wh[:, n % SPLIT, :], raw[:, n % RAW, :], ACT.Copy).then_inc(sem("hi_made"), 1)

                def hidden_high(c):
                    act.wait_ge(sem("hidden_transposed"), e * ECH + c + 1)
                    A(ehh[c % 2][:], ps[:, 6, :].rearrange("p (a b) -> p a b", a=4), ACT.Copy).then_inc(sem("hidden_hi"), 1)

                for q, (what, c, half) in enumerate(EXPERT_ORDER):
                    if what == "up" and half == 1:
                        act.wait_ge(sem("unit_used"), e * E_UNITS + (q + 1 + SPLIT))
                        act.wait_ge(sem("hidden"), e * ECH + (c + 2))
                        A(esg, ps[:, 2 * (c % 2), :], ACT.Sigmoid).then_inc(sem("sigmoid"), 1)
                    if what == "down" and c == ECH - 2 and half == 0:
                        act.wait_ge(sem("bank7_full"), e * 3 + 3)
                        A(GT[:], ps[:, 7, 0:2 * P].rearrange("p (a b) -> p a b", a=2), ACT.Copy).then_inc(sem("bank7_free"), 1)
                    if q == E_UNITS - 1:
                        act.wait_ge(sem("unit_used"), e * E_UNITS + (E_UNITS + SPLIT))
                        A(y_e[:, 0:HALF], ps[:, 4, :], ACT.Copy).then_inc(sem("y_copied"), 1)
                    hi(q + SPLIT)
                    if what == "gate" and half == 1 and c > 0:
                        hidden_high(c - 1)
                    if what == "down" and c == ECH - 2 and half == 1:
                        tokens_high(0, e + 1)
                        hidden_high(ECH - 1)
                        tokens_high(1, e + 1)

        for q in range(2):
            tokens_high(q, 0)
        experts(0, NE)
        with nc.scalar.If(nc.scalar.value_load(over[0:1, 0:1], min_val=0, max_val=1)):
            experts(NE, 2 * NE)

    @block.vector
    def _(dve):
        V = nc.vector
        steps = [0]

        def step(ins):
            ins.then_inc(sem("vector_step"), 1)
            steps[0] += 1
            dve.wait_ge(*reached("vector_step", steps[0]))

        def settle():
            step(V.tensor_copy(lam4[:, 7:8], ones[:, 0:1]))

        made = [0]

        def lo_to(m):
            for n in range(made[0], m):
                dve.wait_ge(sem("hi_made"), n + 1)
                V.tensor_tensor(wl[:, n % SPLIT, :], raw[:, n % RAW, :], wh[:, n % SPLIT, :].bitcast(F32),
                                ALU.subtract).then_inc(sem("lo_made"), 1)
            made[0] = max(made[0], m)

        def oT_low(stage, groups):
            for g in range(groups):
                dve.wait_ge(*reached(stage + "_oT_hi", g + 1))
                V.tensor_tensor(hTl[:, 2 * g:2 * g + 2, :], ps[:, g, :].rearrange("p (a b) -> p a b", a=2),
                                hTh[:, 2 * g:2 * g + 2, :].bitcast(F32), ALU.subtract).then_inc(sem(stage + "_oT"), 1)

        def norm(name, ahead):
            i = NORM_OF[name]
            src = mem if name == "mem_norm" else x
            dve.wait_ge(*reached("norm_ssq", 2 * (i + 1)))
            V.tensor_scalar(msum[:, 2 * i:2 * i + 2], ssq[:, 2 * i:2 * i + 2], 1.0 / D, EPS, ALU.mult,
                            ALU.add).then_inc(sem("norm_ms"), 1)
            dve.wait_ge(*reached("norm_std", i + 1))
            step(V.reciprocal(rstd[:, 2 * i:2 * i + 2], std[:, 2 * i:2 * i + 2]))
            if i > 0:
                dve.wait_ge(*reached("norm_transposed", 4 * i))
            for t in range(TT):
                V.tensor_scalar(xn[:, t, :], src[:, t, :], rstd[:, 2 * i + t:2 * i + t + 1], None,
                                ALU.mult).then_inc(sem("norm_xn"), 1)
            if i == 0:
                lo_to(1)
            dsth, dstl = (memTh, memTl) if name == "mem_norm" else (hTh, hTl)
            for c in range(KD):
                dve.wait_ge(*reached("norm_hi", KD * i + 2 * (c // 2) + 2))
                V.scalar_tensor_tensor(out=dstl[:, c, :], in0=ps[:, c // 2, (c % 2) * S:(c % 2 + 1) * S],
                                       scalar=col(name, c), in1=dsth[:, c, :].bitcast(F32), op0=ALU.mult,
                                       op1=ALU.subtract).then_inc(sem("norm_out"), 1)
            lo_to(ahead)

        def residual(stage, n, following):
            lo_to(following + 1)
            for t in range(TT):
                if t == 1:
                    lo_to(following + 2)
                for h in range(2):
                    dve.wait_ge(*reached(stage, n - 3 + 2 * t + h))
                    xs = x[:, t, h * HALF:(h + 1) * HALF]
                    V.tensor_tensor(xs, ps[:, 4 + 2 * t + h, :], xs, ALU.add).then_inc(sem("x_ready"), 1)

        def attention(stage):
            a = att[stage]
            units = UNITS[stage]
            n = len(units)
            for i in range(n + 2):
                if i < n:
                    u = units[i]
                    dve.wait_ge(*reached(stage + "_att_scores", i + 1))
                    src = ps[:, i % 2, 0:u["nk"]]
                    nm = a["nmax"][:, i:i + 1]
                    if u["dist"] is None:
                        V.reduce_max(nm, src, AX, negate=True).then_inc(sem(stage + "_att_max"), 1)
                    else:
                        if i >= 2:
                            dve.wait_ge(*reached(stage + "_att_probs", i - 1))
                        s = a["s"][i % 2][:, 0:u["nk"]]
                        step(V.scalar_tensor_tensor(out=s, in0=u["dist"], scalar=-u["slope"], in1=src, op0=ALU.mult,
                                                    op1=ALU.add))
                        V.reduce_max(nm, s, AX, negate=True).then_inc(sem(stage + "_att_max"), 1)
                j = i - 2
                if j >= 0:
                    u = units[j]
                    dve.wait_ge(*reached(stage + "_att_probs", j + 1))
                    inv = a["inv"][:, j:j + 1]
                    if u["kind"] == "raw":
                        dve.wait_ge(*reached(stage + "_att_weighted", j + 1))
                        V.tensor_copy(u["out"], ps[:, 4 + j % 2, 0:u["dv"]]).then_inc(sem(stage + "_att_out"), 1)
                        continue
                    step(V.reciprocal(inv, a["sum"][:, j:j + 1]))
                    if u["kind"] == "minus":
                        step(V.tensor_scalar(inv, inv, lam4[:, 4:5], None, ALU.mult))
                    dve.wait_ge(*reached(stage + "_att_weighted", j + 1))
                    if u["kind"] == "plain":
                        V.tensor_scalar(u["out"], ps[:, 4 + j % 2, 0:u["dv"]], inv, None,
                                        ALU.mult).then_inc(sem(stage + "_att_out"), 1)
                    else:
                        dve.wait_ge(*reached(stage + "_att_out", j))
                        V.scalar_tensor_tensor(out=u["out"], in0=ps[:, 4 + j % 2, 0:u["dv"]], scalar=inv, in1=u["out"],
                                               op0=ALU.mult, op1=ALU.add).then_inc(sem(stage + "_att_out"), 1)
            settle()

        def head_norm(buf, n, w, scratch, ms, stdv, inv, ready, std_sem, std_n, gain, scale):
            sq = scratch[:, 0:n * w].rearrange("p (a b) -> p a b", a=n)
            step(V.tensor_tensor(sq, buf, buf, ALU.mult))
            step(V.tensor_reduce(ms, sq, AX, ALU.add))
            V.tensor_scalar(ms, ms, 1.0 / (w * scale * scale), EPS / (scale * scale), ALU.mult,
                            ALU.add).then_inc(sem(ready), 1)
            dve.wait_ge(*reached(std_sem, std_n))
            step(V.reciprocal(inv, stdv))
            step(V.tensor_tensor(buf, buf, inv.unsqueeze(2).to_broadcast([P, n, w]), ALU.mult))
            if gain is not None:
                step(V.tensor_tensor(buf, buf, gain.unsqueeze(1).to_broadcast([P, n, w]), ALU.mult))

        V.memset(xrp[:, :, 0:3], 0.0)
        step(V.memset(xrp[:, :, S + 3:S + 6], 0.0))
        lam = col("lru_lambda", 0, 8)
        dve.wait_ge(*reached("params", 16 * 3))
        norm("attn_norm", 3)
        step(V.tensor_scalar(sp["c"], lam, -1.0, None, ALU.mult))
        V.tensor_tensor(sp["a"], sp["c"], lam, ALU.max).then_inc(sem("lam_abs"), 1)
        lo_to(4)
        dve.wait_ge(*reached("lam_exp", 1))
        step(V.tensor_scalar(sp["s"], sp["b"], 2.0, None, ALU.add))
        step(V.reciprocal(sp["s"], sp["s"]))
        step(V.tensor_tensor(sp["s"], sp["s"], sp["b"], ALU.mult))
        step(V.tensor_tensor(sp["s2"], sp["s"], sp["s"], ALU.mult))
        step(V.tensor_scalar(sp["p"], sp["s2"], 1.0 / 17, None, ALU.mult))
        for n in (15, 13, 11, 9, 7, 5, 3):
            step(V.scalar_tensor_tensor(out=sp["p"], in0=sp["p"], scalar=1.0 / n, in1=sp["s2"], op0=ALU.add, op1=ALU.mult))
        step(V.scalar_tensor_tensor(out=sp["p"], in0=sp["p"], scalar=1.0, in1=sp["s"], op0=ALU.add, op1=ALU.mult))
        step(V.tensor_scalar(sp["c"], sp["c"], 0.0, -8.0, ALU.max, ALU.mult))
        V.scalar_tensor_tensor(out=sp["out"], in0=sp["p"], scalar=-16.0, in1=sp["c"], op0=ALU.mult,
                               op1=ALU.add).then_inc(sem("softplus"), 1)
        lo_to(UNITS_AT["w_uq"])
        for k in range(4):
            for d in range(2):
                for c in range(LC):
                    j = d * LC + c
                    if k == 0:
                        dve.wait_ge(*reached("lru_in_copied", c + 1))
                    elif j == 0:
                        dve.wait_ge(*reached("conv", 8 * k))
                    src = xrp[:, c, k + 3 * d:k + 3 * d + S]
                    w = col("lru_conv_w", (d * 4 + k) * LC + c)
                    if k == 0:
                        ins = V.tensor_scalar(xc[d][:, c, :], src, w, col("lru_conv_b", d * LC + c), ALU.mult, ALU.add)
                    else:
                        ins = V.scalar_tensor_tensor(out=xc[d][:, c, :], in0=src, scalar=w, in1=xc[d][:, c, :],
                                                     op0=ALU.mult, op1=ALU.add)
                    ins.then_inc(sem("conv"), 1)
        dve.wait_ge(*reached("lru_in_copied", 8))
        dve.wait_ge(*reached("conv", 32))
        step(V.tensor_tensor(z, yg[:], yg[:], ALU.mult))
        step(V.tensor_scalar(z, z, 0.044715, 1.0, ALU.mult, ALU.add))
        V.tensor_tensor(z, z, yg[:], ALU.mult).then_inc(sem("gelu_z"), 1)
        lo_to(UNITS_AT["w_ukv"] + 2)
        for d in range(2):
            dve.wait_ge(*reached("lru_sigmoid", 8))
            step(V.tensor_tensor(ri[d][:], ri[d][:], xc[d][:], ALU.mult))
        dve.wait_ge(*reached("gelu_sig", 1))
        step(V.tensor_tensor(yg[:], yg[:], z, ALU.mult))
        for d in range(2):
            dve.wait_ge(*reached("lru_root", d + 1))
            step(V.tensor_tensor(ri[d][:], ri[d][:], root[d], ALU.mult))
            dve.wait_ge(*reached("lru_mult", d + 1))
            dve.wait_ge(*reached("lru_a", 4 * (d + 1)))
            step(V.tensor_tensor(ri[d][:], ri[d][:], th[d][:], ALU.mult))
            for c in range(LC):
                r = slice(None, None, -1) if d else slice(None)
                ins = V.tensor_tensor_scan(xc[d][:, c, r], ra[d][:, c, r], ri[d][:, c, r], 0.0, ALU.mult, ALU.add)
            step(ins)
        step(V.tensor_tensor(xc[0][:], xc[0][:], xc[1][:], ALU.add))
        V.tensor_tensor(ri[0][:], xc[0][:], yg[:], ALU.mult).then_inc(sem("lru_gated"), 1)
        dve.wait_ge(*reached("lru_ssq", 1))
        V.tensor_scalar(ri[1][:, 1, :], ps[:, 0, 0:S], 1.0 / LRU_W, EPS, ALU.mult, ALU.add).then_inc(sem("lru_ms"), 1)
        dve.wait_ge(*reached("lru_std", 1))
        ins = V.reciprocal(ri[1][:, 2, :], ri[1][:, 0, :])
        ins.then_inc(sem("lru_done"), 1)
        dve.wait_ge(*reached("lru_done", 1))
        for c in range(LC):
            V.scalar_tensor_tensor(out=th[0][:, c, :], in0=ri[0][:, c, :], scalar=col("lru_out_norm", c), in1=ri[1][:, 2, :],
                                   op0=ALU.mult, op1=ALU.mult).then_inc(sem("lru_scaled"), 1)
        dve.wait_ge(*reached("latent_ssq", 4))
        V.tensor_scalar(lat["ms"][:, 0:2], lat["ssq"][:, 0:2], 1.0 / Q_LORA, EPS, ALU.mult, ALU.add)
        step(V.tensor_scalar(lat["ms"][:, 2:4], lat["ssq"][:, 2:4], 1.0 / KV_LORA, EPS, ALU.mult, ALU.add))
        V.sem_inc(sem("latent_ms"), 1)
        dve.wait_ge(*reached("latent_std", 1))
        step(V.reciprocal(lat["r"], lat["std"]))
        for j, (t, a, b) in enumerate(((0, 0, 256), (1, 0, 256), (0, 256, 384), (1, 256, 384))):
            V.tensor_scalar(cn[:, t, a:b], tail[:, t, a:b], lat["r"][:, j:j + 1], None, ALU.mult).then_inc(sem("latent_normed"), 1)
        dve.wait_ge(*reached("lru_hi", 1))
        dve.wait_ge(*reached("lru_scaled", LC))
        V.tensor_tensor(hTl[:, 0:LC, :], th[0][:], hTh[:, 0:LC, :].bitcast(F32), ALU.subtract).then_inc(sem("lru_outT"), 1)
        for c in range(3):
            g = col("q_a_norm", c) if c < 2 else col("kv_a_norm", 0)
            dve.wait_ge(*reached("latent_hi", 3))
            V.scalar_tensor_tensor(out=cTl[:, c, :], in0=ps[:, 1 + c // 2, (c % 2) * S:(c % 2) * S + S], scalar=g,
                                   in1=cTh[:, c, :].bitcast(F32), op0=ALU.mult, op1=ALU.subtract).then_inc(sem("latentT"), 1)
        dve.wait_ge(*reached("params", 16 * 3))
        step(V.tensor_copy(posf, pos[:]))
        for t in range(TT):
            ins = V.tensor_scalar(rope["ang"][:, t, :], const("inv_freq", ROPE // 2), posf[:, t:t + 1], None, ALU.mult)
        step(ins)
        turn = 2.0 * math.pi
        c1 = float(np.float32(np.round(turn * 256) / 256))
        c2 = float(np.float32(np.round((turn - c1) * 2 ** 20) / 2 ** 20))
        c3 = float(np.float32(turn - c1 - c2))
        near = 1.5 * 2.0 ** 23

        def reduced(dst, src):
            step(V.tensor_scalar(rope["k"][:], src, 1.0 / turn, near, ALU.mult, ALU.add))
            step(V.tensor_scalar(rope["k"][:], rope["k"][:], near, None, ALU.subtract))
            for n, cc in enumerate((c1, c2, c3)):
                step(V.scalar_tensor_tensor(out=dst, in0=rope["k"][:], scalar=-cc, in1=(src if n == 0 else dst),
                                            op0=ALU.mult, op1=ALU.add))
            step(V.tensor_scalar(dst, dst, math.pi * (1 - 1e-7), -math.pi * (1 - 1e-7), ALU.min, ALU.max))

        reduced(rope["r"][:], rope["ang"][:])
        V.sem_inc(sem("rope_angle"), 1)
        step(V.tensor_scalar(rope["tmp"][:], rope["r"][:], math.pi / 2, None, ALU.add))
        reduced(rope["ang"][:], rope["tmp"][:])
        V.sem_inc(sem("rope_angle"), 1)
        dve.wait_ge(*reached("mla_q_copied", 4))
        dve.wait_ge(*reached("late_params", 32))
        dve.wait_ge(*reached("mla_kv_copied", 4))
        lo_to(UNITS_AT["w_ukv"] + 4)
        for t in range(TT):
            ins = V.tensor_copy(mk[:, t * HEADS:(t + 1) * HEADS, NOPE:QK],
                                tail[:, t, 384:416].unsqueeze(1).to_broadcast([P, HEADS, ROPE]))
        step(ins)
        msq_flat = msq[:].rearrange("p a b -> p (a b)")
        for i, (m, gain, scale) in enumerate(((mq, "mla_q_norm", QK ** -0.5), (mk, "mla_k_norm", 1.0))):
            st = [h[:, 16 * i:16 * i + 16] for h in heads_st]
            head_norm(m, 16, QK, msq_flat, st[0], st[1], st[2], "mla_head_ms", "mla_head_std", i + 1, row(gain, QK), scale)
            dve.wait_ge(*reached("rope_table", 1))
            H2 = ROPE // 2
            m4 = m.rearrange("p (t h) c -> p t h c", t=TT)
            t1, t2 = m4[:, :, :, NOPE:NOPE + H2], m4[:, :, :, NOPE + H2:QK]
            cosb = rope["cos"][:].unsqueeze(2).to_broadcast([P, TT, HEADS, H2])
            sinb = rope["sin"][:].unsqueeze(2).to_broadcast([P, TT, HEADS, H2])
            tmp = [msq_flat[:, 256 * j:256 * j + 256].rearrange("p (t h c) -> p t h c", t=TT, h=HEADS) for j in range(4)]
            V.tensor_tensor(tmp[0], t1, cosb, ALU.mult)
            V.tensor_tensor(tmp[1], t2, sinb, ALU.mult)
            V.tensor_tensor(tmp[2], t1, sinb, ALU.mult)
            step(V.tensor_tensor(tmp[3], t2, cosb, ALU.mult))
            V.tensor_tensor(t1, tmp[0], tmp[1], ALU.subtract)
            step(V.tensor_tensor(t2, tmp[2], tmp[3], ALU.add))
            V.sem_inc(sem("mla_rotated"), 1)
        attention("mla")
        dve.wait_ge(*reached("mla_ssq", TT))
        V.tensor_scalar(osq["ms"], osq["ssq"], 1.0 / HALF, EPS, ALU.mult, ALU.add).then_inc(sem("mla_ms"), 1)
        dve.wait_ge(*reached("mla_std", 1))
        step(V.reciprocal(osq["r"], osq["std"]))
        for t in range(TT):
            V.tensor_scalar(xn[:, t, 0:HALF], mo[:, t, :], osq["r"][:, t:t + 1], None, ALU.mult).then_inc(sem("mla_normed"), 1)
        for c in range(LC):
            dve.wait_ge(*reached("mla_oT_hi", 2 * (c // 2) + 2))
            V.scalar_tensor_tensor(out=hTl[:, LC + c, :], in0=ps[:, c // 2, (c % 2) * S:(c % 2) * S + S],
                                   scalar=col("mla_out_norm", c), in1=hTh[:, LC + c, :].bitcast(F32), op0=ALU.mult,
                                   op1=ALU.subtract).then_inc(sem("mla_oT"), 1)
        residual("mixer_x_change", 7, UNITS_AT["w_mem_kv"])

        norm("mem_attn_norm", UNITS_AT["w_mem_kv"] + 3)
        norm("mem_norm", 0)
        lo_to(UNITS_AT["w_mem_o"] + 3)
        dve.wait_ge(*reached("mem_in_copied", 6))
        for i, (m, scale) in enumerate(((eq, P ** -0.5), (ek, 1.0))):
            st = [h[:, 32 + 8 * i:40 + 8 * i] for h in heads_st]
            head_norm(m[:].rearrange("p t (h c) -> p (t h) c", h=MEM_HEADS), 8, P, esq[:].rearrange("p a b -> p (a b)"),
                      st[0], st[1], st[2], "mem_head_ms", "mem_head_std", i + 1, None, scale)
            V.sem_inc(sem("mem_heads_normed"), 1)
        attention("mem")
        oT_low("mem", 2)
        residual("memory_x_change", 5, UNITS_AT["w_up"])

        def low_hidden(stage, j):
            dve.wait_ge(*reached(stage + "_hid_hi", j + 1))
            V.tensor_tensor(hidl[:, j, :], sg[j % 4], hidh[:, j, :].bitcast(F32), ALU.subtract).then_inc(sem(stage + "_hid"), 1)

        norm("ffn_norm", UNITS_AT["w_up"] + 3)
        for f in range(FT + 2):
            if f < FT:
                dve.wait_ge(*reached("ffn_centre", f + 1))
                lo_to(UNITS_AT["w_up"] + f + 4)
                for tap in range(2):
                    for i in range(2):
                        w = col("ffn_conv_w", tap * 2 * 2 * FT + f + i * FT)
                        y, src = cv[f % 4][i], ps[:, f % 4, i * S:(i + 1) * S]
                        a, b = (slice(1, S), slice(0, S - 1)) if tap == 0 else (slice(0, S - 1), slice(1, S))
                        ins = V.scalar_tensor_tensor(out=y[:, a], in0=src[:, b], scalar=w, in1=y[:, a], op0=ALU.mult,
                                                     op1=ALU.add)
                    if tap == 0:
                        step(ins)
                ins.then_inc(sem("ffn_gated_read"), 1)
            if 1 <= f <= FT:
                j = f - 1
                dve.wait_ge(*reached("ffn_gated_sigmoid", j + 1))
                dve.wait_ge(*reached("ffn_gated_read", j + 1))
                step(V.tensor_tensor(sg[j % 4], sg[j % 4], cv[j % 4][0], ALU.mult))
                V.tensor_tensor(sg[j % 4], sg[j % 4], cv[j % 4][1], ALU.mult).then_inc(sem("ffn_product"), 1)
            if f >= 2:
                low_hidden("ffn", f - 2)
        residual("ffn_x_change", 14, UNITS_AT["attn_w_in"])

        norm("attn_norm_2", UNITS_AT["attn_w_in"] + 3)
        lists = ((dq, 12, 64, 0, 64 ** -0.5), (dk, 12, 64, 24, 1.0), (fq, 8, 32, 48, 32 ** -0.5), (fk, 8, 32, 64, 1.0))

        def head_squares(i, ready):
            m, h, w, o, scale = lists[i]
            n = TT * h
            buf = m[:].rearrange("p t (h c) -> p (t h) c", h=h)
            sq = dsq[:, 0:n * w].rearrange("p (a b) -> p a b", a=n)
            dve.wait_ge(*reached("attn_in_read", ready))
            step(V.tensor_tensor(sq, buf, buf, ALU.mult))
            step(V.tensor_reduce(attn_ms[:, o:o + n], sq, AX, ALU.add))
            V.tensor_scalar(attn_ms[:, o:o + n], attn_ms[:, o:o + n], 1.0 / (w * scale * scale), EPS / (scale * scale),
                            ALU.mult, ALU.add).then_inc(sem("attn_head_ms"), 1)

        def head_scale(i):
            m, h, w, o, scale = lists[i]
            n = TT * h
            buf = m[:].rearrange("p t (h c) -> p (t h) c", h=h)
            dve.wait_ge(*reached("attn_head_std", i + 1))
            step(V.reciprocal(attn_ms[:, o:o + n], attn_std[:, o:o + n]))
            V.tensor_tensor(buf, buf, attn_ms[:, o:o + n].unsqueeze(2).to_broadcast([P, n, w]),
                            ALU.mult).then_inc(sem("attn_heads_normed"), 1)

        at = UNITS_AT["attn_w_in"]
        lo_to(at + 8)
        dve.wait_ge(*reached("late_params", 32))
        for i in range(2):
            step(V.tensor_tensor(junk[:, 0:32], row(f"diff_lambda_q{i + 1}_2", 32), row(f"diff_lambda_k{i + 1}_2", 32), ALU.mult))
            V.tensor_reduce(lam4[:, i:i + 1], junk[:, 0:32], AX, ALU.add).then_inc(sem("lam_dots"), 1)
            dve.wait_ge(*reached("lam_dots", i + 1))
        lo_to(at + 9)
        head_squares(0, 4)
        lo_to(at + 11)
        head_scale(0)
        head_squares(1, 6)
        lo_to(at + 13)
        head_scale(1)
        lo_to(at + 15)
        head_squares(2, 12)
        head_squares(3, 12)
        head_scale(2)
        head_scale(3)
        dve.wait_ge(*reached("lam_exps", 1))
        step(V.tensor_tensor(lam4[:, 4:5], lam4[:, 3:4], lam4[:, 2:3], ALU.subtract))
        step(V.tensor_scalar(lam4[:, 4:5], lam4[:, 4:5], LAM_INIT, None, ALU.subtract))
        attention("dil")
        nm = att["dil"]["nmax"][:, 0:24].rearrange("p (g x) -> p g x", g=3)
        sm = att["dil"]["sum"][:, 0:24].rearrange("p (g x) -> p g x", g=3)
        al = alpha[:, 0].rearrange("p (g x) -> p g x", g=3)
        a2 = alpha[:, 1].rearrange("p (g x) -> p g x", g=3)
        step(V.tensor_tensor(a2[:, 0], nm[:, 0], nm[:, 1], ALU.min))
        step(V.tensor_tensor(a2[:, 0], a2[:, 0], nm[:, 2], ALU.min))
        V.tensor_tensor(al, a2[:, 0:1].to_broadcast([P, 3, 8]), nm, ALU.subtract).then_inc(sem("alpha_diff"), 1)
        dve.wait_ge(*reached("alpha_exp", 1))
        step(V.tensor_tensor(a2, al, sm, ALU.mult))
        step(V.tensor_tensor(a2[:, 0], a2[:, 0], a2[:, 1], ALU.add))
        step(V.tensor_tensor(a2[:, 0], a2[:, 0], a2[:, 2], ALU.add))
        step(V.reciprocal(a2[:, 0], a2[:, 0]))
        step(V.tensor_tensor(al, al, a2[:, 0:1].to_broadcast([P, 3, 8]), ALU.mult))
        af = alpha[:, 0].rearrange("p (h t) -> p t h", t=TT)
        for t in range(TT):
            o = xn[:, t, 0:768].rearrange("p (h v) -> p h v", v=64)
            ins = V.tensor_tensor(o, o, af[:, t, :].unsqueeze(2).to_broadcast([P, 12, 64]), ALU.mult)
        ins.then_inc(sem("attn_mixed"), 1)
        fo = xn[:, :, 768:1024]
        sqv = dsq[:, 0:512].rearrange("p (a b) -> p a b", a=TT)
        step(V.tensor_tensor(sqv, fo, fo, ALU.mult))
        st = [h[:, 48:56] for h in heads_st]
        step(V.tensor_reduce(st[0], dsq[:, 0:512].rearrange("p (a b) -> p a b", a=8), AX, ALU.add))
        k2 = (1.0 - LAM_INIT) ** 2
        V.tensor_scalar(st[0], st[0], 1.0 / (64 * k2), EPS / k2, ALU.mult, ALU.add).then_inc(sem("diff_ms"), 1)
        dve.wait_ge(*reached("diff_std", 1))
        step(V.reciprocal(st[2], st[1]))
        for t in range(TT):
            o = fo[:, t, :].rearrange("p (h v) -> p h v", v=64)
            step(V.tensor_tensor(o, o, st[2][:, 4 * t:4 * t + 4].unsqueeze(2).to_broadcast([P, 4, 64]), ALU.mult))
            ins = V.tensor_tensor(o, o, row("diff_out_gain_2", 64).unsqueeze(1).to_broadcast([P, 4, 64]), ALU.mult)
        ins.then_inc(sem("attn_mixed"), 1)
        oT_low("attn", 4)
        residual("attn_x_change", 7, UNITS_AT["ffn_gate_up"])

        norm("ffn_norm_2", UNITS_AT["ffn_gate_up"] + 3)
        for f in range(FT + 1):
            if f < FT:
                dve.wait_ge(*reached("ffn2_gated_sigmoid", f + 1))
                step(V.tensor_tensor(sg[f % 4], sg[f % 4], ps[:, f % 4, 0:S], ALU.mult))
                V.tensor_tensor(sg[f % 4], sg[f % 4], ps[:, f % 4, S:2 * S], ALU.mult).then_inc(sem("ffn2_gated_read"), 1)
                lo_to(UNITS_AT["ffn_gate_up"] + f + 4)
            if f >= 1:
                low_hidden("ffn2", f - 1)
        residual("ffn2_x_change", 14, UNITS_AT["hgrn_w_in"])

        dve.wait_ge(sem("router_hi"), 1)
        V.tensor_tensor(rl[:], col("moe_w_router_2", 0, KD * NE), rh[:].bitcast(F32), ALU.subtract).then_inc(sem("router_lo"), 1)
        V.tensor_tensor(lbs["d"], col("hgrn_lb_logits_2", 8, 8), col("hgrn_lb_logits_2", 0, 8),
                        ALU.subtract).then_inc(sem("lb_diff"), 1)
        norm("hgrn_norm_2", UNITS_AT["hgrn_w_in"] + 3)
        for g in range(8):
            dve.wait_ge(*reached("hgrn_q_sigmoid", g + 1))
            V.tensor_tensor(gq[:, g, :], gq[:, g, :], ps[:, g, 0:S], ALU.mult).then_inc(sem("hgrn_q_read"), 1)
            if g % 2 == 1:
                lo_to(UNITS_AT["hgrn_w_in"] + g // 2 + 4)
        dve.wait_ge(*reached("lb", 1))
        for g in range(8):
            dve.wait_ge(*reached("hgrn_in_read", g + 1))
            V.tensor_scalar(gB[:, g, :], gB[:, g, :], lbs["one_minus"][:, g:g + 1], lbs["lb"][:, g:g + 1], ALU.mult, ALU.add)
            ins = V.tensor_scalar(gk[:, g, :], gk[:, g, :], lbs["one_minus"][:, g:g + 1], None, ALU.mult)
            if g % 2 == 1:
                lo_to(UNITS_AT["hgrn_w_in"] + 4 + g // 2 + 4)
        step(ins)
        V.sem_inc(sem("hgrn_forget"), 1)
        lo_to(UNITS_AT["hgrn_w_out"] + 3)
        dve.wait_ge(*reached("hgrn_in_read", 16))
        dve.wait_ge(*reached("hgrn_logf", 1))
        V.memset(AT[:], 0.0)
        for h in range(HG_HEADS):
            ins = V.tensor_tensor_scan(gB[:, h, :], const("reset", S), gB[:, h, :], 0.0, ALU.mult, ALU.add)
        step(ins)

        def chunks(v):
            return v.rearrange("p h (c j) -> p (h c) j", j=CHUNK)

        causal = const("chunk_causal", P).bitcast(U32)
        for half in range(2):
            hs = slice(4 * half, 4 * half + 4)
            b16 = chunks(gB[:, hs, :])
            if half == 1:
                dve.wait_ge(*reached("hgrn_factors", 4))
            V.tensor_tensor(chunks(gD[:]), b16, b16[:, :, CHUNK // 2:CHUNK // 2 + 1].to_broadcast([P, 16, CHUNK]),
                            ALU.subtract).then_inc(sem("hgrn_d1"), 1)
            dve.wait_ge(*reached("hgrn_eq", 4 * half + 1))
            V.tensor_tensor(gQ[:], gQ[:], gq[:, hs, :], ALU.mult).then_inc(sem("hgrn_factors"), 1)
            dve.wait_ge(*reached("hgrn_eq", 4 * half + 2))
            V.tensor_tensor(gK[:], gK[:], gk[:, hs, :], ALU.mult).then_inc(sem("hgrn_factors"), 1)
            dve.wait_ge(*reached("hgrn_factors", 4 * half + 2))
            dve.wait_ge(*reached("hgrn_eq", 4 * half + 3))
            V.tensor_tensor(gq[:, hs, :], gq[:, hs, :], gD[:], ALU.mult).then_inc(sem("hgrn_factors"), 1)
            dve.wait_ge(*reached("hgrn_factors", 4 * half + 3))
            V.tensor_tensor(chunks(gD[:]), b16[:, :, CHUNK - 1:CHUNK].to_broadcast([P, 16, CHUNK]), b16,
                            ALU.subtract).then_inc(sem("hgrn_d2"), 1)
            dve.wait_ge(*reached("hgrn_eq", 4 * half + 4))
            V.tensor_tensor(gk[:, hs, :], gk[:, hs, :], gD[:], ALU.mult).then_inc(sem("hgrn_factors"), 1)
            dve.wait_ge(*reached("hgrn_scores", half + 1))
            for h in range(4):
                ins = V.copy_predicated(AT[:, 4 * half + h, :], causal, ps[:, 0, h * P:(h + 1) * P])
            ins.then_inc(sem("hgrn_masked"), 1)
            dve.wait_ge(*reached("hgrn_dec", half + 1))
            for c in range(3):
                for h in range(4):
                    dve.wait_ge(*reached("hgrn_kv", 12 * half + 4 * c + h + 1))
                    kv = ps[:, (3, 6, 7, 0)[h], 0:P]
                    if c == 0:
                        if half == 1:
                            dve.wait_ge(*reached("hgrn_o", 16))
                        V.tensor_copy(state[:, h, :], kv).then_inc(sem("hgrn_state"), 1)
                    else:
                        dve.wait_ge(*reached("hgrn_o", 16 * half + 4 * c + h + 1))
                        dve.wait_ge(*reached("hgrn_state", 12 * half + 4 * (c - 1) + h + 1))
                        V.scalar_tensor_tensor(out=state[:, h, :], in0=state[:, h, :], scalar=dec[:, 16 * half + 4 * h + c:16 * half + 4 * h + c + 1],
                                               in1=kv, op0=ALU.mult, op1=ALU.add).then_inc(sem("hgrn_state"), 1)
        dve.wait_ge(*reached("hgrn_o_copied", 4))
        o16 = xn[:].rearrange("p t (h v) -> p (t h) v", v=P)
        sqg = work[:, 0:2048].rearrange("p (a b) -> p a b", a=16)
        step(V.tensor_tensor(sqg, o16, o16, ALU.mult))
        st = [h[:, 0:16] for h in heads_st]
        step(V.tensor_reduce(st[0], sqg, AX, ALU.add))
        V.tensor_scalar(st[0], st[0], 1.0 / P, EPS, ALU.mult, ALU.add).then_inc(sem("hgrn_ms"), 1)
        dve.wait_ge(*reached("hgrn_std", 1))
        step(V.reciprocal(st[2], st[1]))
        step(V.tensor_tensor(o16, o16, st[2].unsqueeze(2).to_broadcast([P, 16, P]), ALU.mult))
        step(V.tensor_tensor(o16, o16, row("hgrn_out_gain_2", P).unsqueeze(1).to_broadcast([P, 16, P]), ALU.mult))
        V.tensor_tensor(xn[:], xn[:], gg[:], ALU.mult).then_inc(sem("hgrn_gated"), 1)
        oT_low("hgrn", 4)
        residual("hgrn_x_change", 7, N_FIXED)

        norm("moe_norm_2", N_FIXED + SPLIT)
        dve.wait_ge(sem("logits"), 1)
        V.tensor_copy(logitsT, ps[0:NE, 7, 0:S]).then_inc(sem("logits_read"), 1)
        dve.wait_ge(sem("moe_gain"), 16)
        V.tensor_tensor(xn[:], xn[:], moe_gain.unsqueeze(1).to_broadcast([P, TT, D]), ALU.mult).then_inc(sem("tokens_left"), 1)
        L, rank, s1, s2, tmp = (rt[:, i] for i in range(5))
        dve.wait_ge(sem("logits"), 2)
        step(V.tensor_copy(L, ps[:, 6, 0:TT * NE].rearrange("p (t e) -> p t e", t=TT)))
        g3 = [r[:].rearrange("p (t e j) -> p t e j", t=TT, e=NE) for r in rcmp]
        full = [P, TT, NE, NE]
        step(V.tensor_tensor(g3[0], L.unsqueeze(2).to_broadcast(full), L.unsqueeze(3).to_broadcast(full), ALU.is_gt))
        step(V.tensor_tensor(g3[1], L.unsqueeze(2).to_broadcast(full), L.unsqueeze(3).to_broadcast(full), ALU.is_equal))
        tie = const("tie", NE * NE)
        for t in range(TT):
            step(V.tensor_tensor(rcmp[1][:, t * 64:(t + 1) * 64], rcmp[1][:, t * 64:(t + 1) * 64], tie, ALU.mult))
        step(V.tensor_tensor(g3[0], g3[0], g3[1], ALU.add))
        step(V.tensor_reduce(rank, g3[0], AX, ALU.add))
        step(V.tensor_scalar(s1, rank, 2.0, None, ALU.is_lt))
        V.sem_inc(sem("selected"), 1)
        dve.wait_ge(sem("tokens_part"), 1)
        V.tensor_tensor(xn[:], xn[:], parts[0][:], ALU.subtract).then_inc(sem("tokens_left"), 1)
        s1 = xsel
        for s, r, v in ((s1, 0.0, "v1"), (s2, 1.0, "v2")):
            step(V.tensor_scalar(s, rank, r, None, ALU.is_equal))
            step(V.tensor_tensor(tmp, s, L, ALU.mult))
            step(V.tensor_reduce(rtv[v], tmp, AX, ALU.add))
        V.tensor_tensor(rtv["v2"], rtv["v2"], rtv["v1"], ALU.subtract).then_inc(sem("route_diff"), 1)
        dve.wait_ge(sem("tokens_part"), 2)
        step(V.tensor_tensor(parts[2][:], xn[:], parts[1][:], ALU.subtract))
        dve.wait_ge(*reached("route_exp", 1))
        step(V.tensor_scalar(rtv["w1"], rtv["ex"], 1.0, None, ALU.add))
        step(V.reciprocal(rtv["w1"], rtv["w1"]))
        step(V.tensor_tensor(rtv["w2"], rtv["w1"], rtv["ex"], ALU.mult))
        for t in range(TT):
            step(V.tensor_scalar(tmp[:, t, :], s1[:, t, :], rtv["w1"][:, t:t + 1], None, ALU.mult))
            step(V.scalar_tensor_tensor(out=gates[:, 0:NE, t], in0=s2[:, t, :], scalar=rtv["w2"][:, t:t + 1], in1=tmp[:, t, :],
                                        op0=ALU.mult, op1=ALU.add))
        dve.wait_ge(sem("slots_ps"), 1)
        sel = rt[:, 2]
        step(V.tensor_copy(tmp, ps[:, 7, 0:TT * NE].rearrange("p (t e) -> p t e", t=TT)))
        step(V.tensor_reduce(posf[:, 0:1], ps[:, 7, TT * NE:3 * NE], AX, ALU.max))
        step(V.tensor_scalar(over[:], posf[:, 0:1], float(P), None, ALU.is_gt))
        step(V.scalar_tensor_tensor(out=tmp, in0=tmp, scalar=1.0, in1=sel, op0=ALU.add, op1=ALU.mult))
        V.memset(slots[:, 2 * NE, :], -1.0)
        step(V.memset(gates[:, 2 * NE, :], 0.0))
        for t in range(TT):
            V.tensor_scalar(slots[:, 0:NE, t], tmp[:, t, :], -1.0, None, ALU.add)
            V.tensor_scalar(slots[:, NE:2 * NE, t], tmp[:, t, :], -1.0 - P, None, ALU.add)
            ins = V.tensor_copy(gates[:, NE:2 * NE, t], gates[:, 0:NE, t])
        step(ins)
        V.sem_inc(sem("routed"), 1)

        def choose(e):
            for t in range(TT):
                ins = V.tensor_scalar(G[:, t, :], slot, slots[:, bass.ds(e, 1), t], None, ALU.is_equal)
            ins.then_inc(sem("chosen"), 1)

        V.sem_inc(sem("hidden"), 2)
        V.sem_inc(sem("out_added"), 4)
        V.sem_inc(sem("y_copied"), 2)
        choose(0)

        def tokens_low(q, e):
            dve.wait_ge(sem("tokens_hi"), e * 2 + q + 1)
            V.tensor_tensor(xel[:, 4 * q:4 * q + 4, :], ps[:, 7, :].rearrange("p (a b) -> p a b", a=4),
                            xeh[:, 4 * q:4 * q + 4, :].bitcast(F32), ALU.subtract).then_inc(sem("bank7_free"), 1)

        for q in range(2):
            tokens_low(q, 0)

        def experts(first, last):
            with nc.vector.Fori(first, last) as e:
                def lo(j):
                    n = N_FIXED + j
                    dve.wait_ge(sem("hi_made"), e * E_UNITS + (n + 1))
                    V.tensor_tensor(wl[:, n % SPLIT, :], raw[:, n % RAW, :], wh[:, n % SPLIT, :].bitcast(F32),
                                    ALU.subtract).then_inc(sem("lo_made"), 1)

                def hidden_low(c):
                    dve.wait_ge(sem("hidden_hi"), e * ECH + c + 1)
                    V.tensor_tensor(ehl[c % 2][:], ps[:, 6, :].rearrange("p (a b) -> p a b", a=4),
                                    ehh[c % 2][:].bitcast(F32), ALU.subtract).then_inc(sem("expert_hid"), 1)

                for q, (what, c, half) in enumerate(EXPERT_ORDER):
                    if what == "up" and half == 1:
                        dve.wait_ge(sem("sigmoid"), e * ECH + c + 1)
                        if c >= 2:
                            dve.wait_ge(sem("hidden_transposed"), e * ECH + (c - 1))
                        V.tensor_tensor(eh[c % 2], esg, ps[:, 2 * (c % 2), :], ALU.mult).then_inc(sem("silu"), 1)
                        dve.wait_ge(sem("silu"), e * ECH + c + 1)
                        V.tensor_tensor(eh[c % 2], eh[c % 2], ps[:, 2 * (c % 2) + 1, :], ALU.mult).then_inc(sem("hidden"), 1)
                    if q < E_UNITS - 1:
                        lo(q + SPLIT)
                    if what == "gate" and half == 1 and c > 0:
                        hidden_low(c - 1)
                    if q == 12:
                        dve.wait_ge(sem("bank7_full"), e * 3 + 2)
                        for t in range(TT):
                            ins = V.tensor_scalar(Gw[:, t, :], slot, slots[:, bass.ds(e, 1), t], gates[:, bass.ds(e, 1), t],
                                                  ALU.is_equal, ALU.mult)
                        ins.then_inc(sem("weighted"), 1)
                        choose(e + 1)
                    if what == "down" and c == ECH - 2 and half == 1:
                        tokens_low(0, e + 1)
                        hidden_low(ECH - 1)
                        tokens_low(1, e + 1)
                dve.wait_ge(sem("unit_used"), e * E_UNITS + (E_UNITS + SPLIT))
                V.tensor_copy(y_e[:, HALF:D], ps[:, 5, :]).then_inc(sem("y_copied"), 1)
                dve.wait_ge(sem("out_added"), (e + 1) * 4)
                for i in range(4):
                    dve.wait_ge(sem("out_change"), e * 4 + (i + 1))
                    xs = x[:, i // 2, (i % 2) * HALF:(i % 2 + 1) * HALF]
                    V.tensor_tensor(xs, ps[:, (6, 7, 2, 3)[i], :], xs, ALU.add).then_inc(sem("out_added"), 1)
                lo(E_UNITS - 1 + SPLIT)

        experts(0, NE)
        dve.wait_ge(sem("out_added"), 4 * NE + 4)
        with nc.vector.If(nc.vector.value_load(over[0:1, 0:1], min_val=0, max_val=1)):
            experts(NE, 2 * NE)
            dve.wait_ge(sem("out_added"), 8 * NE + 4)
        V.sem_inc(sem("x_final"), 4)

    block_cm.__exit__(None, None, None)


def constants():
    c = np.zeros((P, N_CONST), np.float32)

    def put(name, v):
        v = np.asarray(v, np.float32).reshape(P, -1)
        c[:, CONST[name]:CONST[name] + v.shape[1]] = v

    p = np.arange(P)
    put("ident", np.eye(P))
    put("ones", np.ones((P, P)))
    put("inv_freq", np.broadcast_to(10000.0 ** (-np.arange(0, ROPE, 2) / ROPE), (P, ROPE // 2)))
    put("reset", np.broadcast_to(np.arange(S) % CHUNK != 0, (P, S)))
    put("chunk_causal", (p[:, None] % CHUNK) <= (p[None, :] % CHUNK))
    put("slot", np.broadcast_to(p, (P, P)))
    put("before", p[:, None] < p[None, :])
    put("tie", np.broadcast_to((np.arange(NE)[None, :] < np.arange(NE)[:, None]).reshape(1, -1), (P, NE * NE)))
    dist = []
    for window, dilation in ((128, 1), (512, 4), (2048, 16), (S, 1)):
        for t in range(TT):
            gap = (t * P + p)[:, None] - np.arange(P * (t + 1))[None, :]
            dist.append(np.where((gap >= 0) & (gap % dilation == 0) & (gap <= window), gap, FAR))
    put("dist", np.concatenate(dist, axis=1))
    return c


def by_feature(v, n):
    return np.moveaxis(np.asarray(v, np.float32).reshape(-1, n, P), 2, 0).reshape(P, -1)


def k_tiles(w):
    k, n = w.shape
    return w.reshape(k // P, P, n).transpose(1, 0, 2).reshape(P, -1)


def lay_out(a):
    f = {k: np.asarray(v) for k, v in a.items()}
    cols = np.zeros((P, N_COLS), np.float32)
    for name in COLS:
        v = f[name]
        n = {"ffn_conv_w": 2 * FT, "ffn_conv_b": 2 * FT}.get(name, max(1, v.shape[-1] // P))
        if name in ("dil_q_gain_2", "dil_k_gain_2", "diff_q_gain_2", "diff_k_gain_2"):
            m = np.tile(v.reshape(-1), P // v.size)[:, None]
        elif name == "moe_w_router_2":
            m = k_tiles(v[0])
        else:
            m = by_feature(v, n)
        cols[:, COLS[name]:COLS[name] + m.shape[1]] = m
    rows = np.zeros((1, N_ROWS), np.float32)
    for name in ROWS:
        rows[0, ROWS[name]:ROWS[name] + f[name].size] = f[name].reshape(-1)

    units = np.zeros((N_UNITS, P, UNIT), np.float32)

    def put(n, m):
        units[n, :, 0:m.shape[1]] = m

    def by_columns(at, w):
        for j in range(w.shape[1] // S):
            put(at + j, k_tiles(w[:, j * S:(j + 1) * S]))

    def by_halves(at, w, width=HALF):
        for j in range(w.shape[1] // width):
            for half in range(2):
                put(at + 2 * j + half, k_tiles(w[half * HALF:(half + 1) * HALF, j * width:(j + 1) * width]))

    def by_rows(at, w):
        for j in range(w.shape[0] // S):
            put(at + j, k_tiles(w[j * S:(j + 1) * S]))

    U = UNITS_AT
    w_in = f["w_in"][0]
    by_columns(U["w_in"], w_in[:, 0:2 * LRU_W])
    by_halves(U["w_in_tail"], w_in[:, 2 * LRU_W:], TAIL)
    put(U["w_uq"], k_tiles(f["w_uq"][0]))
    put(U["w_ukv"], k_tiles(f["w_ukv"][0]))
    by_rows(U["w_out"], f["w_out"][0])
    by_halves(U["w_mem_kv"], f["w_mem_kv"][0])
    by_halves(U["w_mem_q"], f["w_mem_q"][0])
    by_rows(U["w_mem_o"], f["w_mem_o"][0])
    w_up = f["w_up"][0]
    for name, gate, up in (("w_up", w_up[:, :D_FF], w_up[:, D_FF:]),
                           ("ffn_gate_up", f["ffn_w_gate_2"][0], f["ffn_w_up_2"][0])):
        for j in range(FT):
            cut = slice(P * j, P * (j + 1))
            put(U[name] + j, k_tiles(np.concatenate([gate[:, cut], up[:, cut]], axis=1)))
    by_rows(U["w_down"], f["w_down"][0])
    by_halves(U["attn_w_in"], f["attn_w_in_2"][0])
    by_rows(U["attn_w_out"], f["attn_w_out_2"][0])
    by_rows(U["ffn_w_down"], f["ffn_w_down_2"][0])
    by_columns(U["hgrn_w_in"], f["hgrn_w_in_2"][0][:, 0:2 * D])
    by_halves(U["hgrn_w_in"] + 8, f["hgrn_w_in_2"][0][:, 2 * D:])
    by_rows(U["hgrn_w_out"], f["hgrn_w_out_2"][0])
    for e in range(NE):
        for j, (what, c, half) in enumerate(EXPERT_ORDER):
            w = f[f"moe_w_{what}_2"][0, e]
            if what == "down":
                w = w[c * HALF + half * S:c * HALF + (half + 1) * S]
            else:
                w = w[half * HALF:(half + 1) * HALF, c * HALF:(c + 1) * HALF]
            put(N_FIXED + e * E_UNITS + j, k_tiles(w))
    gates = np.zeros((P, 2, 2, LC, P), np.float32)
    for i, name in enumerate(("lru_w_a", "lru_w_i")):
        w = f[name][0]
        for d in range(2):
            for c in range(LC):
                for b in range(2):
                    gates[64 * b:64 * b + 64, d, i, c, 64 * b:64 * b + 64] = w[d, 2 * c + b]

    def token_major(v):
        return np.ascontiguousarray(v.reshape(TT, P, -1).transpose(1, 0, 2))

    return {"units": units, "consts": constants(), "cols": cols, "rows": rows,
            "moe_gain": f["moe_norm_2"].reshape(1, D), "lru_w": gates.reshape(P, 16, P), "x": token_major(f["x"]),
            "mem": token_major(f["mem"]),
            "pos": np.ascontiguousarray(f["positions"].reshape(TT, P).T.astype(np.int32))}


def kernel(**inputs):
    import concourse.bacc as bacc
    from concourse.bass_utils import run_bass_kernel_spmd

    nc = bacc.Bacc("TRN2", target_bir_lowering=False, num_devices=1)
    arrays = lay_out(inputs)
    args = [nc.dram_tensor("in_" + name, a.shape, mybir.dt.from_np(a.dtype), kind="ExternalInput").ap()
            for name, a in arrays.items()]
    out = nc.dram_tensor("out", (P, TT, D), F32, kind="ExternalOutput").ap()
    build(nc, *args, out)
    r = run_bass_kernel_spmd(nc, [{"in_" + name: a for name, a in arrays.items()}], core_ids=[0])
    got = r.results[0]["out"]
    return np.ascontiguousarray(got.transpose(1, 0, 2)).reshape(1, S, D)
```

```python
import math

import numpy as np

import concourse.bass as bass
from concourse import mybir

F32 = mybir.dt.float32
I32 = mybir.dt.int32
U32 = mybir.dt.uint32
ALU = mybir.AluOpType
ACT = mybir.ActivationFunctionType
AX = mybir.AxisListType.X

P = 128
S = 256
WORK = 13312
TT = S // P
D = 1024
KD = D // P
EPS = 1e-6
HALF = 512
UNIT = 2048
RAW = 7
SPLIT = 3

LRU_W = 512
LC = LRU_W // P
Q_LORA, KV_LORA, ROPE = 256, 128, 32
HEADS, NOPE, QK, VD = 8, 64, 96, 64
TAIL = Q_LORA + KV_LORA + ROPE
D_FF = 2816
FT = D_FF // P
MEM_HEADS = 4
DIL_HEADS = 12
DIFF_HEADS = 4
HG_HEADS, CHUNK = 8, 64
NE, FE = 8, 3584
ECH = FE // HALF
E_UNITS = 6 * ECH
LAM_INIT = 0.8 - 0.6 * math.exp(-0.3 * 0)
FAR = 1.0e32


def offsets(sizes):
    at, out = 0, {}
    for name, n in sizes:
        out[name] = at
        at += n
    return out, at


CONST, N_CONST = offsets([("ident", P), ("ones", P), ("inv_freq", ROPE // 2), ("reset", S),
                          ("chunk_causal", P), ("tie", NE * NE), ("slot", P), ("before", P), ("dist", 4 * (P + S))])
COLS, N_COLS = offsets([("attn_norm", KD), ("mem_attn_norm", KD), ("mem_norm", KD), ("ffn_norm", KD),
                        ("attn_norm_2", KD), ("ffn_norm_2", KD), ("hgrn_norm_2", KD), ("moe_norm_2", KD),
                        ("q_a_norm", 2), ("kv_a_norm", 1), ("lru_out_norm", LC), ("mla_out_norm", LC),
                        ("mem_q_norm", 1), ("mem_k_norm", 1), ("lru_conv_w", 8 * LC), ("lru_conv_b", 2 * LC),
                        ("lru_b_a", 2 * LC), ("lru_b_i", 2 * LC), ("lru_lambda", 2 * LC),
                        ("ffn_conv_w", 3 * 2 * FT), ("ffn_conv_b", 2 * FT), ("hgrn_lb_logits_2", 2 * HG_HEADS),
                        ("moe_w_router_2", KD * NE), ("dil_q_gain_2", 1), ("dil_k_gain_2", 1), ("diff_q_gain_2", 1),
                        ("diff_k_gain_2", 1), ("mla_q_norm", 1), ("mla_k_norm", 1),
                        ("hgrn_out_gain_2", 1)])
ROWS, N_ROWS = offsets([("mla_q_norm", QK), ("mla_k_norm", QK), ("diff_lambda_q1_2", 32),
                        ("diff_lambda_k1_2", 32), ("diff_lambda_q2_2", 32), ("diff_lambda_k2_2", 32),
                        ("diff_out_gain_2", 64)])
F32R = mybir.dt.float32r

UNITS_AT, N_FIXED = offsets([("w_in", 4), ("w_in_tail", 2), ("w_mem_kv", 4), ("w_uq", 1), ("w_ukv", 1), ("w_out", 4),
                             ("w_mem_q", 2), ("w_mem_o", 2), ("w_up", FT), ("w_down", FT // 2), ("attn_w_in", 12),
                             ("attn_w_out", 4), ("ffn_gate_up", FT), ("ffn_w_down", FT // 2), ("hgrn_w_in", 16),
                             ("hgrn_w_out", 4)])
N_UNITS = N_FIXED + NE * E_UNITS
FIRST_RAW = N_FIXED % RAW
assert E_UNITS % RAW == 0 and E_UNITS % SPLIT == 0
EXPERT_ORDER = []
for _c in range(ECH + 1):
    if _c < ECH:
        EXPERT_ORDER += [("gate", _c, 0), ("gate", _c, 1), ("up", _c, 0), ("up", _c, 1)]
    if _c > 0:
        EXPERT_ORDER += [("down", _c - 1, 0), ("down", _c - 1, 1)]
UNIT_OF = {u: j for j, u in enumerate(EXPERT_ORDER)}
DIL_SLOPES = [2.0 ** (-8.0 * (h + 1) / 16) for h in range(16)]
NORMS = ["attn_norm", "mem_norm", "mem_attn_norm", "ffn_norm", "attn_norm_2", "ffn_norm_2", "hgrn_norm_2", "moe_norm_2"]


def build(nc, units_d, consts_d, cols_d, rows_d, moe_gain_d, lru_w_d, x_d, mem_d, pos_d, out_d):
    def sb(name, shape, dt=F32):
        return nc.alloc_sbuf_tensor(name, [P] + shape, dt)

    raw = sb("raw", [RAW, UNIT])
    wh = sb("wh", [SPLIT, UNIT], F32R)
    wl = sb("wl", [SPLIT, UNIT], F32R)
    x = sb("x", [TT, D])
    hT_at = nc.sbuf_base
    hTh = sb("hTh", [KD, S], F32R)
    hTl = sb("hTl", [KD, S], F32R)
    hP = nc.alloc_sbuf_tensor_at("hP", [P, KD, S], F32, offset=hT_at)
    xn = sb("xn", [TT, D])
    junk = sb("junk", [HALF])
    consts = sb("consts", [N_CONST])
    cols = sb("cols", [N_COLS])
    rows = sb("rows", [N_ROWS])
    pos = sb("pos", [TT], I32)
    small = sb("small", [416])
    work_at = nc.sbuf_base
    work = sb("work", [WORK])
    work_r = nc.alloc_sbuf_tensor_at("work_r", [P, WORK], F32R, offset=work_at)
    work_b = nc.alloc_sbuf_tensor_at("work_b", [P, 2 * WORK], mybir.dt.bfloat16, offset=work_at)
    ps = nc.alloc_psum_tensor("ps", [P, 8, HALF], F32)

    taken = [0]

    def tiny(n):
        taken[0] += n
        assert taken[0] <= 416
        return small[:, taken[0] - n:taken[0]]

    def area(at, *shape, of=None):
        n = int(np.prod(shape))
        assert at + n <= WORK
        v = (work if of is None else of)[:, at:at + n]
        if len(shape) == 2:
            v = v.rearrange("p (a b) -> p a b", a=shape[0])
        if len(shape) == 3:
            v = v.rearrange("p (a b c) -> p a b c", a=shape[0], b=shape[1])
        return v

    def const(name, n, at=0):
        return consts[:, CONST[name] + at:CONST[name] + at + n]

    def col(name, c, n=1):
        return cols[:, COLS[name] + c:COLS[name] + c + n]

    def row(name, n):
        return rows[:, ROWS[name]:ROWS[name] + n]

    ident = const("ident", P)
    ones = const("ones", P)

    sems = {}

    SHARED = {
        "oT_hi": dict(mla=4, mem=2, attn=4, hgrn=4), "hid_hi": dict(ffn=FT, ffn2=FT), "hid": dict(ffn=FT, ffn2=FT),
        "att_scores": (16, 8, 40), "att_max": (16, 8, 40), "att_probs": (16, 8, 40),
        "att_transposed": (16, 8, 40), "att_probsT": (16, 8, 40), "att_weighted": (16, 8, 40), "att_out": (16, 8, 40),
        "qkT_ps": dict(mla=8, mem=4, attn=8), "qkT": dict(mla=8, mem=8, attn=8),
        "oT_ps": dict(mla=2, mem=2, attn=4, hgrn=4), "oT": dict(mla=4, mem=2, attn=4, hgrn=4),
        "x_change": dict(mixer=7, memory=5, ffn=14, attn=7, ffn2=14, hgrn=7),
        "ms": dict(lru=1, latent=1, mem_k=1, mla_head=2, mla=1, mem_q=1, attn_head=4, diff=1, hgrn=2),
        "std": dict(lru=1, latent=1, mem_k=1, mla_head=2, mla=1, mem_q=1, attn_head=4, diff=1, hgrn=2),
        "gu": dict(ffn=FT, ffn2=FT), "gated_sigmoid": dict(ffn=FT, ffn2=FT), "gated_read": dict(ffn=FT, ffn2=FT),
    }
    place = {}
    for shared, parts in SHARED.items():
        start = 0
        for stage, n in (parts.items() if isinstance(parts, dict) else zip(("mla", "mem", "dil"), parts)):
            place[stage + "_" + shared] = (shared, start)
            start += n

    def sem(name):
        shared = place.get(name, (name, 0))[0]
        if shared not in sems:
            sems[shared] = nc.alloc_semaphore(shared)
        return sems[shared]

    def reached(name, value):
        return sem(name), value + place.get(name, (name, 0))[1]

    def tile_of(name, i):
        return reached(name, 3 * (i // TT) + 2 + i % TT)

    raw_loaded = [sem(f"raw_loaded{i}") for i in range(RAW)]
    released = {}

    tail = area(0, TT, TAIL)
    xrp = area(832, LC, S + 6)
    yg = area(1880, LC, S)
    xc = [area(2904 + 1024 * d, LC, S) for d in range(2)]
    ra = [area(4952 + 1024 * d, LC, S) for d in range(2)]
    ri = [area(7000 + 1024 * d, LC, S) for d in range(2)]
    th = [area(9048 + 1024 * d, LC, S) for d in range(2)]
    z = xrp.rearrange("p a b -> p (a b)")[:, 0:1024].rearrange("p (a b) -> p a b", a=4)
    root = [area(11264 + 1024 * d, LC, S) for d in range(2)]
    mq = area(832, 2 * HEADS, QK)
    mk = area(2368, 2 * HEADS, QK)
    mv = area(3904, TT, HEADS * VD)
    mqT = area(4928, HEADS, S)
    mkT = area(6976, HEADS, S)
    msq, msk = area(4928, 2 * HEADS, QK), area(6976, 2 * HEADS, QK)
    mo = area(9024, TT, HEADS * VD)
    cn = area(11616, TT, 384)
    cTh, cTl = area(10080, 3, S, of=work_r), area(10848, 3, S, of=work_r)
    lru_w = area(11264, 16, P)
    mem = xn
    mem_squares = area(7000, TT, D)
    xn_flat = xn[:].rearrange("p t d -> p (t d)")
    ek, ev = [xn_flat[:, TT * HALF * i:TT * HALF * (i + 1)].rearrange("p (t d) -> p t d", t=TT) for i in range(2)]
    eq = area(4096, TT, HALF)
    eqT, ekT = area(7168, MEM_HEADS, S), area(8192, MEM_HEADS, S)
    eo = area(9216, TT, HALF)
    esq = area(11776, TT, HALF)
    hidh, hidl = area(0, FT, S, of=work_r), area(5632, FT, S, of=work_r)
    cv = [[xn[:, b // 2, 512 * (b % 2) + 256 * i:512 * (b % 2) + 256 * (i + 1)] for i in range(2)] for b in range(4)]
    sg = [area(12288 + 256 * b, S) for b in range(4)]
    dq, dk, dv = area(0, TT, 768), area(1536, TT, 768), area(3072, TT, 768)
    fq, fk, fv = area(4608, TT, 256), area(5120, TT, 256), area(5632, TT, 256)
    dqT, dkT, fqT, fkT = area(6144, 6, S), area(7680, 6, S), area(9216, 2, S), area(9728, 2, S)
    dsq = area(11776, 1536)
    gq, gk, gB = area(0, HG_HEADS, S), area(2048, HG_HEADS, S), area(4096, HG_HEADS, S)
    gv, gg = area(6144, TT, D), area(8192, TT, D)
    gD, gQ, gK = area(10240, 4, S), area(11264, 4, S), area(12288, 4, S)
    kstT = hP[:, 0:4, :]
    AT = hP[:, 4:8, :].rearrange("p a b -> p (a b)").rearrange("p (h c) -> p h c", h=8)
    state = junk[:, 0:512].rearrange("p (h v) -> p h v", h=4)
    moe_gain = area(4096, D)
    parts = [work_b[:, 2048 * i:2048 * (i + 1)].rearrange("p (t d) -> p t d", t=TT) for i in range(3)]
    tokens = area(6144, TT, D)
    xeh, xel = area(4096, KD, P, of=work_r), area(5120, KD, P, of=work_r)
    ehh = [area(8192 + 512 * b, 4, P, of=work_r) for b in range(2)]
    ehl = [area(9216 + 512 * b, 4, P, of=work_r) for b in range(2)]
    eh = [area(10240 + 512 * b, HALF) for b in range(2)]
    esg = area(11264, HALF)
    y_e = area(11776, D)
    GT = area(12800, TT, P)
    G = work_b[:, 2 * 13056:2 * 13056 + TT * P].rearrange("p (t s) -> p t s", t=TT)
    Gw = junk[:, 0:256].rearrange("p (t s) -> p t s", t=TT)
    slot = const("slot", P)

    block_cm = nc.Block()
    block = block_cm.__enter__()

    ssq, msum, std, rstd = tiny(16), tiny(16), tiny(16), tiny(16)
    n_ssq = {}

    NORM_OF = {n: i for i, n in enumerate(NORMS)}
    X_AFTER = {"mixer": 4, "memory": 8, "ffn": 12, "attn2": 16, "ffn2": 20, "hgrn": 24}
    NORM_NEEDS = {"mem_attn_norm": 4, "ffn_norm": 8, "attn_norm_2": 12, "ffn_norm_2": 16, "hgrn_norm_2": 20,
                  "moe_norm_2": 24}

    def rows_of(name):
        return area(0, TT, D) if name == "mem_attn_norm" else xn

    def attention_units(stage):
        out = []
        if stage == "mla":
            for h in range(HEADS):
                for t in range(TT):
                    out.append(dict(q=mqT[0:QK, h, t * P:(t + 1) * P], k=mkT[0:QK, h, :], nk=S, dv=VD,
                                    v=[mv[:, j, h * VD:(h + 1) * VD] for j in range(2)], dist=None,
                                    out=mo[:, t, h * VD:(h + 1) * VD], kind="plain"))
        if stage == "mem":
            for h in range(MEM_HEADS):
                for t in range(TT):
                    out.append(dict(q=eqT[:, h, t * P:(t + 1) * P], k=ekT[:, h, :], nk=S, dv=P,
                                    v=[ev[:, j, h * P:(h + 1) * P] for j in range(2)], dist=None,
                                    out=eo[:, t, h * P:(h + 1) * P], kind="plain"))
        if stage == "dil":
            for h in range(DIL_HEADS):
                for t in range(TT):
                    b = 64 * (h % 2)
                    nk = P * (t + 1)
                    g = h // 4
                    out.append(dict(q=dqT[b:b + 64, h // 2, t * P:(t + 1) * P], k=dkT[b:b + 64, h // 2, 0:nk], nk=nk,
                                    dv=64, v=[dv[:, j, h * 64:(h + 1) * 64] for j in range(t + 1)],
                                    dist=const("dist", nk, g * (P + S) + t * P), slope=DIL_SLOPES[h],
                                    out=xn[:, t, h * 64:(h + 1) * 64], kind="raw"))
            for h in range(DIFF_HEADS):
                for t in range(TT):
                    for c in range(2):
                        b = 32 * ((2 * h + c) % 4)
                        a = (2 * h + c) // 4
                        nk = P * (t + 1)
                        out.append(dict(q=fqT[b:b + 32, a, t * P:(t + 1) * P], k=fkT[b:b + 32, a, 0:nk], nk=nk,
                                        dv=64, v=[fv[:, j, h * 64:(h + 1) * 64] for j in range(t + 1)],
                                        dist=const("dist", nk, 3 * (P + S) + t * P), slope=DIL_SLOPES[DIL_HEADS + h],
                                        out=xn[:, t, 768 + h * 64:768 + (h + 1) * 64],
                                        kind="plain" if c == 0 else "minus"))
        return out

    UNITS = {s: attention_units(s) for s in ("mla", "mem", "dil")}
    ATT_AT = {"mla": 10048, "mem": 10240, "dil": 10240}
    SCORE_BANK = (0, 1, 6)
    att = {}
    for s, at in ATT_AT.items():
        n = len(UNITS[s])
        att[s] = dict(s=[area(at + 256 * b, S) for b in range(3)], p=[area(at + 768 + 256 * b, S) for b in range(3)],
                      pT=[area(at + 1536 + 256 * b, S) for b in range(2)],
                      nmax=tiny(n), sum=tiny(n), inv=tiny(n))

    lam4 = tiny(8)
    warm = tiny(1)
    mla_gain = tiny(2)
    sp = {k: tiny(8) for k in ("a", "b", "c", "s", "s2", "p", "out")}
    lat = {k: tiny(4) for k in ("ssq", "ms", "std", "r")}
    osq = {k: tiny(2) for k in ("ssq", "ms", "std", "r")}
    heads_st = [sb(f"heads_st{i}", [64]) for i in range(3)]
    turn_by = [[[junk[:, 256 + 32 * (4 * i + 2 * half + k):288 + 32 * (4 * i + 2 * half + k)].rearrange("p (t c) -> p t c", t=TT)
                 for k in range(2)] for half in range(2)] for i in range(2)]
    rope = {k: area(13120 + 32 * i, TT, ROPE // 2) for i, k in enumerate(("ang", "k", "r", "sin", "cos", "tmp"))}
    lbs = {k: tiny(8) for k in ("d", "lb", "one_minus")}
    dec = tiny(32)
    attn_ms, attn_std = junk[:, 128:208], junk[:, 208:288]
    rh, rl = sb("rh", [KD * NE], F32R), sb("rl", [KD * NE], F32R)
    alpha = sb("alpha", [2, 24])
    rt = junk[:, 324:404].rearrange("p (i t e) -> p i t e", i=5, t=TT)
    rcmp = [area(12288 + 128 * i, TT * NE * NE) for i in range(2)]
    gates = junk[:, 256:290].rearrange("p (e t) -> p e t", t=TT)
    slots = junk[:, 290:324].rearrange("p (e t) -> p e t", t=TT)
    over = sb("over", [1], I32)
    logitsT = work[0:NE, 12288 + 2 * TT * NE * NE:12288 + 2 * TT * NE * NE + S]
    xsel = rcmp[1][:, 0:TT * NE].rearrange("p (t e) -> p t e", t=TT)
    rtv = {k: tiny(2) for k in ("v1", "v2", "ex", "w1", "w2")}
    posf = tiny(2)

    counts = {}

    def counted(ins, name, by=1):
        counts[name] = counts.get(name, 0) + by
        ins.then_inc(sem(name), by)

    @block.tensor
    def _(pe):
        def unit(n):
            pe.wait_ge(sem("lo_made"), n + 1)
            return wh[:, n % SPLIT, :], wl[:, n % SPLIT, :]

        def release(n, name):
            released[n] = reached(name, counts[name])

        def split_product(out, terms, first=True, last=True, ready=None):
            for j, (sh, sl, mh, ml) in enumerate(terms):
                if ready is not None:
                    ready(j)
                nc.tensor.matmul(out, sh, mh, start=(first and j == 0), stop=False)
                nc.tensor.matmul(out, sh, ml, start=False, stop=False)
                ins = nc.tensor.matmul(out, sl, mh, start=False, stop=(last and j == len(terms) - 1))
            return ins

        def by_k(w, k, n):
            return [p[:, 0:k * n].rearrange("p (k n) -> p k n", k=k) for p in w]

        def accumulate(out, pairs, first=True, last=True):
            for j, (l, r) in enumerate(pairs):
                ins = nc.tensor.matmul(out, l, r, start=(first and j == 0), stop=(last and j == len(pairs) - 1))
            return ins

        fresh = [0, 0]

        def norm(name):
            i = NORM_OF[name]
            pe.wait_ge(*reached("norm_xn", TT * (i + 1)))
            if i == 0:
                pe.wait_ge(*reached("params", 16 * 3))
            for g in range(4):
                for c2 in range(2):
                    for t in range(TT):
                        c = 2 * g + c2
                        ins = nc.tensor.transpose(ps[:, g, c2 * S + t * P:c2 * S + (t + 1) * P],
                                                  rows_of(name)[:, t, c * P:(c + 1) * P], ident)
                counted(ins, "norm_transposed")
            fresh[:] = [i, 0]

        def tile_ready(k):
            i, done = fresh
            if k >= done:
                fresh[1] = 2 * (k // 2) + 2
                pe.wait_ge(*reached("norm_out", KD * i + fresh[1]))

        def attention(stage):
            units = UNITS[stage]
            a = att[stage]
            n = len(units)
            for i in range(n + 3):
                if i < n:
                    u = units[i]
                    if i >= 3:
                        pe.wait_ge(*reached(stage + "_att_probs", i - 2))
                    counted(accumulate(ps[:, SCORE_BANK[i % 3], 0:u["nk"]], [(u["q"], u["k"])]), stage + "_att_scores")
                j = i - 2
                if 0 <= j < n:
                    u = units[j]
                    pe.wait_ge(*reached(stage + "_att_probs", j + 1))
                    if j >= 2:
                        pe.wait_ge(*reached(stage + "_att_probsT", j - 1))
                    for b in range(u["nk"] // P):
                        ins = nc.tensor.transpose(ps[:, 2 + j % 2, b * P:(b + 1) * P], a["p"][j % 3][:, b * P:(b + 1) * P],
                                                  ident)
                    counted(ins, stage + "_att_transposed")
                j = i - 3
                if 0 <= j < n:
                    u = units[j]
                    pe.wait_ge(*reached(stage + "_att_probsT", j + 1))
                    if j >= 2:
                        pe.wait_ge(*reached(stage + "_att_out", j - 1))
                    counted(accumulate(ps[:, 4 + j % 2, 0:u["dv"]],
                                       [(a["pT"][j % 2][:, b * P:(b + 1) * P], u["v"][b]) for b in range(u["nk"] // P)]),
                            stage + "_att_weighted")

        def project_out(stage, n0, nk, inh, inl, ready):
            for n in range(nk // 2):
                w = by_k(unit(n0 + n), 2, D)
                last = n == nk // 2 - 1
                ready(2 * n + 1)
                for t in range(TT):
                    for h in range(2):
                        ts, hs = slice(t * P, (t + 1) * P), slice(h * HALF, (h + 1) * HALF)
                        ins = split_product(ps[:, 4 + 2 * t + h, :],
                                            [(inh[:, 2 * n + k, ts], inl[:, 2 * n + k, ts], w[0][:, k, hs], w[1][:, k, hs])
                                             for k in range(2)], first=(n == 0), last=last)
                        if last or h == 1 and t == 1:
                            counted(ins, stage)
                release(n0 + n, stage)

        def feature_major(out, w, c):
            cs = slice(c * P, (c + 1) * P)
            return split_product(out, [(w[0][:, k, cs], w[1][:, k, cs], hTh[:, k, :], hTl[:, k, :]) for k in range(KD)],
                                 ready=tile_ready)

        def token_major(name, n0, srch, srcl, banks, width=HALF):
            for half in range(2):
                w = by_k(unit(n0 + half), KD // 2, width)
                for t in range(TT):
                    ts = slice(t * P, (t + 1) * P)
                    ks = [4 * half + k for k in range(4)]
                    ins = split_product(ps[:, banks[t], 0:width],
                                        [(srch[:, k, ts], srcl[:, k, ts], w[0][:, k - 4 * half, :], w[1][:, k - 4 * half, :])
                                         for k in ks], first=(half == 0), last=(half == 1),
                                        ready=lambda j: tile_ready(4 * half + j))
                    if half == 1 or t == 1:
                        counted(ins, name)
                release(n0 + half, name)

        def transposes(stage, blocks, banks, evacuated):
            for g in range(0, len(blocks), 4):
                b = banks[(g // 4) % len(banks)]
                if g // 4 >= len(banks):
                    pe.wait_ge(*reached(evacuated, g // 4 - len(banks) + 1))
                for j, src in enumerate(blocks[g:g + 4]):
                    w = src.shape[-1]
                    ins = nc.tensor.transpose(ps[0:w, b, j * P:(j + 1) * P], src, ident)
                counted(ins, stage)

        norm("attn_norm")
        for n in range(4):
            w = by_k(unit(UNITS_AT["w_in"] + n), KD, S)
            for c in range(2):
                counted(feature_major(ps[:, (4 + 2 * n + c) % 8, 0:S], w, c), "lru_in")
            release(UNITS_AT["w_in"] + n, "lru_in")
        pe.wait_ge(*reached("lru_in_copied", TT))
        token_major("tail", UNITS_AT["w_in_tail"], hTh, hTl, (4, 5), TAIL)
        pe.wait_ge(*reached("lru_in_copied", 2 * LC))
        norm("mem_norm")

        pe.wait_ge(*reached("lru_w_loaded", 16))
        pe.wait_ge(*reached("conv", 8 * 4))
        tile_ready(KD - 1)
        pe.wait_ge(*reached("tail_copied", TT))
        for d in range(2):
            for c in range(LC):
                for i in range(2):
                    ins = accumulate(ps[:, d * 4 + c, i * S:(i + 1) * S],
                                     [(lru_w[:, (d * 2 + i) * LC + c, :], xc[d][:, c, :])])
                counted(ins, "lru_gates")
        pe.wait_ge(*reached("lru_sigmoid", 8))
        token_major("mem_in", UNITS_AT["w_mem_kv"], hTh, hTl, (0, 1))
        token_major("mem_in", UNITS_AT["w_mem_kv"] + 2, hTh, hTl, (2, 3))
        pe.wait_ge(*reached("lru_sq", 1))
        pe.wait_ge(*reached("mem_in_copied", 4))
        counted(accumulate(ps[:, 0, 0:S], [(ones, th[0][:, c, :]) for c in range(LC)]), "lru_ssq")

        pe.wait_ge(*reached("latent_normed", 4))
        for c in range(3):
            for t in range(TT):
                ins = nc.tensor.transpose(ps[:, 1 + c // 2, (c % 2) * S + t * P:(c % 2) * S + (t + 1) * P],
                                          cn[:, t, c * P:(c + 1) * P], ident)
        counted(ins, "latent_transposed")
        pe.wait_ge(*reached("latentT", 3))
        w = by_k(unit(UNITS_AT["w_uq"]), 2, 768)
        for t in range(TT):
            for h in range(2):
                ts, hs = slice(t * P, (t + 1) * P), slice(h * 384, (h + 1) * 384)
                counted(split_product(ps[:, 4 + 2 * t + h, 0:384],
                                      [(cTh[:, k, ts], cTl[:, k, ts], w[0][:, k, hs], w[1][:, k, hs]) for k in range(2)]),
                        "mla_q")
        release(UNITS_AT["w_uq"], "mla_q")
        w = unit(UNITS_AT["w_ukv"])
        pe.wait_ge(*reached("lru_done", 1))
        for t in range(TT):
            for h in range(2):
                ts, hs = slice(t * P, (t + 1) * P), slice(h * HALF, (h + 1) * HALF)
                counted(split_product(ps[:, 2 * t + h, :], [(cTh[:, 2, ts], cTl[:, 2, ts], w[0][:, hs], w[1][:, hs])]),
                        "mla_kv")
        release(UNITS_AT["w_ukv"], "mla_kv")
        for i, m in enumerate((mq, mk)):
            pe.wait_ge(*reached("mla_rotated", i + 1))
            transposes("mla_qkT_ps", [m[:, t * HEADS + h, :] for h in range(HEADS) for t in range(TT)],
                       range(4 * i, 4 * i + 4), "")
        pe.wait_ge(*reached("mla_qkT", 8))
        attention("mla")
        pe.wait_ge(*reached("mla_normed", TT))
        transposes("mla_oT_ps", [mo[:, t, c * P:(c + 1) * P] for c in range(LC) for t in range(TT)], [0, 1], "")
        pe.wait_ge(*reached("mla_oT", LC))
        pe.wait_ge(*reached("lru_outT", 1))
        project_out("mixer_x_change", UNITS_AT["w_out"], KD, hTh, hTl, lambda k: None)

        norm("mem_attn_norm")
        token_major("mem_in", UNITS_AT["w_mem_q"], hTh, hTl, (4, 5))
        pe.wait_ge(*reached("mem_heads_normed", 2))
        transposes("mem_qkT_ps", [m[:, t, h * P:(h + 1) * P] for m in (eq, ek) for h in range(MEM_HEADS)
                                  for t in range(TT)], range(4), "")
        pe.wait_ge(*reached("mem_qkT", 8))
        attention("mem")
        pe.wait_ge(*reached("mem_att_out", 8))
        transposes("mem_oT_ps", [eo[:, t, c * P:(c + 1) * P] for c in range(4) for t in range(TT)], [0, 1], "")
        pe.wait_ge(*reached("mem_oT", 2))
        project_out("memory_x_change", UNITS_AT["w_mem_o"], 4, hTh, hTl, lambda k: None)

        def gated(stage, n0):
            for f in range(FT):
                w = by_k(unit(n0 + f), KD, S)
                if f >= 4:
                    pe.wait_ge(*reached(stage + "_gated_read", f - 3))
                for i in range(2):
                    ins = feature_major(ps[:, f % 4, i * S:(i + 1) * S], w, i)
                counted(ins, stage + "_gu")
                release(n0 + f, stage + "_gu")

        norm("ffn_norm")
        gated("ffn", UNITS_AT["w_up"])
        project_out("ffn_x_change", UNITS_AT["w_down"], FT, hidh, hidl, lambda k: pe.wait_ge(*reached("ffn_hid", k + 1)))

        norm("attn_norm_2")
        for j in range(6):
            if j >= 4:
                pe.wait_ge(*reached("attn_in_read", 2 * j - 6))
            token_major("attn_in", UNITS_AT["attn_w_in"] + 2 * j, hTh, hTl, ((2 * j) % 8, (2 * j + 1) % 8))
        pe.wait_ge(*reached("attn_in_read", 12))
        bank = 0
        for i, (m, n) in enumerate(((dq, 6), (dk, 6), (fq, 2), (fk, 2))):
            pe.wait_ge(*reached("attn_heads_normed", i + 1))
            transposes("attn_qkT_ps", [m[:, t, c * P:(c + 1) * P] for c in range(n) for t in range(TT)],
                       range(bank, bank + n // 2), "")
            bank += n // 2
        pe.wait_ge(*reached("attn_qkT", 8))
        attention("dil")
        pe.wait_ge(*reached("attn_mixed", 2))
        transposes("attn_oT_ps", [xn[:, t, c * P:(c + 1) * P] for c in range(KD) for t in range(TT)], range(4), "")
        pe.wait_ge(*reached("attn_oT", 4))
        project_out("attn_x_change", UNITS_AT["attn_w_out"], KD, hTh, hTl, lambda k: None)

        norm("ffn_norm_2")
        gated("ffn2", UNITS_AT["ffn_gate_up"])
        project_out("ffn2_x_change", UNITS_AT["ffn_w_down"], FT, hidh, hidl,
                    lambda k: pe.wait_ge(*reached("ffn2_hid", k + 1)))

        norm("hgrn_norm_2")
        for g in range(16):
            if g % 2 == 0:
                w = by_k(unit(UNITS_AT["hgrn_w_in"] + g // 2), KD, S)
            if g >= 8:
                pe.wait_ge(*reached("hgrn_q_read", g - 7))
            counted(feature_major(ps[:, g % 8, 0:S], w, g % 2), "hgrn_in")
            if g % 2 == 1:
                release(UNITS_AT["hgrn_w_in"] + g // 2, "hgrn_in")
        for j in range(4):
            pe.wait_ge(*reached("hgrn_in_read", 2 * j + 2))
            token_major("hgrn_in2", UNITS_AT["hgrn_w_in"] + 8 + 2 * j, hTh, hTl, (2 * j, 2 * j + 1))
        for half in range(2):
            pe.wait_ge(*reached("hgrn_in_read", 16))
            pe.wait_ge(*reached("hgrn_factors", 4 * half + 3))
            if half == 1:
                pe.wait_ge(*reached("hgrn_state", 12))
            for h in range(4):
                for c in range(4):
                    q0 = 64 * (c % 2)
                    for m, lo in ((32, 0), (64, 32)):
                        col0 = h * P + (c // 2) * 64 + lo
                        ins = nc.tensor.matmul(ps[q0:q0 + m, 0, col0:col0 + 32], gK[:, h, c * 64:c * 64 + m],
                                               gQ[:, h, c * 64 + lo:c * 64 + lo + 32], start=True, stop=True)
            counted(ins, "hgrn_scores")
            pe.wait_ge(*reached("hgrn_factors", 4 * half + 4))
            for h in range(4):
                for t in range(TT):
                    ins = nc.tensor.transpose(ps[:, 1 + h // 2, (h % 2) * S + t * P:(h % 2) * S + (t + 1) * P],
                                              gk[:, 4 * half + h, t * P:(t + 1) * P], ident)
            counted(ins, "hgrn_keysT")
            pe.wait_ge(*reached("hgrn_keysT_copied", 2 * (half + 1)))
            pe.wait_ge(*reached("hgrn_masked", half + 1))
            if half == 1:
                pe.wait_ge(*reached("hgrn_o_copied", 2))
            for c in range(4):
                q0, t = 64 * (c % 2), c // 2
                for h in range(4):
                    head = 4 * half + h
                    v = gv[q0:q0 + 64, t, head * P:(head + 1) * P]
                    o = ps[q0:q0 + 64, 4 + h // 2, (h % 2) * S + t * P:(h % 2) * S + (t + 1) * P]
                    ins = nc.tensor.matmul(o, AT[q0:q0 + 64, head, t * 64:(t + 1) * 64], v, start=True, stop=(c == 0))
                    if c > 0:
                        pe.wait_ge(*reached("hgrn_state", 12 * half + 4 * (c - 1) + h + 1))
                        ins = nc.tensor.matmul(o, gq[:, head, c * 64:(c + 1) * 64], state[:, h, :], start=False,
                                               stop=True)
                    counted(ins, "hgrn_o")
                if c < 3:
                    for h in range(4):
                        head = 4 * half + h
                        if c > 0 or half > 0:
                            pe.wait_ge(*reached("hgrn_state", 12 * half + 4 * c + h - 3))
                        counted(nc.tensor.matmul(ps[:, (3, 6, 7, 0)[h], 0:P], kstT[q0:q0 + 64, h, t * P:(t + 1) * P],
                                                 gv[q0:q0 + 64, t, head * P:(head + 1) * P], start=True, stop=True),
                                "hgrn_kv")
        pe.wait_ge(*reached("hgrn_o_copied", 4))
        for half in range(2):
            pe.wait_ge(*reached("hgrn_gated", half + 1))
            transposes("hgrn_oT_ps", [xn[:, t, c * P:(c + 1) * P] for c in range(4 * half, 4 * half + 4) for t in range(TT)],
                       range(2 * half, 2 * half + 2), "")
        pe.wait_ge(*reached("hgrn_oT", 4))
        project_out("hgrn_x_change", UNITS_AT["hgrn_w_out"], KD, hTh, hTl, lambda k: None)

        norm("moe_norm_2")
        pe.wait_ge(sem("router_lo"), 1)
        split_product(ps[0:NE, 7, 0:S], [(rh[:, k * NE:(k + 1) * NE], rl[:, k * NE:(k + 1) * NE], hTh[:, k, :], hTl[:, k, :])
                                         for k in range(KD)], ready=tile_ready).then_inc(sem("logits"), 1)
        pe.wait_ge(sem("logits_read"), 1)
        for t in range(TT):
            ins = nc.tensor.transpose(ps[:, 6, t * NE:(t + 1) * NE], logitsT[:, t * P:(t + 1) * P], ident[0:NE, 0:NE])
        ins.then_inc(sem("logits"), 1)
        pe.wait_ge(sem("selected"), 1)
        before = const("before", P)
        sel = rt[:, 2]
        accumulate(ps[:, 7, 0:NE], [(before, sel[:, 0, :])])
        accumulate(ps[:, 7, NE:2 * NE], [(ones, sel[:, 0, :]), (before, sel[:, 1, :])])
        accumulate(ps[:, 7, 2 * NE:3 * NE], [(ones, sel[:, 0, :]), (ones, sel[:, 1, :])]).then_inc(sem("slots_ps"), 1)
        pe.wait_ge(sem("routed"), 1)
        pe.sem_inc(sem("unit_used"), 3)

        def gather(q, value):
            pe.wait_ge(sem("chosen"), value + 1)
            if isinstance(value, int):
                pe.wait_ge(sem("tokens_left"), 3)
            if not (isinstance(value, int) and value == 0 and q == 0):
                pe.wait_ge(sem("bank7_free"), value * 3 + q)
            for d in range(4):
                c = 4 * q + d
                for t in range(TT):
                    for i in range(3):
                        ins = nc.tensor.matmul(ps[:, 7, d * P:(d + 1) * P], parts[i][:, t, c * P:(c + 1) * P], G[:, t, :],
                                               start=(t == 0 and i == 0), stop=(t == TT - 1 and i == 2))
            ins.then_inc(sem("bank7_full"), 1)

        def experts(first, last):
            with nc.tensor.Fori(first, last) as e:
                def unit_of(what):
                    j = UNIT_OF[what]
                    pe.wait_ge(sem("lo_made"), e * E_UNITS + (N_FIXED + j + 1))
                    s = (N_FIXED + j) % SPLIT
                    n = HALF if what[0] != "down" else D
                    return by_k((wh[:, s, :], wl[:, s, :]), UNIT // n, n)

                for c in range(ECH + 1):
                    b = 2 * (c % 2)
                    if c < ECH:
                        if c == 0:
                            pe.wait_ge(sem("bank7_free"), e * 3 + 2)
                        pe.wait_ge(sem("hidden"), e * ECH + (c + 1))
                        if c == 1:
                            pe.wait_ge(sem("out_added"), (e + 1) * 4)
                    for i, what in enumerate(("gate", "up")):
                        if c == ECH:
                            break
                        if i == 1 and c > 0:
                            transposed(e, c - 1)
                        for half in range(2):
                            w = unit_of((what, c, half))
                            ks = [4 * half + k for k in range(4)]
                            ins = split_product(ps[:, b + i, :],
                                                [(xeh[:, k, :], xel[:, k, :], w[0][:, k - 4 * half, :], w[1][:, k - 4 * half, :])
                                                 for k in ks], first=(half == 0), last=(half == 1))
                            ins.then_inc(sem("unit_used"), 1)
                    if c == ECH:
                        transposed(e, c - 1)
                        gather(1, e + 1)
                    if c > 0:
                        d = c - 1
                        if c == ECH - 1:
                            pe.wait_ge(sem("weighted"), e + 1)
                            pe.wait_ge(sem("bank7_free"), e * 3 + 2)
                            for t in range(TT):
                                ins = nc.tensor.transpose(ps[:, 7, t * P:(t + 1) * P], Gw[:, t, :], ident)
                            ins.then_inc(sem("bank7_full"), 1)
                        pe.wait_ge(sem("expert_hid"), e * ECH + d + 1)
                        if d == 0:
                            pe.wait_ge(sem("y_copied"), (e + 1) * 2)
                        for half in range(2):
                            w = unit_of(("down", d, half))
                            for h in range(2):
                                hs = slice(h * HALF, (h + 1) * HALF)
                                ins = split_product(ps[:, 4 + h, :],
                                                    [(ehh[d % 2][:, 2 * half + k, :], ehl[d % 2][:, 2 * half + k, :],
                                                      w[0][:, k, hs], w[1][:, k, hs]) for k in range(2)],
                                                    first=(d == 0 and half == 0), last=(d == ECH - 1 and half == 1))
                            ins.then_inc(sem("unit_used"), 1)
                        if c == ECH - 1:
                            gather(0, e + 1)
                pe.wait_ge(sem("y_copied"), (e + 2) * 2)
                pe.wait_ge(sem("bank7_free"), e * 3 + 5)
                for t in range(TT):
                    for h in range(2):
                        nc.tensor.matmul(ps[:, (6, 7, 2, 3)[2 * t + h], :], GT[:, t, :], y_e[:, h * HALF:(h + 1) * HALF],
                                         start=True, stop=True).then_inc(sem("out_change"), 1)

        def transposed(e, c):
            pe.wait_ge(sem("hidden"), e * ECH + (c + 3))
            if c == 0:
                pe.wait_ge(sem("out_added"), (e + 1) * 4)
            else:
                pe.wait_ge(sem("expert_hid"), e * ECH + c)
            for f in range(4):
                ins = nc.tensor.transpose(ps[:, 6, f * P:(f + 1) * P], eh[c % 2][:, f * P:(f + 1) * P], ident)
            ins.then_inc(sem("hidden_transposed"), 1)

        for q in range(2):
            gather(q, 0)
        experts(0, NE)
        with nc.tensor.If(nc.tensor.value_load(over[0:1, 0:1], min_val=0, max_val=1)):
            experts(NE, 2 * NE)

    @block.sync
    def _(sp_):
        sp_.dma_start(x[:], x_d).then_inc(sem("x_loaded"), 16)
        small_consts = CONST["dist"]
        sp_.dma_start(cols[:], cols_d).then_inc(sem("params"), 16)
        sp_.dma_start(consts[:, 0:small_consts], consts_d[:, 0:small_consts]).then_inc(sem("params"), 16)
        sp_.dma_start(pos[:], pos_d).then_inc(sem("params"), 16)

        def load(n, slot_n, source):
            sp_.dma_start(raw[:, slot_n % RAW, :], source).then_inc(raw_loaded[slot_n % RAW], 16)

        head = RAW + FIRST_RAW
        for n in range(head):
            if n >= RAW:
                sp_.wait_ge(sem("lo_made"), n - RAW + 1)
            load(n, n, units_d[n])
            if n == 3:
                sp_.dma_start(lru_w[:], lru_w_d).then_inc(sem("lru_w_loaded"), 16)
            if n == RAW - 1:
                sp_.wait_ge(*reached("norm_transposed", 4))
                sp_.dma_start(mem[:], mem_d).then_inc(sem("mem_loaded"), 16)
                sp_.dma_start(rows[:], rows_d.partition_broadcast(P)).then_inc(sem("late_params"), 16)
                sp_.dma_start(consts[:, small_consts:], consts_d[:, small_consts:]).then_inc(sem("late_params"), 16)
        assert (N_UNITS - head) % RAW == 0
        with nc.sync.Fori(0, (N_UNITS - head) // RAW) as g:
            for j in range(RAW):
                sp_.wait_ge(sem("lo_made"), g * RAW + (head + j - RAW + 1))
                load(None, head + j, units_d[g * RAW + (head + j)])

        def follow(n, source):
            sp_.wait_ge(sem("lo_made"), n - RAW + 1)
            load(None, n, units_d[source])

        for j in range(SPLIT):
            follow(N_UNITS + j, N_FIXED + j)
        sp_.wait_ge(sem("routed"), 1)
        with nc.sync.If(nc.sync.value_load(over[0:1, 0:1], min_val=0, max_val=1)):
            groups = (NE * E_UNITS - SPLIT) // RAW
            with nc.sync.Fori(0, groups) as g:
                for j in range(RAW):
                    n = N_UNITS + SPLIT + j
                    sp_.wait_ge(sem("lo_made"), g * RAW + (n - RAW + 1))
                    load(None, n, units_d[g * RAW + (N_FIXED + SPLIT + j)])
            for j in range(SPLIT + groups * RAW, NE * E_UNITS + SPLIT):
                follow(N_UNITS + j, N_FIXED + j % (NE * E_UNITS))
        for t in range(TT):
            sp_.wait_ge(*reached("x_final", 4))
            sp_.dma_start(out_d[:, t, :], x[:, t, :]).then_inc(sem("stored"), 16)
        sp_.wait_ge(*reached("stored", 16 * TT))

    @block.scalar
    def _(act):
        A = nc.scalar.activation
        made = [0]

        def hi_to(m):
            for n in range(made[0], m):
                act.wait_ge(raw_loaded[n % RAW], 16 * (n // RAW + 1))
                if n >= SPLIT:
                    act.wait_ge(*released[n - SPLIT])
                A(wh[:, n % SPLIT, :], raw[:, n % RAW, :], ACT.Copy).then_inc(sem("hi_made"), 1)
            made[0] = max(made[0], m)

        def norm(name, ahead):
            i = NORM_OF[name]
            src = mem if name == "mem_norm" else x
            if name == "attn_norm":
                act.wait_ge(*reached("x_loaded", 16))
            elif name == "mem_norm":
                act.wait_ge(*reached("mem_loaded", 16))
            else:
                A(warm, ones[:, 0:1], ACT.Sqrt)
            for t in range(TT):
                if name in NORM_NEEDS:
                    act.wait_ge(*reached("x_ready", NORM_NEEDS[name] - (2 if t == 0 else 0)))
                squares = mem_squares if name == "mem_norm" else rows_of(name)
                A(squares[:, t, :], src[:, t, :], ACT.Square, accum_out=ssq[:, 2 * i + t:2 * i + t + 1]).then_inc(sem("norm_ssq"), 1)
            act.wait_ge(*reached("norm_ms", i + 1))
            A(std[:, 2 * i:2 * i + 2], msum[:, 2 * i:2 * i + 2], ACT.Sqrt).then_inc(sem("norm_std"), 1)
            if i == 0:
                hi_to(1)
                act.wait_ge(*reached("params", 16 * 3))
            for c in range(KD):
                act.wait_ge(*reached("norm_transposed", 4 * i + c // 2 + 1))
                A(hTh[:, c, :], ps[:, c // 2, (c % 2) * S:(c % 2 + 1) * S], ACT.Identity,
                  scale=col(name, c)).then_inc(sem("norm_hi"), 1)
            hi_to(ahead)

        def sqrt_of(dst, src, ready, done):
            act.wait_ge(*reached(ready, 1))
            A(dst, src, ACT.Sqrt).then_inc(sem(done), 1)

        def attention(stage):
            a = att[stage]
            units = UNITS[stage]
            n = len(units)
            for i in range(n + 2):
                if stage == "dil" and i == DIL_HEADS * TT + 5:
                    act.wait_ge(*reached("alpha_diff", 1))
                    A(alpha[:, 0], alpha[:, 0], ACT.Exp).then_inc(sem("alpha_exp"), 1)
                j = i - 2
                if j >= 0:
                    u = units[j]
                    act.wait_ge(*reached(stage + "_att_transposed", j + 1))
                    if j >= 2:
                        act.wait_ge(*reached(stage + "_att_weighted", j - 1))
                    A(a["pT"][j % 2][:, 0:u["nk"]], ps[:, 2 + j % 2, 0:u["nk"]], ACT.Copy).then_inc(sem(stage + "_att_probsT"), 1)
                if i < n:
                    u = units[i]
                    act.wait_ge(*reached(stage + "_att_max", i + 1))
                    if i >= 3:
                        act.wait_ge(*reached(stage + "_att_transposed", i - 2))
                    src = ps[:, SCORE_BANK[i % 3], 0:u["nk"]] if u["dist"] is None else a["s"][i % 3][:, 0:u["nk"]]
                    ins = A(a["p"][i % 3][:, 0:u["nk"]], src, ACT.Exp, bias=a["nmax"][:, i:i + 1],
                            accum_out=a["sum"][:, i:i + 1])
                    ins.then_inc(sem(stage + "_att_probs"), 1)

        def oT_high(stage, groups, gain=1.0):
            for g in range(groups):
                act.wait_ge(*reached(stage + "_oT_ps", g + 1))
                A(hTh[:, 2 * g:2 * g + 2, :], ps[:, g, :].rearrange("p (a b) -> p a b", a=2), ACT.Identity,
                  scale=gain).then_inc(sem(stage + "_oT_hi"), 1)

        norm("attn_norm", 3)
        act.wait_ge(*reached("lam_abs", 1))
        A(sp["b"], sp["a"], ACT.Exp, scale=-1.0).then_inc(sem("lam_exp"), 1)
        for j in range(2 * LC):
            act.wait_ge(*reached("lru_in", j + 1))
            c = j % LC
            dst = xrp[:, c, 3:3 + S] if j < LC else yg[:, c, :]
            A(dst, ps[:, (4 + j) % 8, 0:S], ACT.Copy).then_inc(sem("lru_in_copied"), 1)
            if j % 2 == 1:
                hi_to(j // 2 + 4)
        norm("mem_norm", UNITS_AT["w_mem_kv"] + 3)
        for t in range(TT):
            act.wait_ge(*tile_of("tail", t))
            A(tail[:, t, :], ps[:, 4 + t, 0:TAIL], ACT.Copy).then_inc(sem("tail_copied"), 1)

        def mem_copied(j):
            act.wait_ge(*tile_of("mem_in", j))
            A((ek, ev, eq)[j // 2][:, j % 2, :], ps[:, j, :], ACT.Copy).then_inc(sem("mem_in_copied"), 1)

        for d in range(2):
            for c in range(LC):
                act.wait_ge(*reached("lru_gates", d * LC + c + 1))
                A(ra[d][:, c, :], ps[:, d * 4 + c, 0:S], ACT.Sigmoid, bias=col("lru_b_a", d * LC + c))
                A(ri[d][:, c, :], ps[:, d * 4 + c, S:2 * S], ACT.Sigmoid,
                  bias=col("lru_b_i", d * LC + c)).then_inc(sem("lru_sigmoid"), 1)
        act.wait_ge(*reached("gelu_z", 1))
        A(z, z, ACT.Sigmoid, scale=2.0 * math.sqrt(2.0 / math.pi)).then_inc(sem("gelu_sig"), 1)
        act.wait_ge(*reached("softplus", 1))
        act.wait_ge(*reached("lru_sigmoid", 8))
        for d in range(2):
            for c in range(LC):
                s = sp["out"][:, d * LC + c:d * LC + c + 1]
                A(th[d][:, c, :], ra[d][:, c, :], ACT.Tanh, scale=s).then_inc(sem("lru_tanh"), 1)
        act.wait_ge(*reached("lru_tanh", 8))
        hi_to(UNITS_AT["w_mem_kv"] + 4)
        for d in range(2):
            A(root[d], th[d][:], ACT.Ln, scale=-1.0, bias=ones[:, 0:1]).then_inc(sem("lru_ln"), 1)
        for d in range(2):
            act.wait_ge(*reached("lru_ln", d + 1))
            A(root[d], root[d], ACT.Exp, scale=-0.5).then_inc(sem("lru_root"), 1)
        mem_copied(0)
        mem_copied(1)
        hi_to(UNITS_AT["w_uq"] + 1)
        for d in range(2):
            for c in range(LC):
                s = sp["out"][:, d * LC + c:d * LC + c + 1]
                A(ra[d][:, c, :], ra[d][:, c, :], ACT.Exp, scale=s).then_inc(sem("lru_a"), 1)
        for d in range(2):
            act.wait_ge(*reached("lru_ln", 2))
            A(th[d][:], th[d][:], ACT.Sqrt, scale=-2.0).then_inc(sem("lru_mult"), 1)
        hi_to(UNITS_AT["w_ukv"] + 1)
        mem_copied(2)
        mem_copied(3)
        hi_to(UNITS_AT["w_ukv"] + 2)
        act.wait_ge(*reached("lru_gated", 1))
        A(th[0][:], ri[0][:], ACT.Square).then_inc(sem("lru_sq"), 1)
        sqrt_of(ri[1][:, 0, :], ri[1][:, 1, :], "lru_ms", "lru_std")
        for j, (t, a, b) in enumerate(((0, 0, 256), (1, 0, 256), (0, 256, 384), (1, 256, 384))):
            if j == 0:
                act.wait_ge(*reached("tail_copied", TT))
                act.wait_ge(*reached("norm_ssq", 2))
            else:
                act.wait_ge(*reached("latent_ssq", j))
            A(junk[:, 0:b - a], tail[:, t, a:b], ACT.Square, accum_out=lat["ssq"][:, j:j + 1]).then_inc(sem("latent_ssq"), 1)
        sqrt_of(lat["std"], lat["ms"], "latent_ms", "latent_std")
        act.wait_ge(*reached("lru_scaled", LC))
        A(hTh[:, 0:LC, :], th[0][:], ACT.Copy).then_inc(sem("lru_hi"), 1)
        act.wait_ge(*reached("latent_transposed", 1))
        for c in range(3):
            g = col("q_a_norm", c) if c < 2 else col("kv_a_norm", 0)
            A(cTh[:, c, :], ps[:, 1 + c // 2, (c % 2) * S:(c % 2) * S + S], ACT.Identity,
              scale=g).then_inc(sem("latent_hi"), 1)
        for t in range(TT):
            A(mk[:, t * HEADS:(t + 1) * HEADS, NOPE:QK], tail[:, t, 384:416].unsqueeze(1).to_broadcast([P, HEADS, ROPE]),
              ACT.Copy)
        for t in range(TT):
            for h in range(2):
                act.wait_ge(*reached("mla_q", 2 * t + h + 1))
                A(mq[:, t * HEADS + 4 * h:t * HEADS + 4 * h + 4, :],
                  ps[:, 4 + 2 * t + h, 0:384].rearrange("p (a b) -> p a b", a=4), ACT.Copy).then_inc(sem("mla_q_copied"), 1)
        for t in range(TT):
            for h in range(2):
                act.wait_ge(*reached("mla_kv", 2 * t + h + 1))
                kv = ps[:, 2 * t + h, :].rearrange("p (a b) -> p a b", a=4)
                A(mk[:, t * HEADS + 4 * h:t * HEADS + 4 * h + 4, 0:NOPE], kv[:, :, 0:NOPE], ACT.Copy)
                A(mv[:, t, h * 256:(h + 1) * 256].rearrange("p (a b) -> p a b", a=4), kv[:, :, NOPE:NOPE + VD],
                  ACT.Copy).then_inc(sem("mla_kv_copied"), 1)
        act.wait_ge(*reached("mla_q_copied", 4))
        A(msq[:], mq[:], ACT.Square).then_inc(sem("mla_squares"), 1)
        act.wait_ge(*reached("mla_kv_copied", 4))
        A(msk[:], mk[:], ACT.Square).then_inc(sem("mla_squares"), 1)
        act.wait_ge(*reached("rope_angle", 2))
        A(rope["sin"][:], rope["r"][:], ACT.Sin)
        A(rope["cos"][:], rope["ang"][:], ACT.Sin).then_inc(sem("rope_table"), 1)
        sqrt_of(heads_st[1][:, 40:48], heads_st[0][:, 40:48], "mem_k_ms", "mem_k_std")
        for i in range(2):
            act.wait_ge(*reached("mla_head_ms", i + 1))
            A(heads_st[1][:, 16 * i:16 * i + 16], heads_st[0][:, 16 * i:16 * i + 16], ACT.Sqrt).then_inc(sem("mla_head_std"), 1)
        hi_to(UNITS_AT["w_ukv"] + 4)
        for g in range(8):
            act.wait_ge(*reached("mla_qkT_ps", g + 1))
            dst = (mqT if g < 4 else mkT)[0:QK, 2 * (g % 4):2 * (g % 4) + 2, :]
            A(dst, ps[0:QK, g, :].rearrange("p (a b) -> p a b", a=2), ACT.Identity,
              scale=mla_gain[0:QK, g // 4:g // 4 + 1]).then_inc(sem("mla_qkT"), 1)
        attention("mla")
        for t in range(TT):
            act.wait_ge(*reached("mla_att_out", 16))
            if t == 0:
                act.wait_ge(*reached("latent_ssq", 4))
            else:
                act.wait_ge(*reached("mla_ssq", 1))
            A(junk[:, 0:HALF], mo[:, t, :], ACT.Square, accum_out=osq["ssq"][:, t:t + 1]).then_inc(sem("mla_ssq"), 1)
        sqrt_of(osq["std"], osq["ms"], "mla_ms", "mla_std")
        for c in range(LC):
            act.wait_ge(*reached("mla_oT_ps", c // 2 + 1))
            A(hTh[:, LC + c, :], ps[:, c // 2, (c % 2) * S:(c % 2) * S + S], ACT.Identity,
              scale=col("mla_out_norm", c)).then_inc(sem("mla_oT_hi"), 1)
        hi_to(UNITS_AT["w_mem_q"] + 2)

        norm("mem_attn_norm", UNITS_AT["w_mem_q"] + 3)
        hi_to(UNITS_AT["w_mem_o"] + 2)
        mem_copied(4)
        mem_copied(5)
        sqrt_of(heads_st[1][:, 32:40], heads_st[0][:, 32:40], "mem_q_ms", "mem_q_std")
        for j in range(8):
            act.wait_ge(*reached("mem_qkT_ps", j // 2 + 1))
            h = j % 4
            A((eqT if j < 4 else ekT)[:, h, :], ps[:, j // 2, (j % 2) * S:(j % 2) * S + S], ACT.Identity,
              scale=col("mem_q_norm" if j < 4 else "mem_k_norm", 0)).then_inc(sem("mem_qkT"), 1)
        attention("mem")
        oT_high("mem", 2)
        hi_to(UNITS_AT["w_up"] + 2)

        norm("ffn_norm", UNITS_AT["w_up"] + 3)
        for f in range(FT + 2):
            if f < FT:
                act.wait_ge(*reached("ffn_gu", f + 1))
                if f >= 4:
                    act.wait_ge(*reached("ffn_product", f - 3))
                for i in range(2):
                    c = f + i * FT
                    ins = A(cv[f % 4][i], ps[:, f % 4, i * S:(i + 1) * S], ACT.Identity,
                            scale=col("ffn_conv_w", 2 * FT + c), bias=col("ffn_conv_b", c))
                ins.then_inc(sem("ffn_centre"), 1)
                hi_to(UNITS_AT["w_up"] + f + 4)
            if 1 <= f <= FT:
                j = f - 1
                act.wait_ge(*reached("ffn_gated_read", j + 1))
                A(sg[j % 4], cv[j % 4][0], ACT.Sigmoid).then_inc(sem("ffn_gated_sigmoid"), 1)
            if f >= 2:
                j = f - 2
                act.wait_ge(*reached("ffn_product", j + 1))
                A(hidh[:, j, :], sg[j % 4], ACT.Copy).then_inc(sem("ffn_hid_hi"), 1)
        hi_to(UNITS_AT["attn_w_in"] + 2)

        norm("attn_norm_2", UNITS_AT["attn_w_in"] + 3)
        pieces = [(dq, 0, 768), (dk, 768, 1536), (dv, 1536, 2304), (fq, 2304, 2560), (fk, 2560, 2816), (fv, 2816, 3072)]
        for j in range(6):
            hi_to(UNITS_AT["attn_w_in"] + 2 * j + 4)
            for t in range(TT):
                act.wait_ge(*tile_of("attn_in", 2 * j + t))
                for dst, a, b in pieces:
                    lo, hi = max(a, j * HALF), min(b, (j + 1) * HALF)
                    if lo < hi:
                        ins = A(dst[:, t, lo - a:hi - a], ps[:, (2 * j + t) % 8, lo - j * HALF:hi - j * HALF], ACT.Copy)
                ins.then_inc(sem("attn_in_read"), 1)
            hi_to(UNITS_AT["attn_w_in"] + 2 * j + 5)
            for i in {2: (0,), 3: (1,), 5: (2, 3)}.get(j, ()):
                o, n = (0, 24, 48, 64)[i], (24, 24, 16, 16)[i]
                act.wait_ge(*reached("attn_head_ms", i + 1))
                A(attn_std[:, o:o + n], attn_ms[:, o:o + n], ACT.Sqrt).then_inc(sem("attn_head_std"), 1)
        act.wait_ge(*reached("lam_dots", 2))
        A(lam4[:, 2:4], lam4[:, 0:2], ACT.Exp).then_inc(sem("lam_exps"), 1)
        for g in range(8):
            act.wait_ge(*reached("attn_qkT_ps", g + 1))
            dst = [dqT, dqT, dqT, dkT, dkT, dkT, fqT, fkT][g]
            c = 2 * (g % 3) if g < 6 else 0
            gain = ("dil_q_gain_2", "dil_k_gain_2")[g // 3] if g < 6 else ("diff_q_gain_2", "diff_k_gain_2")[g - 6]
            A(dst[:, c:c + 2, :], ps[:, g, :].rearrange("p (a b) -> p a b", a=2), ACT.Identity,
              scale=col(gain, 0)).then_inc(sem("attn_qkT"), 1)
        attention("dil")
        act.wait_ge(*reached("diff_ms", 1))
        A(heads_st[1][:, 48:56], heads_st[0][:, 48:56], ACT.Sqrt).then_inc(sem("diff_std"), 1)
        oT_high("attn", 4)
        hi_to(UNITS_AT["ffn_gate_up"] + 2)

        norm("ffn_norm_2", UNITS_AT["ffn_gate_up"] + 3)
        for f in range(FT + 1):
            if f < FT:
                act.wait_ge(*reached("ffn2_gu", f + 1))
                A(sg[f % 4], ps[:, f % 4, 0:S], ACT.Sigmoid).then_inc(sem("ffn2_gated_sigmoid"), 1)
                hi_to(UNITS_AT["ffn_gate_up"] + f + 4)
            if f >= 1:
                j = f - 1
                act.wait_ge(*reached("ffn2_gated_read", j + 1))
                A(hidh[:, j, :], sg[j % 4], ACT.Copy).then_inc(sem("ffn2_hid_hi"), 1)
        hi_to(UNITS_AT["hgrn_w_in"] + 2)

        A(rh[:], col("moe_w_router_2", 0, KD * NE), ACT.Copy).then_inc(sem("router_hi"), 1)
        norm("hgrn_norm_2", UNITS_AT["hgrn_w_in"] + 3)
        act.wait_ge(*reached("lb_diff", 1))
        A(lbs["lb"], lbs["d"], ACT.Sigmoid)
        A(lbs["one_minus"], lbs["d"], ACT.Sigmoid, scale=-1.0).then_inc(sem("lb"), 1)

        def factors(half, step_):
            if step_ == 0:
                act.wait_ge(*reached("hgrn_d1", half + 1))
                if half == 1:
                    act.wait_ge(*reached("hgrn_scores", 1))
                A(gQ[:], gD[:], ACT.Exp).then_inc(sem("hgrn_eq"), 1)
                A(gK[:], gD[:], ACT.Exp, scale=-1.0).then_inc(sem("hgrn_eq"), 1)
                act.wait_ge(*reached("hgrn_eq", 4 * half + 2))
                A(gD[:], gB[:, 4 * half:4 * half + 4, :], ACT.Exp).then_inc(sem("hgrn_eq"), 1)
                A(dec[:, 16 * half:16 * half + 16],
                  gB[:, 4 * half:4 * half + 4, :].rearrange("p h (c j) -> p (h c) j", j=CHUNK)[:, :, CHUNK - 1],
                  ACT.Exp).then_inc(sem("hgrn_dec"), 1)
            else:
                act.wait_ge(*reached("hgrn_d2", half + 1))
                A(gD[:], gD[:], ACT.Exp).then_inc(sem("hgrn_eq"), 1)

        for g in range(24):
            if g >= 16 and g % 2 == 0:
                hi_to(UNITS_AT["hgrn_w_in"] + g - 8 + 4)
            if g == 20:
                act.wait_ge(*reached("hgrn_forget", 1))
                A(gB[:], gB[:], ACT.Ln).then_inc(sem("hgrn_logf"), 1)
            if g in (21, 22):
                factors(0, g - 21)
            act.wait_ge(*(reached("hgrn_in", g + 1) if g < 16 else tile_of("hgrn_in2", g - 16)))
            if g < 8:
                A(gq[:, g, :], ps[:, g % 8, 0:S], ACT.Sigmoid).then_inc(sem("hgrn_q_sigmoid"), 1)
            elif g < 16:
                A(gB[:, g - 8, :], ps[:, g % 8, 0:S], ACT.Sigmoid)
                A(gk[:, g - 8, :], ps[:, g % 8, 0:S], ACT.Sigmoid, scale=-1.0).then_inc(sem("hgrn_in_read"), 1)
            elif g < 20:
                A(gg[:, g % 2, ((g - 16) // 2) * HALF:((g - 16) // 2 + 1) * HALF], ps[:, g % 8, :],
                  ACT.Sigmoid).then_inc(sem("hgrn_in_read"), 1)
            else:
                A(gv[:, g % 2, ((g - 20) // 2) * HALF:((g - 20) // 2 + 1) * HALF], ps[:, g % 8, :],
                  ACT.Copy).then_inc(sem("hgrn_in_read"), 1)
            if g % 2 == 1:
                hi_to(UNITS_AT["hgrn_w_in"] + (g // 2 if g < 16 else g - 8) + 4)
        for half in range(2):
            act.wait_ge(*reached("hgrn_keysT", half + 1))
            if half == 1:
                act.wait_ge(*reached("hgrn_kv", 12))
            for b in range(2):
                A(kstT[:, 2 * b:2 * b + 2, :], ps[:, 1 + b, :].rearrange("p (a c) -> p a c", a=2),
                  ACT.Copy).then_inc(sem("hgrn_keysT_copied"), 1)
            if half == 0:
                factors(1, 0)
                factors(1, 1)
            else:
                act.wait_ge(*reached("hgrn_ms", 1))
                A(heads_st[1][:, 0:8], heads_st[0][:, 0:8], ACT.Sqrt).then_inc(sem("hgrn_std"), 1)
            for b in range(2):
                act.wait_ge(*reached("hgrn_o", 16 * (half + 1)))
                for t in range(TT):
                    dst = xn[:, t, (4 * half + 2 * b) * P:(4 * half + 2 * b + 2) * P].rearrange("p (a v) -> p a v", a=2)
                    src = ps[:, 4 + b, :].rearrange("p (a t v) -> p t a v", a=2, t=TT)[:, t]
                    ins = A(dst, src, ACT.Copy)
                ins.then_inc(sem("hgrn_o_copied"), 1)
        act.wait_ge(*reached("hgrn_ms", 2))
        A(heads_st[1][:, 8:16], heads_st[0][:, 8:16], ACT.Sqrt).then_inc(sem("hgrn_std"), 1)
        oT_high("hgrn", 4, col("hgrn_out_gain_2", 0))
        hi_to(N_FIXED + 2)

        norm("moe_norm_2", N_FIXED + SPLIT)
        for i in range(2):
            act.wait_ge(sem("tokens_left"), i + 1)
            A(parts[i][:], tokens[:], ACT.Copy).then_inc(sem("tokens_part"), 1)
        def tokens_high(q, e):
            act.wait_ge(sem("bank7_full"), e * 3 + q + 1)
            A(xeh[:, 4 * q:4 * q + 4, :], ps[:, 7, :].rearrange("p (a b) -> p a b", a=4), ACT.Copy).then_inc(sem("tokens_hi"), 1)

        def experts(first, last):
            with nc.scalar.Fori(first, last) as e:
                def hi(j):
                    n = N_FIXED + j
                    act.wait_ge(raw_loaded[n % RAW], e * (16 * E_UNITS // RAW) + 16 * (n // RAW + 1))
                    act.wait_ge(sem("unit_used"), e * E_UNITS + (j + 1))
                    A(wh[:, n % SPLIT, :], raw[:, n % RAW, :], ACT.Copy).then_inc(sem("hi_made"), 1)

                def hidden_high(c):
                    act.wait_ge(sem("hidden_transposed"), e * ECH + c + 1)
                    A(ehh[c % 2][:], ps[:, 6, :].rearrange("p (a b) -> p a b", a=4), ACT.Copy).then_inc(sem("hidden_hi"), 1)

                for q, (what, c, half) in enumerate(EXPERT_ORDER):
                    if what == "up" and half == 1:
                        act.wait_ge(sem("unit_used"), e * E_UNITS + (q + 1 + SPLIT))
                        act.wait_ge(sem("hidden"), e * ECH + (c + 2))
                        A(esg, ps[:, 2 * (c % 2), :], ACT.Sigmoid).then_inc(sem("sigmoid"), 1)
                    if what == "down" and c == ECH - 2 and half == 0:
                        act.wait_ge(sem("bank7_full"), e * 3 + 3)
                        A(GT[:], ps[:, 7, 0:2 * P].rearrange("p (a b) -> p a b", a=2), ACT.Copy).then_inc(sem("bank7_free"), 1)
                    if q == E_UNITS - 1:
                        act.wait_ge(sem("unit_used"), e * E_UNITS + (E_UNITS + SPLIT))
                        A(y_e[:, 0:HALF], ps[:, 4, :], ACT.Copy).then_inc(sem("y_copied"), 1)
                    if what == "down" and c == ECH - 2 and half == 1:
                        tokens_high(0, e + 1)
                        hidden_high(ECH - 1)
                    hi(q + SPLIT)
                    if what == "gate" and half == 1 and c > 0:
                        hidden_high(c - 1)
                    if what == "down" and c == ECH - 2 and half == 1:
                        tokens_high(1, e + 1)

        for q in range(2):
            tokens_high(q, 0)
        act.wait_ge(*reached("route_diff", 1))
        A(rtv["ex"], rtv["v2"], ACT.Exp).then_inc(sem("route_exp"), 1)
        experts(0, NE)
        with nc.scalar.If(nc.scalar.value_load(over[0:1, 0:1], min_val=0, max_val=1)):
            experts(NE, 2 * NE)

    @block.gpsimd
    def _(pool):
        G_ = nc.gpsimd
        pool.wait_ge(*reached("x_ready", X_AFTER["hgrn"]))
        pool.dma_start(moe_gain, moe_gain_d.partition_broadcast(P)).then_inc(sem("moe_gain"), 16)
        pool.wait_ge(*reached("norm_xn", TT * len(NORMS)))
        pool.wait_ge(sem("moe_gain"), 16)
        for t in range(TT):
            ins = G_.tensor_tensor(tokens[:, t, :], xn[:, t, :], moe_gain, ALU.mult)
        ins.then_inc(sem("tokens_left"), 1)
        pool.wait_ge(sem("tokens_part"), 1)
        pool.wait_ge(sem("tokens_left"), 1)
        G_.tensor_tensor(tokens[:], tokens[:], parts[0][:], ALU.subtract).then_inc(sem("tokens_left"), 1)

    @block.vector
    def _(dve):
        V = nc.vector
        steps = [0]

        def step(ins):
            ins.then_inc(sem("vector_step"), 1)
            steps[0] += 1
            dve.wait_ge(*reached("vector_step", steps[0]))

        def settle():
            step(V.tensor_copy(lam4[:, 7:8], ones[:, 0:1]))

        made = [0]

        def lo_to(m):
            for n in range(made[0], m):
                dve.wait_ge(sem("hi_made"), n + 1)
                V.tensor_tensor(wl[:, n % SPLIT, :], raw[:, n % RAW, :], wh[:, n % SPLIT, :].bitcast(F32),
                                ALU.subtract).then_inc(sem("lo_made"), 1)
            made[0] = max(made[0], m)

        def oT_low(stage, groups, gain=1.0):
            for g in range(groups):
                dve.wait_ge(*reached(stage + "_oT_hi", g + 1))
                V.scalar_tensor_tensor(out=hTl[:, 2 * g:2 * g + 2, :], in0=ps[:, g, :].rearrange("p (a b) -> p a b", a=2),
                                       scalar=gain, in1=hTh[:, 2 * g:2 * g + 2, :].bitcast(F32), op0=ALU.mult,
                                       op1=ALU.subtract).then_inc(sem(stage + "_oT"), 1)

        def norm_rows(name):
            i = NORM_OF[name]
            src = mem if name == "mem_norm" else x
            dve.wait_ge(*reached("norm_ssq", 2 * (i + 1)))
            V.tensor_scalar(msum[:, 2 * i:2 * i + 2], ssq[:, 2 * i:2 * i + 2], 1.0 / D, EPS, ALU.mult,
                            ALU.add).then_inc(sem("norm_ms"), 1)
            dve.wait_ge(*reached("norm_std", i + 1))
            step(V.reciprocal(rstd[:, 2 * i:2 * i + 2], std[:, 2 * i:2 * i + 2]))
            if i > 0:
                dve.wait_ge(*reached("norm_transposed", 4 * i))
            for t in range(TT):
                V.tensor_scalar(rows_of(name)[:, t, :], src[:, t, :], rstd[:, 2 * i + t:2 * i + t + 1], None,
                                ALU.mult).then_inc(sem("norm_xn"), 1)
            if i == 0:
                lo_to(1)

        def norm_low(name, ahead):
            i = NORM_OF[name]
            for c in range(KD):
                dve.wait_ge(*reached("norm_hi", KD * i + 2 * (c // 2) + 2))
                V.scalar_tensor_tensor(out=hTl[:, c, :], in0=ps[:, c // 2, (c % 2) * S:(c % 2 + 1) * S],
                                       scalar=col(name, c), in1=hTh[:, c, :].bitcast(F32), op0=ALU.mult,
                                       op1=ALU.subtract).then_inc(sem("norm_out"), 1)
            lo_to(ahead)

        def norm(name, ahead):
            norm_rows(name)
            if name != "attn_norm":
                lo_to(ahead - (0 if name == "moe_norm_2" else 1))
            norm_low(name, ahead)

        def residual(stage, n, following):
            lo_to(following + 1)
            for t in range(TT):
                for h in range(2):
                    dve.wait_ge(*reached(stage, n - 3 + 2 * t + h))
                    xs = x[:, t, h * HALF:(h + 1) * HALF]
                    V.tensor_tensor(xs, ps[:, 4 + 2 * t + h, :], xs, ALU.add).then_inc(sem("x_ready"), 1)

        def attention(stage, between={}):
            a = att[stage]
            units = UNITS[stage]
            n = len(units)
            for i in range(n + 3):
                if i in between:
                    between[i]()
                if i < n:
                    u = units[i]
                    dve.wait_ge(*reached(stage + "_att_scores", i + 1))
                    src = ps[:, SCORE_BANK[i % 3], 0:u["nk"]]
                    nm = a["nmax"][:, i:i + 1]
                    if u["dist"] is None:
                        V.reduce_max(nm, src, AX, negate=True).then_inc(sem(stage + "_att_max"), 1)
                    else:
                        if i >= 3:
                            dve.wait_ge(*reached(stage + "_att_probs", i - 2))
                        s = a["s"][i % 3][:, 0:u["nk"]]
                        step(V.scalar_tensor_tensor(out=s, in0=u["dist"], scalar=-u["slope"], in1=src, op0=ALU.mult,
                                                    op1=ALU.add))
                        V.reduce_max(nm, s, AX, negate=True).then_inc(sem(stage + "_att_max"), 1)
                j = i - 3
                if j >= 0:
                    u = units[j]
                    dve.wait_ge(*reached(stage + "_att_probs", j + 1))
                    inv = a["inv"][:, j:j + 1]
                    if u["kind"] == "raw":
                        dve.wait_ge(*reached(stage + "_att_weighted", j + 1))
                        V.tensor_copy(u["out"], ps[:, 4 + j % 2, 0:u["dv"]]).then_inc(sem(stage + "_att_out"), 1)
                        continue
                    step(V.reciprocal(inv, a["sum"][:, j:j + 1]))
                    if u["kind"] == "minus":
                        step(V.tensor_scalar(inv, inv, lam4[:, 4:5], None, ALU.mult))
                    dve.wait_ge(*reached(stage + "_att_weighted", j + 1))
                    if u["kind"] == "plain":
                        V.tensor_scalar(u["out"], ps[:, 4 + j % 2, 0:u["dv"]], inv, None,
                                        ALU.mult).then_inc(sem(stage + "_att_out"), 1)
                    else:
                        dve.wait_ge(*reached(stage + "_att_out", j))
                        V.scalar_tensor_tensor(out=u["out"], in0=ps[:, 4 + j % 2, 0:u["dv"]], scalar=inv, in1=u["out"],
                                               op0=ALU.mult, op1=ALU.add).then_inc(sem(stage + "_att_out"), 1)
            settle()

        def head_norm(buf, n, w, scratch, ms, stdv, inv, ready, std_sem, std_n, gain, scale):
            sq = scratch[:, 0:n * w].rearrange("p (a b) -> p a b", a=n)
            step(V.tensor_tensor(sq, buf, buf, ALU.mult))
            step(V.tensor_reduce(ms, sq, AX, ALU.add))
            V.tensor_scalar(ms, ms, 1.0 / (w * scale * scale), EPS / (scale * scale), ALU.mult,
                            ALU.add).then_inc(sem(ready), 1)
            dve.wait_ge(*reached(std_sem, std_n))
            step(V.reciprocal(inv, stdv))
            step(V.tensor_tensor(buf, buf, inv.unsqueeze(2).to_broadcast([P, n, w]), ALU.mult))
            if gain is not None:
                step(V.tensor_tensor(buf, buf, gain.unsqueeze(1).to_broadcast([P, n, w]), ALU.mult))

        V.memset(xrp[:, :, 0:3], 0.0)
        step(V.memset(xrp[:, :, S + 3:S + 6], 0.0))
        lam = col("lru_lambda", 0, 8)
        dve.wait_ge(*reached("params", 16 * 3))
        norm("attn_norm", 3)
        step(V.tensor_scalar(sp["c"], lam, -1.0, None, ALU.mult))
        V.tensor_tensor(sp["a"], sp["c"], lam, ALU.max).then_inc(sem("lam_abs"), 1)
        lo_to(4)
        dve.wait_ge(*reached("lam_exp", 1))
        step(V.tensor_scalar(sp["s"], sp["b"], 2.0, None, ALU.add))
        step(V.reciprocal(sp["s"], sp["s"]))
        step(V.tensor_tensor(sp["s"], sp["s"], sp["b"], ALU.mult))
        step(V.tensor_tensor(sp["s2"], sp["s"], sp["s"], ALU.mult))
        step(V.tensor_scalar(sp["p"], sp["s2"], 1.0 / 17, None, ALU.mult))
        for n in (15, 13, 11, 9, 7, 5, 3):
            step(V.scalar_tensor_tensor(out=sp["p"], in0=sp["p"], scalar=1.0 / n, in1=sp["s2"], op0=ALU.add, op1=ALU.mult))
        step(V.scalar_tensor_tensor(out=sp["p"], in0=sp["p"], scalar=1.0, in1=sp["s"], op0=ALU.add, op1=ALU.mult))
        step(V.tensor_scalar(sp["c"], sp["c"], 0.0, -8.0, ALU.max, ALU.mult))
        V.scalar_tensor_tensor(out=sp["out"], in0=sp["p"], scalar=-16.0, in1=sp["c"], op0=ALU.mult,
                               op1=ALU.add).then_inc(sem("softplus"), 1)
        lo_to(UNITS_AT["w_mem_kv"])
        for k in range(4):
            if k == 3:
                norm_rows("mem_norm")
            for d in range(2):
                for c in range(LC):
                    j = d * LC + c
                    if k == 0:
                        dve.wait_ge(*reached("lru_in_copied", c + 1))
                    elif j == 0:
                        dve.wait_ge(*reached("conv", 8 * k))
                    src = xrp[:, c, k + 3 * d:k + 3 * d + S]
                    w = col("lru_conv_w", (d * 4 + k) * LC + c)
                    if k == 0:
                        ins = V.tensor_scalar(xc[d][:, c, :], src, w, col("lru_conv_b", d * LC + c), ALU.mult, ALU.add)
                    else:
                        ins = V.scalar_tensor_tensor(out=xc[d][:, c, :], in0=src, scalar=w, in1=xc[d][:, c, :],
                                                     op0=ALU.mult, op1=ALU.add)
                    ins.then_inc(sem("conv"), 1)
        dve.wait_ge(*reached("lru_in_copied", 8))
        dve.wait_ge(*reached("conv", 32))
        step(V.tensor_tensor(z, yg[:], yg[:], ALU.mult))
        step(V.tensor_scalar(z, z, 0.044715, 1.0, ALU.mult, ALU.add))
        V.tensor_tensor(z, z, yg[:], ALU.mult).then_inc(sem("gelu_z"), 1)
        norm_low("mem_norm", UNITS_AT["w_mem_kv"] + 3)
        for d in range(2):
            dve.wait_ge(*reached("lru_sigmoid", 8))
            step(V.tensor_tensor(ri[d][:], ri[d][:], xc[d][:], ALU.mult))
        dve.wait_ge(*reached("gelu_sig", 1))
        step(V.tensor_tensor(yg[:], yg[:], z, ALU.mult))
        lo_to(UNITS_AT["w_mem_kv"] + 4)
        for d in range(2):
            dve.wait_ge(*reached("lru_root", d + 1))
            step(V.tensor_tensor(ri[d][:], ri[d][:], root[d], ALU.mult))
            if d == 1:
                lo_to(UNITS_AT["w_uq"] + 1)
            dve.wait_ge(*reached("lru_mult", d + 1))
            dve.wait_ge(*reached("lru_a", 4 * (d + 1)))
            step(V.tensor_tensor(ri[d][:], ri[d][:], th[d][:], ALU.mult))
            for c in range(LC):
                r = slice(None, None, -1) if d else slice(None)
                ins = V.tensor_tensor_scan(xc[d][:, c, r], ra[d][:, c, r], ri[d][:, c, r], 0.0, ALU.mult, ALU.add)
            step(ins)
        step(V.tensor_tensor(xc[0][:], xc[0][:], xc[1][:], ALU.add))
        V.tensor_tensor(ri[0][:], xc[0][:], yg[:], ALU.mult).then_inc(sem("lru_gated"), 1)
        dve.wait_ge(*reached("lru_ssq", 1))
        V.tensor_scalar(ri[1][:, 1, :], ps[:, 0, 0:S], 1.0 / LRU_W, EPS, ALU.mult, ALU.add).then_inc(sem("lru_ms"), 1)
        dve.wait_ge(*reached("lru_std", 1))
        ins = V.reciprocal(ri[1][:, 2, :], ri[1][:, 0, :])
        ins.then_inc(sem("lru_done"), 1)
        dve.wait_ge(*reached("lru_done", 1))
        for c in range(LC):
            V.scalar_tensor_tensor(out=th[0][:, c, :], in0=ri[0][:, c, :], scalar=col("lru_out_norm", c), in1=ri[1][:, 2, :],
                                   op0=ALU.mult, op1=ALU.mult).then_inc(sem("lru_scaled"), 1)
        lo_to(UNITS_AT["w_ukv"] + 1)
        dve.wait_ge(*reached("latent_ssq", 4))
        V.tensor_scalar(lat["ms"][:, 0:2], lat["ssq"][:, 0:2], 1.0 / Q_LORA, EPS, ALU.mult, ALU.add)
        step(V.tensor_scalar(lat["ms"][:, 2:4], lat["ssq"][:, 2:4], 1.0 / KV_LORA, EPS, ALU.mult, ALU.add))
        V.sem_inc(sem("latent_ms"), 1)
        dve.wait_ge(*reached("latent_std", 1))
        step(V.reciprocal(lat["r"], lat["std"]))
        for j, (t, a, b) in enumerate(((0, 0, 256), (1, 0, 256), (0, 256, 384), (1, 256, 384))):
            V.tensor_scalar(cn[:, t, a:b], tail[:, t, a:b], lat["r"][:, j:j + 1], None, ALU.mult).then_inc(sem("latent_normed"), 1)
        dve.wait_ge(*reached("lru_hi", 1))
        dve.wait_ge(*reached("lru_scaled", LC))
        V.tensor_tensor(hTl[:, 0:LC, :], th[0][:], hTh[:, 0:LC, :].bitcast(F32), ALU.subtract).then_inc(sem("lru_outT"), 1)
        for c in range(3):
            g = col("q_a_norm", c) if c < 2 else col("kv_a_norm", 0)
            dve.wait_ge(*reached("latent_hi", 3))
            V.scalar_tensor_tensor(out=cTl[:, c, :], in0=ps[:, 1 + c // 2, (c % 2) * S:(c % 2) * S + S], scalar=g,
                                   in1=cTh[:, c, :].bitcast(F32), op0=ALU.mult, op1=ALU.subtract).then_inc(sem("latentT"), 1)
        lo_to(UNITS_AT["w_ukv"] + 2)
        ek_heads, ek_sq = ek.rearrange("p t (h c) -> p (t h) c", h=MEM_HEADS), esq[:].rearrange("p t (h c) -> p (t h) c", h=MEM_HEADS)
        dve.wait_ge(*reached("mem_in_copied", 4))
        step(V.tensor_tensor(ek_sq, ek_heads, ek_heads, ALU.mult))
        step(V.tensor_reduce(heads_st[0][:, 40:48], ek_sq, AX, ALU.add))
        V.tensor_scalar(heads_st[0][:, 40:48], heads_st[0][:, 40:48], 1.0 / P, EPS, ALU.mult,
                        ALU.add).then_inc(sem("mem_k_ms"), 1)
        dve.wait_ge(*reached("params", 16 * 3))
        step(V.tensor_copy(posf, pos[:]))
        for t in range(TT):
            ins = V.tensor_scalar(rope["ang"][:, t, :], const("inv_freq", ROPE // 2), posf[:, t:t + 1], None, ALU.mult)
        step(ins)
        turn = 2.0 * math.pi
        c1 = float(np.float32(np.round(turn * 256) / 256))
        c2 = float(np.float32(np.round((turn - c1) * 2 ** 20) / 2 ** 20))
        c3 = float(np.float32(turn - c1 - c2))
        near = 1.5 * 2.0 ** 23

        def reduced(dst, src):
            step(V.tensor_scalar(rope["k"][:], src, 1.0 / turn, near, ALU.mult, ALU.add))
            step(V.tensor_scalar(rope["k"][:], rope["k"][:], near, None, ALU.subtract))
            for n, cc in enumerate((c1, c2, c3)):
                step(V.scalar_tensor_tensor(out=dst, in0=rope["k"][:], scalar=-cc, in1=(src if n == 0 else dst),
                                            op0=ALU.mult, op1=ALU.add))
            step(V.tensor_scalar(dst, dst, math.pi * (1 - 1e-7), -math.pi * (1 - 1e-7), ALU.min, ALU.max))

        reduced(rope["r"][:], rope["ang"][:])
        V.sem_inc(sem("rope_angle"), 1)
        step(V.tensor_scalar(rope["tmp"][:], rope["r"][:], math.pi / 2, None, ALU.add))
        reduced(rope["ang"][:], rope["tmp"][:])
        V.sem_inc(sem("rope_angle"), 1)
        dve.wait_ge(*reached("late_params", 32))
        step(V.memset(mla_gain[:], 1.0))
        for i, name in enumerate(("mla_q_norm", "mla_k_norm")):
            ins = V.tensor_copy(mla_gain[0:NOPE, i:i + 1], col(name, 0)[0:NOPE])
        step(ins)
        H2 = ROPE // 2
        dve.wait_ge(*reached("rope_table", 1))
        for i, name in enumerate(("mla_q_norm", "mla_k_norm")):
            for half in range(2):
                g = row(name, QK)[:, NOPE + half * H2:NOPE + (half + 1) * H2].unsqueeze(1).to_broadcast([P, TT, H2])
                V.tensor_tensor(turn_by[i][half][0], rope["cos"][:], g, ALU.mult)
                ins = V.tensor_tensor(turn_by[i][half][1], rope["sin"][:], g, ALU.mult)
        step(ins)
        for i, (m, sq, scale) in enumerate(((mq, msq, QK ** -0.5), (mk, msk, 1.0))):
            st = [h[:, 16 * i:16 * i + 16] for h in heads_st]
            dve.wait_ge(*reached("mla_squares", i + 1))
            step(V.tensor_reduce(st[0], sq[:], AX, ALU.add))
            V.tensor_scalar(st[0], st[0], 1.0 / (QK * scale * scale), EPS / (scale * scale), ALU.mult,
                            ALU.add).then_inc(sem("mla_head_ms"), 1)
        for i, (m, sq) in enumerate(((mq, msq), (mk, msk))):
            st = [h[:, 16 * i:16 * i + 16] for h in heads_st]
            dve.wait_ge(*reached("mla_head_std", i + 1))
            step(V.reciprocal(st[2], st[1]))
            step(V.tensor_tensor(m[:], m[:], st[2].unsqueeze(2).to_broadcast([P, 2 * HEADS, QK]), ALU.mult))
            m4 = m.rearrange("p (t h) c -> p t h c", t=TT)
            t1, t2 = m4[:, :, :, NOPE:NOPE + H2], m4[:, :, :, NOPE + H2:QK]
            flat = sq[:].rearrange("p a b -> p (a b)")
            tmp = [flat[:, 256 * j:256 * j + 256].rearrange("p (t h c) -> p t h c", t=TT, h=HEADS) for j in range(4)]
            (cos1, sin1), (cos2, sin2) = [[v.unsqueeze(2).to_broadcast([P, TT, HEADS, H2]) for v in pair]
                                          for pair in turn_by[i]]
            V.tensor_tensor(tmp[0], t1, cos1, ALU.mult)
            V.tensor_tensor(tmp[1], t2, sin2, ALU.mult)
            V.tensor_tensor(tmp[2], t1, sin1, ALU.mult)
            step(V.tensor_tensor(tmp[3], t2, cos2, ALU.mult))
            V.tensor_tensor(t1, tmp[0], tmp[1], ALU.subtract)
            V.tensor_tensor(t2, tmp[2], tmp[3], ALU.add).then_inc(sem("mla_rotated"), 1)
        lo_to(UNITS_AT["w_ukv"] + 4)
        dve.wait_ge(*reached("mem_k_std", 1))
        step(V.reciprocal(heads_st[2][:, 40:48], heads_st[1][:, 40:48]))
        V.tensor_tensor(ek_heads, ek_heads, heads_st[2][:, 40:48].unsqueeze(2).to_broadcast([P, 8, P]),
                        ALU.mult).then_inc(sem("mem_heads_normed"), 1)
        attention("mla")
        dve.wait_ge(*reached("mla_ssq", TT))
        V.tensor_scalar(osq["ms"], osq["ssq"], 1.0 / HALF, EPS, ALU.mult, ALU.add).then_inc(sem("mla_ms"), 1)
        dve.wait_ge(*reached("mla_std", 1))
        step(V.reciprocal(osq["r"], osq["std"]))
        for t in range(TT):
            V.tensor_scalar(mo[:, t, :], mo[:, t, :], osq["r"][:, t:t + 1], None, ALU.mult).then_inc(sem("mla_normed"), 1)
        for c in range(LC):
            dve.wait_ge(*reached("mla_oT_hi", 2 * (c // 2) + 2))
            V.scalar_tensor_tensor(out=hTl[:, LC + c, :], in0=ps[:, c // 2, (c % 2) * S:(c % 2) * S + S],
                                   scalar=col("mla_out_norm", c), in1=hTh[:, LC + c, :].bitcast(F32), op0=ALU.mult,
                                   op1=ALU.subtract).then_inc(sem("mla_oT"), 1)
        residual("mixer_x_change", 7, UNITS_AT["w_mem_q"])

        norm("mem_attn_norm", UNITS_AT["w_mem_q"] + 3)
        lo_to(UNITS_AT["w_mem_o"] + 2)
        dve.wait_ge(*reached("mem_in_copied", 6))
        head_norm(eq.rearrange("p t (h c) -> p (t h) c", h=MEM_HEADS), 8, P, esq[:].rearrange("p a b -> p (a b)"),
                  *[h[:, 32:40] for h in heads_st], "mem_q_ms", "mem_q_std", 1, None, P ** -0.5)
        V.sem_inc(sem("mem_heads_normed"), 1)
        attention("mem")
        oT_low("mem", 2)
        residual("memory_x_change", 5, UNITS_AT["w_up"])

        def low_hidden(stage, j):
            dve.wait_ge(*reached(stage + "_hid_hi", j + 1))
            V.tensor_tensor(hidl[:, j, :], sg[j % 4], hidh[:, j, :].bitcast(F32), ALU.subtract).then_inc(sem(stage + "_hid"), 1)

        norm("ffn_norm", UNITS_AT["w_up"] + 3)
        for f in range(FT + 2):
            if f < FT:
                dve.wait_ge(*reached("ffn_centre", f + 1))
                lo_to(UNITS_AT["w_up"] + f + 4)
                for tap in range(2):
                    for i in range(2):
                        w = col("ffn_conv_w", tap * 2 * 2 * FT + f + i * FT)
                        y, src = cv[f % 4][i], ps[:, f % 4, i * S:(i + 1) * S]
                        a, b = (slice(1, S), slice(0, S - 1)) if tap == 0 else (slice(0, S - 1), slice(1, S))
                        ins = V.scalar_tensor_tensor(out=y[:, a], in0=src[:, b], scalar=w, in1=y[:, a], op0=ALU.mult,
                                                     op1=ALU.add)
                    if tap == 0:
                        step(ins)
                ins.then_inc(sem("ffn_gated_read"), 1)
            if 1 <= f <= FT:
                j = f - 1
                dve.wait_ge(*reached("ffn_gated_sigmoid", j + 1))
                dve.wait_ge(*reached("ffn_gated_read", j + 1))
                step(V.tensor_tensor(sg[j % 4], sg[j % 4], cv[j % 4][0], ALU.mult))
                V.tensor_tensor(sg[j % 4], sg[j % 4], cv[j % 4][1], ALU.mult).then_inc(sem("ffn_product"), 1)
            if f >= 2:
                low_hidden("ffn", f - 2)
        residual("ffn_x_change", 14, UNITS_AT["attn_w_in"])

        norm("attn_norm_2", UNITS_AT["attn_w_in"] + 3)
        lists = ((dq, 12, 64, 0, 64 ** -0.5), (dk, 12, 64, 24, 1.0), (fq, 8, 32, 48, 32 ** -0.5), (fk, 8, 32, 64, 1.0))

        def head_squares(i, ready):
            m, h, w, o, scale = lists[i]
            n = TT * h
            buf = m[:].rearrange("p t (h c) -> p (t h) c", h=h)
            sq = dsq[:, 0:n * w].rearrange("p (a b) -> p a b", a=n)
            dve.wait_ge(*reached("attn_in_read", ready))
            step(V.tensor_tensor(sq, buf, buf, ALU.mult))
            step(V.tensor_reduce(attn_ms[:, o:o + n], sq, AX, ALU.add))
            V.tensor_scalar(attn_ms[:, o:o + n], attn_ms[:, o:o + n], 1.0 / (w * scale * scale), EPS / (scale * scale),
                            ALU.mult, ALU.add).then_inc(sem("attn_head_ms"), 1)

        def head_scale(i):
            m, h, w, o, scale = lists[i]
            n = TT * h
            buf = m[:].rearrange("p t (h c) -> p (t h) c", h=h)
            dve.wait_ge(*reached("attn_head_std", i + 1))
            step(V.reciprocal(attn_ms[:, o:o + n], attn_std[:, o:o + n]))
            V.tensor_tensor(buf, buf, attn_ms[:, o:o + n].unsqueeze(2).to_broadcast([P, n, w]),
                            ALU.mult).then_inc(sem("attn_heads_normed"), 1)

        at = UNITS_AT["attn_w_in"]
        lo_to(at + 8)
        dve.wait_ge(*reached("late_params", 32))
        for i in range(2):
            step(V.tensor_tensor(junk[:, 0:32], row(f"diff_lambda_q{i + 1}_2", 32), row(f"diff_lambda_k{i + 1}_2", 32), ALU.mult))
            V.tensor_reduce(lam4[:, i:i + 1], junk[:, 0:32], AX, ALU.add).then_inc(sem("lam_dots"), 1)
            dve.wait_ge(*reached("lam_dots", i + 1))
        lo_to(at + 9)
        head_squares(0, 4)
        lo_to(at + 11)
        head_scale(0)
        head_squares(1, 6)
        lo_to(at + 13)
        head_scale(1)
        lo_to(at + 15)
        head_squares(2, 12)
        head_squares(3, 12)
        head_scale(2)
        head_scale(3)
        dve.wait_ge(*reached("lam_exps", 1))
        step(V.tensor_tensor(lam4[:, 4:5], lam4[:, 3:4], lam4[:, 2:3], ALU.subtract))
        step(V.tensor_scalar(lam4[:, 4:5], lam4[:, 4:5], LAM_INIT, None, ALU.subtract))
        def dilated_weights():
            settle()
            nm = att["dil"]["nmax"][:, 0:24].rearrange("p (g x) -> p g x", g=3)
            sm = att["dil"]["sum"][:, 0:24].rearrange("p (g x) -> p g x", g=3)
            al = alpha[:, 0].rearrange("p (g x) -> p g x", g=3)
            a2 = alpha[:, 1].rearrange("p (g x) -> p g x", g=3)
            step(V.tensor_tensor(a2[:, 0], nm[:, 0], nm[:, 1], ALU.min))
            step(V.tensor_tensor(a2[:, 0], a2[:, 0], nm[:, 2], ALU.min))
            V.tensor_tensor(al, a2[:, 0:1].to_broadcast([P, 3, 8]), nm, ALU.subtract).then_inc(sem("alpha_diff"), 1)

        def dilated_mixed():
            sm = att["dil"]["sum"][:, 0:24].rearrange("p (g x) -> p g x", g=3)
            al = alpha[:, 0].rearrange("p (g x) -> p g x", g=3)
            a2 = alpha[:, 1].rearrange("p (g x) -> p g x", g=3)
            dve.wait_ge(*reached("alpha_exp", 1))
            step(V.tensor_tensor(a2, al, sm, ALU.mult))
            step(V.tensor_tensor(a2[:, 0], a2[:, 0], a2[:, 1], ALU.add))
            step(V.tensor_tensor(a2[:, 0], a2[:, 0], a2[:, 2], ALU.add))
            step(V.reciprocal(a2[:, 0], a2[:, 0]))
            step(V.tensor_tensor(al, al, a2[:, 0:1].to_broadcast([P, 3, 8]), ALU.mult))
            af = alpha[:, 0].rearrange("p (h t) -> p t h", t=TT)
            for t in range(TT):
                o = xn[:, t, 0:768].rearrange("p (h v) -> p h v", v=64)
                ins = V.tensor_tensor(o, o, af[:, t, :].unsqueeze(2).to_broadcast([P, 12, 64]), ALU.mult)
            ins.then_inc(sem("attn_mixed"), 1)

        attention("dil", {DIL_HEADS * TT + 3: dilated_weights, DIL_HEADS * TT + 8: dilated_mixed})
        fo = xn[:, :, 768:1024]
        sqv = dsq[:, 0:512].rearrange("p (a b) -> p a b", a=TT)
        step(V.tensor_tensor(sqv, fo, fo, ALU.mult))
        st = [h[:, 48:56] for h in heads_st]
        step(V.tensor_reduce(st[0], dsq[:, 0:512].rearrange("p (a b) -> p a b", a=8), AX, ALU.add))
        k2 = (1.0 - LAM_INIT) ** 2
        V.tensor_scalar(st[0], st[0], 1.0 / (64 * k2), EPS / k2, ALU.mult, ALU.add).then_inc(sem("diff_ms"), 1)
        dve.wait_ge(*reached("diff_std", 1))
        step(V.reciprocal(st[2], st[1]))
        for t in range(TT):
            o = fo[:, t, :].rearrange("p (h v) -> p h v", v=64)
            step(V.tensor_tensor(o, o, st[2][:, 4 * t:4 * t + 4].unsqueeze(2).to_broadcast([P, 4, 64]), ALU.mult))
            ins = V.tensor_tensor(o, o, row("diff_out_gain_2", 64).unsqueeze(1).to_broadcast([P, 4, 64]), ALU.mult)
        ins.then_inc(sem("attn_mixed"), 1)
        oT_low("attn", 4)
        residual("attn_x_change", 7, UNITS_AT["ffn_gate_up"])

        norm("ffn_norm_2", UNITS_AT["ffn_gate_up"] + 3)
        for f in range(FT + 1):
            if f < FT:
                dve.wait_ge(*reached("ffn2_gated_sigmoid", f + 1))
                step(V.tensor_tensor(sg[f % 4], sg[f % 4], ps[:, f % 4, 0:S], ALU.mult))
                V.tensor_tensor(sg[f % 4], sg[f % 4], ps[:, f % 4, S:2 * S], ALU.mult).then_inc(sem("ffn2_gated_read"), 1)
                lo_to(UNITS_AT["ffn_gate_up"] + f + 4)
            if f >= 1:
                low_hidden("ffn2", f - 1)
        residual("ffn2_x_change", 14, UNITS_AT["hgrn_w_in"])

        norm_rows("hgrn_norm_2")
        dve.wait_ge(sem("router_hi"), 1)
        V.tensor_tensor(rl[:], col("moe_w_router_2", 0, KD * NE), rh[:].bitcast(F32), ALU.subtract).then_inc(sem("router_lo"), 1)
        V.tensor_tensor(lbs["d"], col("hgrn_lb_logits_2", 8, 8), col("hgrn_lb_logits_2", 0, 8),
                        ALU.subtract).then_inc(sem("lb_diff"), 1)
        lo_to(UNITS_AT["hgrn_w_in"] + 2)
        norm_low("hgrn_norm_2", UNITS_AT["hgrn_w_in"] + 3)
        for g in range(8):
            dve.wait_ge(*reached("hgrn_q_sigmoid", g + 1))
            V.tensor_tensor(gq[:, g, :], gq[:, g, :], ps[:, g, 0:S], ALU.mult).then_inc(sem("hgrn_q_read"), 1)
            if g % 2 == 1:
                lo_to(UNITS_AT["hgrn_w_in"] + g // 2 + 4)
        dve.wait_ge(*reached("lb", 1))
        for g in range(8):
            dve.wait_ge(*reached("hgrn_in_read", g + 1))
            V.tensor_scalar(gB[:, g, :], gB[:, g, :], lbs["one_minus"][:, g:g + 1], lbs["lb"][:, g:g + 1], ALU.mult, ALU.add)
            ins = V.tensor_scalar(gk[:, g, :], gk[:, g, :], lbs["one_minus"][:, g:g + 1], None, ALU.mult)
            if g % 2 == 1:
                lo_to(UNITS_AT["hgrn_w_in"] + 4 + g // 2 + 4)
        step(ins)
        V.sem_inc(sem("hgrn_forget"), 1)
        at = UNITS_AT["hgrn_w_in"]
        lo_to(at + 16)
        dve.wait_ge(*reached("hgrn_logf", 1))
        for h in range(HG_HEADS):
            ins = V.tensor_tensor_scan(gB[:, h, :], const("reset", S), gB[:, h, :], 0.0, ALU.mult, ALU.add)
        step(ins)

        def chunks(v):
            return v.rearrange("p h (c j) -> p (h c) j", j=CHUNK)

        causal = const("chunk_causal", P).bitcast(U32)

        def factors(half, step_):
            hs = slice(4 * half, 4 * half + 4)
            b16 = chunks(gB[:, hs, :])
            if step_ == 0:
                if half == 1:
                    dve.wait_ge(*reached("hgrn_factors", 4))
                V.tensor_tensor(chunks(gD[:]), b16, b16[:, :, CHUNK // 2:CHUNK // 2 + 1].to_broadcast([P, 16, CHUNK]),
                                ALU.subtract).then_inc(sem("hgrn_d1"), 1)
            if step_ == 1:
                dve.wait_ge(*reached("hgrn_eq", 4 * half + 1))
                V.tensor_tensor(gQ[:], gQ[:], gq[:, hs, :], ALU.mult).then_inc(sem("hgrn_factors"), 1)
                dve.wait_ge(*reached("hgrn_eq", 4 * half + 2))
                V.tensor_tensor(gK[:], gK[:], gk[:, hs, :], ALU.mult).then_inc(sem("hgrn_factors"), 1)
                dve.wait_ge(*reached("hgrn_factors", 4 * half + 2))
                dve.wait_ge(*reached("hgrn_eq", 4 * half + 3))
                V.tensor_tensor(gq[:, hs, :], gq[:, hs, :], gD[:], ALU.mult).then_inc(sem("hgrn_factors"), 1)
            if step_ == 2:
                dve.wait_ge(*reached("hgrn_factors", 4 * half + 3))
                V.tensor_tensor(chunks(gD[:]), b16[:, :, CHUNK - 1:CHUNK].to_broadcast([P, 16, CHUNK]), b16,
                                ALU.subtract).then_inc(sem("hgrn_d2"), 1)
            if step_ == 3:
                dve.wait_ge(*reached("hgrn_eq", 4 * half + 4))
                V.tensor_tensor(gk[:, hs, :], gk[:, hs, :], gD[:], ALU.mult).then_inc(sem("hgrn_factors"), 1)

        def out_norm(half, step_):
            o = xn[:, :, half * HALF:(half + 1) * HALF]
            heads = o.rearrange("p t (h v) -> p t h v", v=P)
            st = [h[:, 8 * half:8 * half + 8] for h in heads_st]
            if step_ == 0:
                sq = gB[:, 4 * half:4 * half + 4, :].rearrange("p a b -> p (a b)").rearrange("p (t h v) -> p t h v", t=TT, v=P)
                dve.wait_ge(*reached("hgrn_o_copied", 2 * (half + 1)))
                step(V.tensor_tensor(sq, heads, heads, ALU.mult))
                step(V.tensor_reduce(st[0], sq.rearrange("p t h v -> p (t h) v"), AX, ALU.add))
                V.tensor_scalar(st[0], st[0], 1.0 / P, EPS, ALU.mult, ALU.add).then_inc(sem("hgrn_ms"), 1)
            else:
                dve.wait_ge(*reached("hgrn_std", half + 1))
                step(V.reciprocal(st[2], st[1]))
                r_ = st[2].rearrange("p (t h) -> p t h", t=TT).unsqueeze(3).to_broadcast([P, TT, 4, P])
                step(V.tensor_tensor(heads, heads, r_, ALU.mult))
                V.tensor_tensor(o, o, gg[:, :, half * HALF:(half + 1) * HALF], ALU.mult).then_inc(sem("hgrn_gated"), 1)

        factors(0, 0)
        factors(0, 1)
        factors(0, 2)
        lo_to(at + 18)
        factors(0, 3)
        lo_to(UNITS_AT["hgrn_w_out"] + 3)
        dve.wait_ge(*reached("hgrn_in_read", 16))
        step(V.memset(AT[:], 0.0))
        for half in range(2):
            dve.wait_ge(*reached("hgrn_scores", half + 1))
            for h in range(4):
                ins = V.copy_predicated(AT[:, 4 * half + h, :], causal, ps[:, 0, h * P:(h + 1) * P])
            ins.then_inc(sem("hgrn_masked"), 1)
            dve.wait_ge(*reached("hgrn_dec", half + 1))
            if half == 0:
                factors(1, 0)
            else:
                out_norm(0, 0)
            for c in range(3):
                for h in range(4):
                    dve.wait_ge(*reached("hgrn_kv", 12 * half + 4 * c + h + 1))
                    kv = ps[:, (3, 6, 7, 0)[h], 0:P]
                    if c == 0:
                        if half == 1:
                            dve.wait_ge(*reached("hgrn_o", 16))
                        V.tensor_copy(state[:, h, :], kv).then_inc(sem("hgrn_state"), 1)
                    else:
                        dve.wait_ge(*reached("hgrn_o", 16 * half + 4 * c + h + 1))
                        dve.wait_ge(*reached("hgrn_state", 12 * half + 4 * (c - 1) + h + 1))
                        V.scalar_tensor_tensor(out=state[:, h, :], in0=state[:, h, :], scalar=dec[:, 16 * half + 4 * h + c:16 * half + 4 * h + c + 1],
                                               in1=kv, op0=ALU.mult, op1=ALU.add).then_inc(sem("hgrn_state"), 1)
                if half == 0 and c == 0:
                    factors(1, 1)
                elif half == 0 and c == 1:
                    factors(1, 2)
                    factors(1, 3)
                elif half == 1 and c == 0:
                    out_norm(0, 1)
        out_norm(1, 0)
        out_norm(1, 1)
        oT_low("hgrn", 4, col("hgrn_out_gain_2", 0))
        residual("hgrn_x_change", 7, N_FIXED)

        norm("moe_norm_2", N_FIXED + SPLIT - 1)
        dve.wait_ge(sem("logits"), 1)
        V.tensor_copy(logitsT, ps[0:NE, 7, 0:S]).then_inc(sem("logits_read"), 1)
        L, rank, s1, s2, tmp = (rt[:, i] for i in range(5))
        dve.wait_ge(sem("logits"), 2)
        step(V.tensor_copy(L, ps[:, 6, 0:TT * NE].rearrange("p (t e) -> p t e", t=TT)))
        g3 = [r[:].rearrange("p (t e j) -> p t e j", t=TT, e=NE) for r in rcmp]
        full = [P, TT, NE, NE]
        step(V.tensor_tensor(g3[0], L.unsqueeze(2).to_broadcast(full), L.unsqueeze(3).to_broadcast(full), ALU.is_gt))
        step(V.tensor_tensor(g3[1], L.unsqueeze(2).to_broadcast(full), L.unsqueeze(3).to_broadcast(full), ALU.is_equal))
        tie = const("tie", NE * NE)
        for t in range(TT):
            step(V.tensor_tensor(rcmp[1][:, t * 64:(t + 1) * 64], rcmp[1][:, t * 64:(t + 1) * 64], tie, ALU.mult))
        step(V.tensor_tensor(g3[0], g3[0], g3[1], ALU.add))
        step(V.tensor_reduce(rank, g3[0], AX, ALU.add))
        step(V.tensor_scalar(s1, rank, 2.0, None, ALU.is_lt))
        V.sem_inc(sem("selected"), 1)
        lo_to(N_FIXED + SPLIT)
        dve.wait_ge(sem("slots_ps"), 1)
        sel = rt[:, 2]
        step(V.tensor_copy(tmp, ps[:, 7, 0:TT * NE].rearrange("p (t e) -> p t e", t=TT)))
        step(V.tensor_reduce(posf[:, 0:1], ps[:, 7, TT * NE:3 * NE], AX, ALU.max))
        step(V.tensor_scalar(over[:], posf[:, 0:1], float(P), None, ALU.is_gt))
        step(V.scalar_tensor_tensor(out=tmp, in0=tmp, scalar=1.0, in1=sel, op0=ALU.add, op1=ALU.mult))
        V.memset(slots[:, 2 * NE, :], -1.0)
        for t in range(TT):
            V.tensor_scalar(slots[:, 0:NE, t], tmp[:, t, :], -1.0, None, ALU.add)
            ins = V.tensor_scalar(slots[:, NE:2 * NE, t], tmp[:, t, :], -1.0 - P, None, ALU.add)
        step(ins)
        V.sem_inc(sem("routed"), 1)

        def choose(e):
            for t in range(TT):
                ins = V.tensor_scalar(G[:, t, :], slot, slots[:, bass.ds(e, 1), t], None, ALU.is_equal)
            ins.then_inc(sem("chosen"), 1)

        V.sem_inc(sem("hidden"), 2)
        V.sem_inc(sem("out_added"), 4)
        V.sem_inc(sem("y_copied"), 2)
        choose(0)
        dve.wait_ge(sem("tokens_part"), 2)
        V.tensor_tensor(parts[2][:], tokens[:], parts[1][:], ALU.subtract).then_inc(sem("tokens_left"), 1)

        def tokens_low(q, e):
            dve.wait_ge(sem("tokens_hi"), e * 2 + q + 1)
            V.tensor_tensor(xel[:, 4 * q:4 * q + 4, :], ps[:, 7, :].rearrange("p (a b) -> p a b", a=4),
                            xeh[:, 4 * q:4 * q + 4, :].bitcast(F32), ALU.subtract).then_inc(sem("bank7_free"), 1)

        s1 = xsel
        for s, r, v in ((s1, 0.0, "v1"), (s2, 1.0, "v2")):
            step(V.tensor_scalar(s, rank, r, None, ALU.is_equal))
            step(V.tensor_tensor(tmp, s, L, ALU.mult))
            step(V.tensor_reduce(rtv[v], tmp, AX, ALU.add))
        V.tensor_tensor(rtv["v2"], rtv["v2"], rtv["v1"], ALU.subtract).then_inc(sem("route_diff"), 1)
        for q in range(2):
            tokens_low(q, 0)
        dve.wait_ge(*reached("route_exp", 1))
        step(V.tensor_scalar(rtv["w1"], rtv["ex"], 1.0, None, ALU.add))
        step(V.reciprocal(rtv["w1"], rtv["w1"]))
        step(V.tensor_tensor(rtv["w2"], rtv["w1"], rtv["ex"], ALU.mult))
        for t in range(TT):
            step(V.tensor_scalar(tmp[:, t, :], s1[:, t, :], rtv["w1"][:, t:t + 1], None, ALU.mult))
            step(V.scalar_tensor_tensor(out=gates[:, 0:NE, t], in0=s2[:, t, :], scalar=rtv["w2"][:, t:t + 1], in1=tmp[:, t, :],
                                        op0=ALU.mult, op1=ALU.add))
        for t in range(TT):
            step(V.tensor_copy(gates[:, NE:2 * NE, t], gates[:, 0:NE, t]))

        def experts(first, last):
            with nc.vector.Fori(first, last) as e:
                def lo(j):
                    n = N_FIXED + j
                    dve.wait_ge(sem("hi_made"), e * E_UNITS + (n + 1))
                    V.tensor_tensor(wl[:, n % SPLIT, :], raw[:, n % RAW, :], wh[:, n % SPLIT, :].bitcast(F32),
                                    ALU.subtract).then_inc(sem("lo_made"), 1)

                def hidden_low(c):
                    dve.wait_ge(sem("hidden_hi"), e * ECH + c + 1)
                    V.tensor_tensor(ehl[c % 2][:], ps[:, 6, :].rearrange("p (a b) -> p a b", a=4),
                                    ehh[c % 2][:].bitcast(F32), ALU.subtract).then_inc(sem("expert_hid"), 1)

                for q, (what, c, half) in enumerate(EXPERT_ORDER):
                    if what == "up" and half == 1:
                        dve.wait_ge(sem("sigmoid"), e * ECH + c + 1)
                        if c >= 2:
                            dve.wait_ge(sem("hidden_transposed"), e * ECH + (c - 1))
                        V.tensor_tensor(eh[c % 2], esg, ps[:, 2 * (c % 2), :], ALU.mult).then_inc(sem("silu"), 1)
                        dve.wait_ge(sem("silu"), e * ECH + c + 1)
                        V.tensor_tensor(eh[c % 2], eh[c % 2], ps[:, 2 * (c % 2) + 1, :], ALU.mult).then_inc(sem("hidden"), 1)
                    if what == "down" and c == ECH - 2 and half == 1:
                        tokens_low(0, e + 1)
                        hidden_low(ECH - 1)
                        tokens_low(1, e + 1)
                    if q < E_UNITS - 2:
                        lo(q + SPLIT)
                    if what == "gate" and half == 1 and c > 0:
                        hidden_low(c - 1)
                    if q == 12:
                        dve.wait_ge(sem("bank7_full"), e * 3 + 2)
                        for t in range(TT):
                            ins = V.tensor_scalar(Gw[:, t, :], slot, slots[:, bass.ds(e, 1), t], gates[:, bass.ds(e, 1), t],
                                                  ALU.is_equal, ALU.mult)
                        ins.then_inc(sem("weighted"), 1)
                        choose(e + 1)
                dve.wait_ge(sem("unit_used"), e * E_UNITS + (E_UNITS + SPLIT))
                V.tensor_copy(y_e[:, HALF:D], ps[:, 5, :]).then_inc(sem("y_copied"), 1)
                lo(E_UNITS - 2 + SPLIT)
                dve.wait_ge(sem("out_added"), (e + 1) * 4)
                for i in range(4):
                    dve.wait_ge(sem("out_change"), e * 4 + (i + 1))
                    xs = x[:, i // 2, (i % 2) * HALF:(i % 2 + 1) * HALF]
                    V.tensor_tensor(xs, ps[:, (6, 7, 2, 3)[i], :], xs, ALU.add).then_inc(sem("out_added"), 1)
                lo(E_UNITS - 1 + SPLIT)

        experts(0, NE)
        dve.wait_ge(sem("out_added"), 4 * NE + 4)
        with nc.vector.If(nc.vector.value_load(over[0:1, 0:1], min_val=0, max_val=1)):
            experts(NE, 2 * NE)
            dve.wait_ge(sem("out_added"), 8 * NE + 4)
        V.sem_inc(sem("x_final"), 4)

    block_cm.__exit__(None, None, None)


def constants():
    c = np.zeros((P, N_CONST), np.float32)

    def put(name, v):
        v = np.asarray(v, np.float32).reshape(P, -1)
        c[:, CONST[name]:CONST[name] + v.shape[1]] = v

    p = np.arange(P)
    put("ident", np.eye(P))
    put("ones", np.ones((P, P)))
    put("inv_freq", np.broadcast_to(10000.0 ** (-np.arange(0, ROPE, 2) / ROPE), (P, ROPE // 2)))
    put("reset", np.broadcast_to(np.arange(S) % CHUNK != 0, (P, S)))
    put("chunk_causal", (p[:, None] % CHUNK) <= (p[None, :] % CHUNK))
    put("slot", np.broadcast_to(p, (P, P)))
    put("before", p[:, None] < p[None, :])
    put("tie", np.broadcast_to((np.arange(NE)[None, :] < np.arange(NE)[:, None]).reshape(1, -1), (P, NE * NE)))
    dist = []
    for window, dilation in ((128, 1), (512, 4), (2048, 16), (S, 1)):
        for t in range(TT):
            gap = (t * P + p)[:, None] - np.arange(P * (t + 1))[None, :]
            dist.append(np.where((gap >= 0) & (gap % dilation == 0) & (gap <= window), gap, FAR))
    put("dist", np.concatenate(dist, axis=1))
    return c


def by_feature(v, n):
    return np.moveaxis(np.asarray(v, np.float32).reshape(-1, n, P), 2, 0).reshape(P, -1)


def k_tiles(w):
    k, n = w.shape
    return w.reshape(k // P, P, n).transpose(1, 0, 2).reshape(P, -1)


def lay_out(a):
    f = {k: np.asarray(v) for k, v in a.items()}
    cols = np.zeros((P, N_COLS), np.float32)
    for name in COLS:
        v = f[name]
        n = {"ffn_conv_w": 2 * FT, "ffn_conv_b": 2 * FT}.get(name, max(1, v.shape[-1] // P))
        if name in ("dil_q_gain_2", "dil_k_gain_2", "diff_q_gain_2", "diff_k_gain_2"):
            m = np.tile(v.reshape(-1), P // v.size)[:, None]
        elif name in ("mla_q_norm", "mla_k_norm"):
            m = np.pad(v.reshape(-1), (0, P - v.size))[:, None]
        elif name == "moe_w_router_2":
            m = k_tiles(v[0])
        else:
            m = by_feature(v, n)
        cols[:, COLS[name]:COLS[name] + m.shape[1]] = m
    rows = np.zeros((1, N_ROWS), np.float32)
    for name in ROWS:
        rows[0, ROWS[name]:ROWS[name] + f[name].size] = f[name].reshape(-1)

    units = np.zeros((N_UNITS, P, UNIT), np.float32)

    def put(n, m):
        units[n, :, 0:m.shape[1]] = m

    def by_columns(at, w):
        for j in range(w.shape[1] // S):
            put(at + j, k_tiles(w[:, j * S:(j + 1) * S]))

    def by_halves(at, w, width=HALF):
        for j in range(w.shape[1] // width):
            for half in range(2):
                put(at + 2 * j + half, k_tiles(w[half * HALF:(half + 1) * HALF, j * width:(j + 1) * width]))

    def by_rows(at, w):
        for j in range(w.shape[0] // S):
            put(at + j, k_tiles(w[j * S:(j + 1) * S]))

    U = UNITS_AT
    w_in = f["w_in"][0]
    by_columns(U["w_in"], w_in[:, 0:2 * LRU_W])
    by_halves(U["w_in_tail"], w_in[:, 2 * LRU_W:], TAIL)
    put(U["w_uq"], k_tiles(f["w_uq"][0]))
    put(U["w_ukv"], k_tiles(f["w_ukv"][0]))
    by_rows(U["w_out"], f["w_out"][0])
    by_halves(U["w_mem_kv"], f["w_mem_kv"][0])
    by_halves(U["w_mem_q"], f["w_mem_q"][0])
    by_rows(U["w_mem_o"], f["w_mem_o"][0])
    w_up = f["w_up"][0]
    for name, gate, up in (("w_up", w_up[:, :D_FF], w_up[:, D_FF:]),
                           ("ffn_gate_up", f["ffn_w_gate_2"][0], f["ffn_w_up_2"][0])):
        for j in range(FT):
            cut = slice(P * j, P * (j + 1))
            put(U[name] + j, k_tiles(np.concatenate([gate[:, cut], up[:, cut]], axis=1)))
    by_rows(U["w_down"], f["w_down"][0])
    by_halves(U["attn_w_in"], f["attn_w_in_2"][0])
    by_rows(U["attn_w_out"], f["attn_w_out_2"][0])
    by_rows(U["ffn_w_down"], f["ffn_w_down_2"][0])
    by_columns(U["hgrn_w_in"], f["hgrn_w_in_2"][0][:, 0:2 * D])
    by_halves(U["hgrn_w_in"] + 8, f["hgrn_w_in_2"][0][:, 3 * D:])
    by_halves(U["hgrn_w_in"] + 12, f["hgrn_w_in_2"][0][:, 2 * D:3 * D])
    by_rows(U["hgrn_w_out"], f["hgrn_w_out_2"][0])
    for e in range(NE):
        for j, (what, c, half) in enumerate(EXPERT_ORDER):
            w = f[f"moe_w_{what}_2"][0, e]
            if what == "down":
                w = w[c * HALF + half * S:c * HALF + (half + 1) * S]
            else:
                w = w[half * HALF:(half + 1) * HALF, c * HALF:(c + 1) * HALF]
            put(N_FIXED + e * E_UNITS + j, k_tiles(w))
    gates = np.zeros((P, 2, 2, LC, P), np.float32)
    for i, name in enumerate(("lru_w_a", "lru_w_i")):
        w = f[name][0]
        for d in range(2):
            for c in range(LC):
                for b in range(2):
                    gates[64 * b:64 * b + 64, d, i, c, 64 * b:64 * b + 64] = w[d, 2 * c + b]

    def token_major(v):
        return np.ascontiguousarray(v.reshape(TT, P, -1).transpose(1, 0, 2))

    return {"units": units, "consts": constants(), "cols": cols, "rows": rows,
            "moe_gain": f["moe_norm_2"].reshape(1, D), "lru_w": gates.reshape(P, 16, P), "x": token_major(f["x"]),
            "mem": token_major(f["mem"]),
            "pos": np.ascontiguousarray(f["positions"].reshape(TT, P).T.astype(np.int32))}


def kernel(**inputs):
    import concourse.bacc as bacc
    from concourse.bass_utils import run_bass_kernel_spmd

    nc = bacc.Bacc("TRN2", target_bir_lowering=False, num_devices=1)
    arrays = lay_out(inputs)
    args = [nc.dram_tensor("in_" + name, a.shape, mybir.dt.from_np(a.dtype), kind="ExternalInput").ap()
            for name, a in arrays.items()]
    out = nc.dram_tensor("out", (P, TT, D), F32, kind="ExternalOutput").ap()
    build(nc, *args, out)
    r = run_bass_kernel_spmd(nc, [{"in_" + name: a for name, a in arrays.items()}], core_ids=[0])
    got = r.results[0]["out"]
    return np.ascontiguousarray(got.transpose(1, 0, 2)).reshape(1, S, D)
```
